# Optimizing a Trainium2 kernel written in Bass

```python
import math
import jax, jax.numpy as jnp
from jax import lax
import numpy as np

D_MODEL = 1024
BATCH = 1
SEQ = 256
DEPTH = 1
DEC_BATCH = 8
DEC_SEQ = 8
PAST_LEN = 2048
PAGE_SIZE = 128

GLA_HEADS = 4
GLA_DK = D_MODEL // 8
GLA_DV = D_MODEL // 4
GLA_KEY = GLA_HEADS * GLA_DK
GLA_VAL = GLA_HEADS * GLA_DV
GATE_RANK = 16
GATE_NORMALIZER = 16.0
GLA_CHUNK = 64
RMS_EPS = 1e-6
POOL_GROUPS = 4
POOL_WIDTH = D_MODEL // 2
POOL_GC = POOL_WIDTH // POOL_GROUPS
POOL_WINDOWS = (2, 4, 8, 16)
POOL_WMAX = 16
POOL_BUF = POOL_WMAX - 1
N_EXPERTS = 32
TOP_K = 4
D_FF = D_MODEL
SWIGLU_LIMIT = 7.0
GLU_ALPHA = 1.702
MOE_BLOCK = 128
LN_EPS = 1e-5
DEEPNORM_ALPHA = (2.0 * DEPTH) ** 0.25
DEEPNORM_BETA = (8.0 * DEPTH) ** -0.25
IN_SIZES = (GLA_KEY, GLA_KEY, GLA_VAL, GATE_RANK, GLA_VAL, POOL_WIDTH, D_MODEL, D_MODEL)
N_IN = sum(IN_SIZES)

kernel_name = 'gla_pool_gated_moe_deepnorm_step'

def _split_in(h):
    parts = []
    off = 0
    for n in IN_SIZES:
        parts.append(h[..., off:off + n])
        off += n
    return parts

def _layer_norm(x, g, b):
    xf = x.astype(jnp.float32)
    mu = jnp.mean(xf, -1, keepdims=True)
    var = jnp.mean(jnp.square(xf - mu), -1, keepdims=True)
    y = (xf - mu) * lax.rsqrt(var + LN_EPS) * g.astype(jnp.float32) + b.astype(jnp.float32)
    return y.astype(x.dtype)

def _gla_chunked(q, k, v, glog, s0):
    B, L = q.shape[:2]
    C = math.gcd(L, GLA_CHUNK)
    n = L // C

    def to_chunks(t):
        return jnp.moveaxis(t.reshape(B, n, C, *t.shape[2:]), 1, 0)

    mask = jnp.tril(jnp.ones((C, C), dtype=bool))[None, None]

    def step(s, inp):
        qc, kc, vc, gc = inp
        b = jnp.cumsum(gc, axis=1)
        b_ref = b[:, C // 2:C // 2 + 1]
        a = jnp.einsum('bihd,bjhd->bhij', qc * jnp.exp(b - b_ref), kc * jnp.exp(b_ref - b))
        a = jnp.where(mask, a, 0.0)
        o = (jnp.einsum('bhij,bjhv->bihv', a, vc)
             + jnp.einsum('bihd,bhdv->bihv', qc * jnp.exp(b), s))
        b_last = b[:, -1]
        s = (jnp.exp(b_last)[..., None] * s
             + jnp.einsum('bjhd,bjhv->bhdv', kc * jnp.exp(b_last[:, None] - b), vc))
        return s, o

    s, o = lax.scan(step, s0, (to_chunks(q), to_chunks(k), to_chunks(v), to_chunks(glog)))
    o = jnp.moveaxis(o, 0, 1).reshape(B, L, GLA_HEADS, GLA_DV)
    return o, s

def _pool_mix(u, buf, w_grp, scale):
    L = u.shape[1]
    ext = jnp.concatenate([buf.astype(jnp.float32), u.astype(jnp.float32)], axis=1)
    N = ext.shape[1]
    W = POOL_WMAX
    cs = jnp.cumsum(jnp.pad(ext, ((0, 0), (W, 0), (0, 0))), axis=1)
    cs = jnp.pad(cs, ((0, 0), (1, 0), (0, 0)))
    e = jnp.arange(N - L, N)
    outs = []
    for gi, w in enumerate(POOL_WINDOWS):
        sl = slice(gi * POOL_GC, (gi + 1) * POOL_GC)
        win_sum = cs[:, W + 1 + N - L:W + 1 + N, sl] - cs[:, W + 1 - w + N - L:W + 1 - w + N, sl]
        cnt = jnp.minimum(w, e + 1).astype(jnp.float32)[None, :, None]
        outs.append(win_sum / cnt - ext[:, N - L:, sl])
    pooled = jnp.concatenate(outs, axis=-1)
    B = pooled.shape[0]
    pooled = jnp.einsum('blgc,gcd->blgd', pooled.reshape(B, L, POOL_GROUPS, POOL_GC),
                        w_grp.astype(jnp.float32)).reshape(B, L, POOL_WIDTH)
    pooled = pooled * scale.astype(jnp.float32)
    return pooled, ext[:, N - POOL_BUF:]

def _mixer(x, s0, buf0, w_in, w_gk2, b_gk, gla_norm_w, w_branch_gla, w_pool_grp, pool_scale,
           w_branch_pool, b_gates, w_out):
    B, L, _ = x.shape
    f32 = jnp.float32
    h = x @ w_in
    q, k, v, lr, g, u, ga, gb = _split_in(h)
    q = q.astype(f32).reshape(B, L, GLA_HEADS, GLA_DK) * (GLA_DK ** -0.5)
    k = k.astype(f32).reshape(B, L, GLA_HEADS, GLA_DK)
    v = v.astype(f32).reshape(B, L, GLA_HEADS, GLA_DV)
    glog = jax.nn.log_sigmoid((lr @ w_gk2 + b_gk).astype(f32)) / GATE_NORMALIZER
    glog = glog.reshape(B, L, GLA_HEADS, GLA_DK)
    o, s_new = _gla_chunked(q, k, v, glog, s0.astype(f32))
    o = o * lax.rsqrt(jnp.mean(jnp.square(o), -1, keepdims=True) + RMS_EPS) * gla_norm_w.astype(f32)
    o = o * jax.nn.silu(g.astype(f32).reshape(B, L, GLA_HEADS, GLA_DV))
    branch_a = o.reshape(B, L, GLA_VAL).astype(x.dtype) @ w_branch_gla
    pooled, buf_new = _pool_mix(u, buf0, w_pool_grp, pool_scale)
    branch_b = pooled.astype(x.dtype) @ w_branch_pool
    gate_a = jax.nn.sigmoid(ga + b_gates[:D_MODEL])
    gate_b = jax.nn.sigmoid(gb + b_gates[D_MODEL:])
    merged = gate_a * branch_a + gate_b * branch_b
    return merged @ w_out, s_new, buf_new

def _moe(x2, w_router, b_router, w_gu, b_gu, w_down, b_down):
    M, D = x2.shape
    MK = M * TOP_K
    logits = (x2 @ w_router).astype(jnp.float32) + b_router.astype(jnp.float32)
    top_v, top_i = lax.top_k(logits, TOP_K)
    gate_w = jax.nn.softmax(top_v, axis=-1)
    flat_e = top_i.reshape(-1)
    flat_tok = jnp.arange(MK, dtype=jnp.int32) // TOP_K
    order = jnp.argsort(flat_e)
    se = flat_e[order]
    stok = flat_tok[order]
    sw = gate_w.reshape(-1)[order]
    counts = jnp.bincount(flat_e, length=N_EXPERTS)
    padded = (counts + MOE_BLOCK - 1) // MOE_BLOCK * MOE_BLOCK
    pad_end = jnp.cumsum(padded)
    pad_start = pad_end - padded
    start = jnp.cumsum(counts) - counts
    dest = pad_start[se] + jnp.arange(MK, dtype=jnp.int32) - start[se]
    n_blocks = -(-(MK + N_EXPERTS * (MOE_BLOCK - 1)) // MOE_BLOCK)
    n_rows = n_blocks * MOE_BLOCK
    row_tok = jnp.full((n_rows,), M, dtype=jnp.int32).at[dest].set(stok)
    x_pad = jnp.concatenate([x2, jnp.zeros((1, D), x2.dtype)], axis=0)
    xb = x_pad[row_tok].reshape(n_blocks, MOE_BLOCK, D)
    block_e = jnp.minimum(jnp.searchsorted(pad_end, jnp.arange(n_blocks) * MOE_BLOCK, side='right'),
                          N_EXPERTS - 1)

    def expert_block(args):
        xblk, e = args
        hh = xblk @ w_gu[e] + b_gu[e]
        gate = jnp.minimum(hh[:, :D_FF], SWIGLU_LIMIT)
        up = jnp.clip(hh[:, D_FF:], -SWIGLU_LIMIT, SWIGLU_LIMIT)
        act = (up + 1.0) * (gate * jax.nn.sigmoid(GLU_ALPHA * gate))
        return act @ w_down[e] + b_down[e]

    res = lax.map(expert_block, (xb, block_e)).reshape(n_rows, D)
    y = jnp.zeros((M, D), jnp.float32).at[stok].add(sw[:, None] * res[dest].astype(jnp.float32))
    return y.astype(x2.dtype)

def _layer(x, s0, buf0, mix_w, ln1_g, ln1_b, moe_w, ln2_g, ln2_b):
    B, L, D = x.shape
    mix, s_new, buf_new = _mixer(x, s0, buf0, *mix_w)
    h = _layer_norm(DEEPNORM_ALPHA * x + mix, ln1_g, ln1_b)
    f = _moe(h.reshape(B * L, D), *moe_w).reshape(B, L, D)
    y = _layer_norm(DEEPNORM_ALPHA * h + f, ln2_g, ln2_b)
    return y, s_new, buf_new

def setup_inputs(seed: int = 0) -> dict:
    key = jax.random.key(seed)
    ks = jax.random.split(key, 32)
    nrm = jax.random.normal
    f32 = jnp.float32
    col_scale = jnp.concatenate([jnp.full((n,), DEEPNORM_BETA if i == 2 else 1.0, f32)
                                 for i, n in enumerate(IN_SIZES)])
    return {
        'x_prompt': nrm(ks[0], (BATCH, SEQ, D_MODEL), f32),
        'x_sample': nrm(ks[1], (DEC_BATCH, DEC_SEQ, D_MODEL), f32),
        'state_gla': 0.3 * nrm(ks[2], (DEPTH, DEC_BATCH, GLA_HEADS, GLA_DK, GLA_DV), f32),
        'state_pool': nrm(ks[3], (DEPTH, DEC_BATCH, POOL_BUF, POOL_WIDTH), f32),
        'w_in': nrm(ks[4], (DEPTH, D_MODEL, N_IN), f32) * D_MODEL ** -0.5 * col_scale,
        'w_gk2': nrm(ks[5], (DEPTH, GATE_RANK, GLA_KEY), f32) * GATE_RANK ** -0.5,
        'b_gk': 0.1 * nrm(ks[6], (DEPTH, GLA_KEY), f32),
        'gla_norm_w': 1.0 + 0.02 * nrm(ks[7], (DEPTH, GLA_DV), f32),
        'w_branch_gla': nrm(ks[8], (DEPTH, GLA_VAL, D_MODEL), f32) * GLA_VAL ** -0.5,
        'w_pool_grp': nrm(ks[9], (DEPTH, POOL_GROUPS, POOL_GC, POOL_GC), f32) * POOL_GC ** -0.5,
        'pool_scale': 1.0 + 0.1 * nrm(ks[10], (DEPTH, POOL_WIDTH), f32),
        'w_branch_pool': nrm(ks[11], (DEPTH, POOL_WIDTH, D_MODEL), f32) * POOL_WIDTH ** -0.5,
        'b_gates': 0.1 * nrm(ks[12], (DEPTH, 2 * D_MODEL), f32),
        'w_out': nrm(ks[13], (DEPTH, D_MODEL, D_MODEL), f32) * D_MODEL ** -0.5 * DEEPNORM_BETA,
        'ln1_g': 1.0 + 0.02 * nrm(ks[14], (DEPTH, D_MODEL), f32),
        'ln1_b': 0.02 * nrm(ks[15], (DEPTH, D_MODEL), f32),
        'w_router': nrm(ks[16], (DEPTH, D_MODEL, N_EXPERTS), f32) * D_MODEL ** -0.5,
        'b_router': 0.01 * nrm(ks[17], (DEPTH, N_EXPERTS), f32),
        'w_gu': nrm(ks[18], (DEPTH, N_EXPERTS, D_MODEL, 2 * D_FF), f32) * D_MODEL ** -0.5,
        'b_gu': 0.02 * nrm(ks[19], (DEPTH, N_EXPERTS, 2 * D_FF), f32),
        'w_down': nrm(ks[20], (DEPTH, N_EXPERTS, D_FF, D_MODEL), f32) * D_FF ** -0.5 * DEEPNORM_BETA,
        'b_down': 0.02 * nrm(ks[21], (DEPTH, N_EXPERTS, D_MODEL), f32),
        'ln2_g': 1.0 + 0.02 * nrm(ks[22], (DEPTH, D_MODEL), f32),
        'ln2_b': 0.02 * nrm(ks[23], (DEPTH, D_MODEL), f32),
    }

def reference(x_prompt, x_sample, state_gla, state_pool, w_in, w_gk2, b_gk, gla_norm_w, w_branch_gla,
              w_pool_grp, pool_scale, w_branch_pool, b_gates, w_out, ln1_g, ln1_b, w_router, b_router,
              w_gu, b_gu, w_down, b_down, ln2_g, ln2_b):
    yp = x_prompt
    ys = x_sample
    Bp = x_prompt.shape[0]
    gla_p, pool_p, gla_s, pool_s = [], [], [], []
    for l in range(DEPTH):
        mix_w = (w_in[l], w_gk2[l], b_gk[l], gla_norm_w[l], w_branch_gla[l], w_pool_grp[l],
                 pool_scale[l], w_branch_pool[l], b_gates[l], w_out[l])
        moe_w = (w_router[l], b_router[l], w_gu[l], b_gu[l], w_down[l], b_down[l])
        s0_p = jnp.zeros((Bp, GLA_HEADS, GLA_DK, GLA_DV), jnp.float32)
        buf0_p = jnp.zeros((Bp, 0, POOL_WIDTH), jnp.float32)
        yp, sp, bp = _layer(yp, s0_p, buf0_p, mix_w, ln1_g[l], ln1_b[l], moe_w, ln2_g[l], ln2_b[l])
        ys, ss, bs = _layer(ys, state_gla[l], state_pool[l], mix_w, ln1_g[l], ln1_b[l], moe_w,
                            ln2_g[l], ln2_b[l])
        gla_p.append(sp.astype(state_gla.dtype))
        pool_p.append(bp.astype(state_pool.dtype))
        gla_s.append(ss.astype(state_gla.dtype))
        pool_s.append(bs.astype(state_pool.dtype))
    new_gla_prompt = jnp.stack(gla_p, 0)
    new_pool_prompt = jnp.stack(pool_p, 0)
    new_gla_sample = jnp.stack(gla_s, 0)
    new_pool_sample = jnp.stack(pool_s, 0)
    return (yp, ys, new_gla_prompt, new_pool_prompt, new_gla_sample, new_pool_sample)


_drawn_inputs = setup_inputs


def setup_inputs(seed=0):
    import zlib

    import numpy as np

    out = dict(_drawn_inputs(seed))
    spreads = {}
    factors = {'gla_norm_w': 4.362,
     'b_router': 3.849,
     'b_gu': 8.0,
     'b_down': 6.459,
     'ln2_g': 2.827,
     'ln2_b': 2.909}
    for name, (base, spread) in spreads.items():
        noise = np.random.default_rng([zlib.crc32(name.encode()), seed]).standard_normal(out[name].shape)
        drawn = base * np.exp(spread * noise) if base else spread * noise
        out[name] = __import__('jax').numpy.asarray(drawn.astype(out[name].dtype))
    for name, factor in factors.items():
        out[name] = (out[name] * factor).astype(out[name].dtype)
    return out
```

```python
from contextlib import ExitStack

import concourse.bass as bass
from concourse import mybir

D = 1024
KC = D // 128
NP, B, L = 256, 8, 8
NS = B * L
NT = NP + NS
HEADS, DK, DV = 4, 128, 256
C = 64
PBUF = 15
WMAX = 16
NE, TOPK = 32, 4
CAP = 64
PASSES = NT // CAP
RANKS = 24
ALPHA = 2.0 ** 0.25
LIMIT, GLU_ALPHA = 7.0, 1.702
RMS_EPS, LN_EPS = 1e-6, 1e-5
TILES = [(0, 128), (128, 128), (256, 64)]

RING = 12
UNIT = 2048
MIX_UNITS = ([("k", i) for i in range(2)] + [("q", i) for i in range(2)] + [("v", i) for i in range(4)]
             + [("g", i) for i in range(4)] + [("ga", i) for i in range(4)] + [("ba", i) for i in range(4)]
             + [("u", i) for i in range(2)] + [("gb", i) for i in range(4)] + [("bb", i) for i in range(2)]
             + [("out", i) for i in range(4)])
UNIT_NO = {u: n for n, u in enumerate(MIX_UNITS)}
NMIX = len(MIX_UNITS)
UP_UNITS, DOWN_UNITS = KC, KC // 2
EXP_UNITS = UP_UNITS + DOWN_UNITS
COL0 = {"q": 0, "k": 512, "v": 1024, "lr": 2048, "g": 2064, "u": 3088, "ga": 3600, "gb": 4624}

PRODUCTS = ([("xt", i) for i in range(KC)] + [("cols",), ("bdt",), ("bgt",), ("lr",)]
            + [("k", i) for i in range(4)] + [("gk", i) for i in range(4)] + [("q", i) for i in range(4)]
            + [("v", j, t) for j in range(4) for t in range(3)] + [("g", i) for i in range(8)]
            + [("a", t) for t in range(3)] + [("kt", t) for t in range(3)]
            + [x for h in range(HEADS) for x in
               [("kv", h, 0), ("kv", h, 1)] + [("kvs", h, i) for i in range(4)] + [("o", h, 0), ("o", h, 1)]]
            + [("rms", h) for h in range(HEADS)]
            + [("ga", i) for i in range(8)] + [("ba", i) for i in range(8)] + [("u", i) for i in range(4)]
            + [("pb",), ("up",), ("us",)] + [("gb", i) for i in range(8)] + [("grp", i) for i in range(4)]
            + [("bb", i) for i in range(8)] + [("out", j, t) for j in range(4) for t in range(3)]
            + [("ht", i) for i in range(KC)] + [("lg", t) for t in range(3)] + [("rk", t) for t in range(3)]
            + [("cnt",)])
NO = {p: n for n, p in enumerate(PRODUCTS)}
NPROD = len(PRODUCTS)

CST = {}
NCST = 0
for _name, _n in (("ident", 128), ("ones", 128), ("pmask", 128), ("smask", 64), ("before", 128),
                  ("iota64", 64), ("iota32", 32), ("bmask", B), ("rcnt", 64)):
    CST[_name] = (NCST, _n)
    NCST += _n


def constants():
    import numpy as np
    c = np.zeros((128, NCST), np.float32)
    p = np.arange(128)

    def put(name, value):
        at, n = CST[name]
        c[:, at:at + n] = value
    i = np.arange(128)
    put("ident", p[:, None] == i)
    put("ones", 1.0)
    put("pmask", (p[:, None] // C == i // C) & (p[:, None] <= i))
    j = np.arange(64)
    put("smask", (p[:, None] // L == j // L) & (p[:, None] <= j))
    put("before", p[:, None] < i)
    put("iota64", j)
    put("iota32", np.arange(32))
    put("bmask", p[:, None] // L == np.arange(B))
    t = np.arange(16)
    put("rcnt", np.concatenate([1.0 / np.minimum(2 ** (g + 1), t + 1) for g in range(4)]))
    starts = np.ones((128, HEADS, NT), np.float32)
    starts[:, :, 0:NP:C] = 0.0
    starts[:, :, NP:NT:L] = 0.0
    ids = np.arange(NE, NE * PASSES, dtype=np.float32)
    lists = np.stack([ids, (ids // NE) * CAP])
    return c, starts.reshape(128, HEADS * NT), lists.reshape(1, -1)


NID = NE * (PASSES - 1)

XT = 0
QR = 2560
KR = 3840
QE = 5120
KE = 6400
BB = 7680
EE = 8960
VR = 10240
KLT = 13312
OT = 14848
SP = 17408
SS = 19456
G = 21504
GA = 24064
CONST = 26624
BGU = CONST + NCST
BDN = BGU + 512
COLS = BDN + 256
DEC = COLS + 32
BR = DEC + 48
MISC = BR + 32
ARENA = MISC + 64
H = 0
Y = 3072
XGT = 6144
PH = 7168
ACTT = 7552
G1 = 8064
U1 = 8576
SG = 9088
YSB = 9600
RES = 10112
ST = 11136
RK = 11904
GW = 12384
MSK = 12480
LG = 12576
MX = 12672
RT = 12704
LISTS = 12832


def build(nc, x_p, x_s, state_gla, state_pool, w_in, w_gk2, b_gk, gla_norm_w, w_bgla, w_grp, pool_scale,
          w_bpool, b_gates, w_out, ln1_g, ln1_b, w_router, b_router, w_gu, b_gu, w_down, b_down, ln2_g, ln2_b,
          c_cols, c_starts, c_lists, y_p, y_s, ngp, npp, ngs, nps):
    f32 = mybir.dt.float32
    i32 = mybir.dt.int32
    u32 = mybir.dt.uint32
    ALU = mybir.AluOpType
    ACT = mybir.ActivationFunctionType
    ds = bass.ds

    with ExitStack() as ctx:
        def sem(name):
            return ctx.enter_context(nc.semaphore(name))

        ar = ctx.enter_context(nc.sbuf_tensor("arena", [128, ARENA], f32))
        ring = ctx.enter_context(nc.sbuf_tensor("ring", [128, RING, UNIT], f32))
        top_idx = ctx.enter_context(nc.sbuf_tensor("top_idx", [128, 8], u32))
        later = ctx.enter_context(nc.sbuf_tensor("later", [1, 2, RANKS], i32))
        n_later = ctx.enter_context(nc.sbuf_tensor("n_later", [1, 8], i32))
        ps = [ctx.enter_context(nc.psum_tensor(f"bank{i}", [128, 512], f32)) for i in range(8)]

        def reg(at, n, *dims, p=128, p0=0):
            v = ar[p0:p0 + p, at:at + n]
            if len(dims) == 1:
                v = v.rearrange("p (a b) -> p a b", a=dims[0])
            if len(dims) == 2:
                v = v.rearrange("p (a b c) -> p a b c", a=dims[0], b=dims[1])
            return v

        def cst(name, p=128, n=None):
            at, full = CST[name]
            return ar[0:p, CONST + at:CONST + at + (n or full)]

        ident = cst("ident")
        xt = reg(XT, KC * NT, KC)
        q = reg(QR, HEADS * NT, HEADS)
        k = reg(KR, HEADS * NT, HEADS)
        qe = reg(QE, HEADS * NT, HEADS)
        ke = reg(KE, HEADS * NT, HEADS)
        bb = reg(BB, HEADS * NT, HEADS)
        ee = reg(EE, HEADS * NT, HEADS)
        xr = reg(VR, 3 * D, 3)
        v = xr
        klt = reg(KLT, 3 * 512, 3)
        ot = reg(OT, 8 * NT, 8)
        starts = reg(OT, HEADS * NT)
        eb = reg(OT + HEADS * NT, HEADS * NT, HEADS)
        bl = reg(SP, HEADS * NT, HEADS)
        at_ = reg(BB, 3 * 512, 3)
        sq = reg(QE, 8 * NT, 8)
        rms = reg(BB, HEADS * NT, HEADS)
        sp_st = reg(SP, 2 * 4 * DV, 2, 4)
        ss_st = [reg(SS, B * DV, B), reg(GA, B * DV, B)]
        gs = reg(G, 8 * NT, 8)
        ga = reg(GA, 8 * NT, 8)
        gb = reg(OT, 8 * NT, 8)
        klm = reg(KR, B * DK, B, p=NS)
        pg = reg(QR, 4 * NT, 4)
        po = reg(KR, 4 * NT, 4)
        up_pad = reg(QE, 4 * (PBUF + NP), 4)
        us_pad = reg(QE + 4 * (PBUF + NP), 4 * B * (PBUF + L), 4, B)
        spb = reg(SP, 512, p=B * PBUF)
        wgrp = reg(SP + 512, 512, 4)
        wrt = reg(SP + 1024, 256, KC)
        pool_out_p = ar[0:PBUF, SP + 1280:SP + 1792]
        pool_out_s = ar[0:NS, SS:SS + 512]
        ln_g = reg(G, D)
        ln_b = reg(G + D, D)
        wlr = reg(KE, KC * 16, KC)
        wgk2 = ar[0:16, KE + 128:KE + 640]
        lrt = ar[0:16, KE + 640:KE + 960]
        rows = ar[0:26, KE + 960:KE + 1088]
        bgu_rows = ar[0:NE, G:G + 2048]
        bdn_rows = ar[0:NE, KLT:KLT + D]
        bgu = reg(BGU, 512, 16)
        bdn = reg(BDN, 256, 8)
        cols = reg(COLS, 26)
        dec = reg(DEC, 48, HEADS)
        brt = reg(BR, NE)
        hrow = reg(H, 3 * D, 3)
        y = reg(Y, 3 * D, 3)
        xgt = reg(XGT, 2 * 512, 2, KC)
        onehot = reg(PH, 2 * 3 * CAP, 2, 3)
        actt = reg(ACTT, 512, KC)
        g1 = reg(G1, 512, KC)
        u1 = reg(U1, 512, KC)
        sg = reg(SG, 512, KC)
        ysb = reg(YSB, 512, KC)
        res = ar[0:CAP, RES:RES + D]
        slot_t = reg(ST, 2 * 384, 2, p=CAP)
        rank = reg(RK, 3 * PASSES * NE, 3)
        gw = reg(GW, 3 * NE, 3)
        msk = reg(MSK, 3 * NE, 3)
        lg = reg(LG, 3 * NE, 3)
        mx = reg(MX, 8)
        oh = reg(RT, 4 * NE, 4)
        lists = ar[0:1, LISTS:LISTS + 2 * NID]
        found = ar[0:1, LISTS + 2 * NID:LISTS + 4 * NID]
        st6 = reg(MISC, 12, 2)
        mv = reg(MISC + 12, 2)
        rstd = reg(MISC + 14, 1)
        eps_rms = reg(MISC + 16, 1)
        eps_ln = reg(MISC + 17, 1)
        tmp8 = reg(MISC + 18, 8)
        idxf = reg(MISC + 26, 8)
        sm = reg(MISC + 34, 8)
        top24 = ar[0:1, LISTS + 4 * NID:LISTS + 4 * NID + RANKS]
        low = ar[0:1, LISTS + 4 * NID + RANKS:LISTS + 4 * NID + 2 * RANKS]

        filled = [sem(f"slot{i}_filled") for i in range(RING)]
        bank_full = [sem(f"bank{i}_full") for i in range(8)]
        bank_free = [sem(f"bank{i}_free") for i in range(8)]
        x_in = sem("x_in")
        cst_in = sem("cst_in")
        small_in = sem("small_in")
        bgu_in = sem("bgu_in")
        starts_in = sem("starts_in")
        ss_in = [sem(f"ss_in{i}") for i in range(HEADS)]
        x_again = sem("x_again")
        late_in = sem("late_in")
        ln1_in = sem("ln1_in")
        ln2_in = sem("ln2_in")
        stored_s = sem("stored_s")
        stored_p = sem("stored_p")
        stored = sem("stored")
        y_stored = sem("y_stored")
        xt_ready = sem("xt_ready")
        cols_ready = sem("cols_ready")
        lr_ready = sem("lr_ready")
        z_ready = sem("z_ready")
        soft_ready = sem("soft_ready")
        diff_ready = sem("diff_ready")
        exp_ready = sem("exp_ready")
        qk_in = sem("qk_in")
        qk_ready = sem("qk_ready")
        v_ready = sem("v_ready")
        sig_ready = sem("sig_ready")
        g_ready = sem("g_ready")
        at_ready = sem("at_ready")
        klt_ready = sem("klt_ready")
        klm_ready = sem("klm_ready")
        sp_ready = sem("sp_ready")
        ss_ready = sem("ss_ready")
        sq_ready = sem("sq_ready")
        sqrt_ready = sem("sqrt_ready")
        ot_ready = sem("ot_ready")
        ga_ready = sem("ga_ready")
        merged = sem("merged")
        pads_zero = sem("pads_zero")
        u_ready = sem("u_ready")
        pb_ready = sem("pb_ready")
        po_ready = sem("po_ready")
        pg_ready = sem("pg_ready")
        pool_out_ready = sem("pool_out_ready")
        gb_ready = sem("gb_ready")
        var_ready = sem("var_ready")
        std_ready = sem("std_ready")
        h_ready = sem("h_ready")
        ln_read = sem("ln_read")
        ht_ready = sem("ht_ready")
        mask_ready = sem("mask_ready")
        max_ready = sem("max_ready")
        soft4_ready = sem("soft4_ready")
        lists_ready = sem("lists_ready")
        y_final = sem("y_final")
        dve_step = sem("dve_step")
        act_step = sem("act_step")
        onehot_ready = sem("onehot_ready")
        gathered = sem("gathered")
        xgt_ready = sem("xgt_ready")
        units_used = sem("units_used")
        gate_ready = sem("gate_ready")
        swish_ready = sem("swish_ready")
        act_ready = sem("act_ready")
        ysb_ready = sem("ysb_ready")
        yt_turned = sem("yt_turned")
        res_ready = sem("res_ready")
        slots_turned = sem("slots_turned")
        slot_ready = sem("slot_ready")
        pieces = sem("pieces")
        added = sem("added")
        blk = sem("blk_step")

        def full(name):
            n = NO[name]
            return bank_full[n % 8], n // 8 + 1

        def freed(name):
            return bank_free[NO[name] % 8]

        def bank(name):
            return ps[NO[name] % 8]

        def unit_landed(kind, i):
            n = UNIT_NO[(kind, i)]
            return filled[n % RING], 16 * (n // RING + 1)

        def unit(kind, i):
            return ring[:, UNIT_NO[(kind, i)] % RING, :]

        def slot_of(j):
            return (NMIX + j) % RING

        def slot_count(idx, j):
            return idx * 16 + 16 * ((NMIX + j) // RING + 1)

        LAST = {}
        for kind, i in MIX_UNITS:
            if kind == "v" or kind == "out":
                LAST[(kind, i)] = (kind, i, 2)
            elif kind == "bb":
                LAST[(kind, i)] = (kind, 4 * i + 3)
            else:
                LAST[(kind, i)] = (kind, 2 * i + 1)

        def by_chunk(view, t):
            if t == 0:
                return view[:, :, 0:NP].rearrange("p h (c i) -> p h c i", i=C)
            return view[:, :, NP:NT].rearrange("p h (c i) -> p h c i", i=L)

        block = ctx.enter_context(nc.Block())

        @block.sync
        def _(sp):
            for n, (kind, i) in enumerate(MIX_UNITS):
                if n >= RING:
                    sp.wait_ge(*full(LAST[MIX_UNITS[n - RING]]))
                dst = ring[:, n % RING, :]
                if kind in COL0:
                    src = w_in[0, :, COL0[kind] + 256 * i:COL0[kind] + 256 * (i + 1)]
                    sp.dma_start(dst.rearrange("p (c n) -> p c n", c=KC),
                                 src.rearrange("(c p) n -> p c n", p=128)).then_inc(filled[n % RING], 16)
                elif kind == "bb":
                    src = w_bpool[0, :, 512 * i:512 * (i + 1)]
                    sp.dma_start(dst.rearrange("p (c n) -> p c n", c=4),
                                 src.rearrange("(c p) n -> p c n", p=128)).then_inc(filled[n % RING], 16)
                else:
                    w = w_bgla if kind == "ba" else w_out
                    src = w[0, :, 256 * i:256 * (i + 1)]
                    sp.dma_start(dst.rearrange("p (c n) -> p c n", c=KC),
                                 src.rearrange("(c p) n -> p c n", p=128)).then_inc(filled[n % RING], 16)

            def load_unit(e, j):
                s = slot_of(j)
                if j < UP_UNITS:
                    src = w_gu[0, ds(e, 1), j * 128:(j + 1) * 128, :].rearrange("e p n -> p (e n)")
                    sp.dma_start(ring[:, s, :], src).then_inc(filled[s], 16)
                else:
                    r = (j - UP_UNITS) * 256
                    src = w_down[0, ds(e, 1), r:r + 256, :].rearrange("e (c p) n -> p (e c) n", p=128)
                    sp.dma_start(ring[:, s, :].rearrange("p (c n) -> p c n", c=2), src).then_inc(filled[s], 16)

            for j in range(EXP_UNITS):
                sp.wait_ge(*full(LAST[MIX_UNITS[NMIX + j - RING]]))
                load_unit(0, j)
            with sp.Fori(1, NE) as idx:
                e = sp.snap(idx)
                for j in range(EXP_UNITS):
                    sp.wait_ge(units_used, (e - 1) * EXP_UNITS + j + 1)
                    load_unit(e, j)
            sp.wait_ge(lists_ready, 1)
            count = sp.value_load(n_later[0:1, 0:1], min_val=0, max_val=RANKS)
            with sp.If(count > 0):
                with sp.Fori(0, count) as b:
                    e = sp.value_load(later[0:1, 1, ds(b, 1)], min_val=0, max_val=NE - 1)
                    sp.wait_ge(units_used, b * EXP_UNITS + NE * EXP_UNITS)
                    for j in range(EXP_UNITS):
                        load_unit(e, j)
            for t, (t0, n) in enumerate(TILES):
                sp.wait_ge(y_final, t + 1)
                dst = y_p[0, t0:t0 + n, :] if t < 2 else y_s.rearrange("b s d -> (b s) d")
                sp.dma_start(dst, y[0:n, t, :]).then_inc(y_stored, 16)
            sp.wait_ge(y_stored, 16 * 3)
            sp.wait_ge(stored_s, 16 * 4)
            sp.wait_ge(stored_p, 16 * 4)

        @block.gpsimd
        def _(pool):
            def load_x(s):
                for t, (t0, n) in enumerate(TILES):
                    src = x_p[0, t0:t0 + n, :] if t < 2 else x_s.rearrange("b s d -> (b s) d")
                    pool.dma_start(xr[0:n, t, :], src).then_inc(s, 16)

            pool.dma_start(ar[:, CONST:CONST + NCST], c_cols).then_inc(cst_in, 16)
            load_x(x_in)
            pool.dma_start(wlr, w_in[0, :, COL0["lr"]:COL0["lr"] + 16].rearrange("(c p) n -> p c n", p=128))\
                .then_inc(small_in, 16)
            pool.dma_start(wgk2, w_gk2[0, :, :]).then_inc(small_in, 16)
            at = 0
            for vec, n in ((b_gates, 16), (b_gk, 4), (gla_norm_w, 2), (pool_scale, 4)):
                pool.dma_start(rows[at:at + n, :], vec[0, :].rearrange("(c p) -> c p", p=128)).then_inc(small_in, 16)
                at += n
            pool.dma_start(bdn_rows, b_down[0, :, :]).then_inc(bgu_in, 16)
            pool.dma_start(bgu_rows, b_gu[0, :, :]).then_inc(bgu_in, 16)
            pool.dma_start(starts, c_starts).then_inc(starts_in, 16)
            pool.dma_start(brt, b_router.partition_broadcast(128).rearrange("p a n -> p (a n)")
                           if 0 else b_router[0:1, :].broadcast_to([128, NE])).then_inc(starts_in, 16)

            def load_states(h):
                pool.dma_start(ss_st[h % 2], state_gla[0, :, h, :, :].rearrange("b d v -> d b v"))\
                    .then_inc(ss_in[h], 16)
            load_states(0)
            load_states(1)
            for h in range(HEADS):
                pool.wait_ge(sp_ready, 4 * (h + 1))
                pool.dma_start(ngp[0, 0, h, :, :], sp_st[:, h % 2, 3, :]).then_inc(stored_p, 16)
                pool.wait_ge(ss_ready, h + 1)
                pool.dma_start(ngs[0, :, h, :, :].rearrange("b d v -> d b v"), ss_st[h % 2]).then_inc(stored_s, 16)
                if h < 2:
                    pool.wait_ge(stored_s, 16 * (h + 1))
                    load_states(h + 2)
            pool.wait_ge(*full(("o", 3, 1)))
            load_x(x_again)
            pool.wait_ge(stored_p, 16 * 4)
            pool.wait_ge(stored_s, 16 * 4)
            pool.dma_start(spb, state_pool[0, :, :, :].rearrange("b r c -> (b r) c")).then_inc(late_in, 16)
            pool.dma_start(wgrp, w_grp[0, :, :, :].rearrange("g c d -> c g d")).then_inc(late_in, 16)
            pool.dma_start(wrt, w_router[0, :, :].rearrange("(c p) n -> p c n", p=128)).then_inc(late_in, 16)
            pool.wait_ge(ot_ready, 1)
            pool.dma_start(ln_g, ln1_g[0:1, :].broadcast_to([128, D])).then_inc(ln1_in, 16)
            pool.dma_start(ln_b, ln1_b[0:1, :].broadcast_to([128, D])).then_inc(ln1_in, 16)
            pool.dma_start(nps[0, :, 0:PBUF - L, :], state_pool[0, :, L:PBUF, :]).then_inc(stored, 16)
            pool.wait_ge(pool_out_ready, 2)
            pool.dma_start(npp[0, 0, :, :], pool_out_p).then_inc(stored, 16)
            for b in range(B):
                pool.dma_start(nps[0, b, PBUF - L:PBUF, :], pool_out_s[b * L:(b + 1) * L, :]).then_inc(late_in, 16)
            pool.wait_ge(late_in, 16 * (3 + B))
            pool.wait_ge(h_ready, 3)
            pool.dma_start(lists, c_lists).then_inc(late_in, 16)
            pool.wait_ge(ln_read, 3)
            pool.dma_start(ln_g, ln2_g[0:1, :].broadcast_to([128, D])).then_inc(ln2_in, 16)
            pool.dma_start(ln_b, ln2_b[0:1, :].broadcast_to([128, D])).then_inc(ln2_in, 16)
            pool.wait_ge(stored, 16 * 2)

        @block.tensor
        def _(pe):
            mm = nc.tensor.matmul

            def claim(name):
                n = NO[name]
                if n >= 8:
                    pe.wait_ge(bank_free[n % 8], n // 8)
                return ps[n % 8]

            def weights_times(kind, i, rhs, chunks=KC, cols_per_unit=2):
                w = unit(kind, i // cols_per_unit).rearrange("p (c n) -> p c n", c=chunks)
                if i % cols_per_unit == 0:
                    pe.wait_ge(*unit_landed(kind, i // cols_per_unit))
                o = claim((kind, i))
                f0 = (i % cols_per_unit) * 128
                for c in range(chunks):
                    last = mm(o[:, 0:NT], w[:, c, f0:f0 + 128], rhs[:, c, :], start=c == 0, stop=c == chunks - 1)
                last.then_inc(full((kind, i))[0], 1)

            pe.wait_ge(cst_in, 16)
            pe.wait_ge(x_in, 48)
            for c in range(KC):
                o = claim(("xt", c))
                for t, (t0, n) in enumerate(TILES):
                    last = nc.tensor.transpose(o[:, t0:t0 + n], xr[0:n, t, c * 128:(c + 1) * 128], ident[0:n, 0:n])
                last.then_inc(full(("xt", c))[0], 1)
            pe.wait_ge(small_in, 16 * 6)
            o = claim(("cols",))
            nc.tensor.transpose(o[:, 0:26], rows, ident[0:26, 0:26]).then_inc(full(("cols",))[0], 1)
            pe.wait_ge(bgu_in, 32)
            o = claim(("bdt",))
            for c in range(8):
                last = nc.tensor.transpose(o[:, c * NE:(c + 1) * NE], bdn_rows[:, c * 128:(c + 1) * 128],
                                           ident[0:NE, 0:NE])
            last.then_inc(full(("bdt",))[0], 1)
            o = claim(("bgt",))
            for c in range(16):
                last = nc.tensor.transpose(o[:, c * NE:(c + 1) * NE], bgu_rows[:, c * 128:(c + 1) * 128],
                                           ident[0:NE, 0:NE])
            last.then_inc(full(("bgt",))[0], 1)
            pe.wait_ge(xt_ready, KC)
            o = claim(("lr",))
            for c in range(KC):
                last = mm(o[0:16, 0:NT], wlr[:, c, :], xt[:, c, :], start=c == 0, stop=c == KC - 1)
            last.then_inc(full(("lr",))[0], 1)
            for i in range(4):
                weights_times("k", i, xt)
            pe.wait_ge(lr_ready, 1)
            for i in range(4):
                o = claim(("gk", i))
                mm(o[:, 0:NT], wgk2[:, i * 128:(i + 1) * 128], lrt, start=True, stop=True)\
                    .then_inc(full(("gk", i))[0], 1)
            for i in range(4):
                weights_times("q", i, xt)
            for j in range(4):
                w = unit("v", j).rearrange("p (c n) -> p c n", c=KC)
                pe.wait_ge(*unit_landed("v", j))
                for t, (t0, n) in enumerate(TILES):
                    o = claim(("v", j, t))
                    for c in range(KC):
                        last = mm(o[0:n, 0:256], xt[:, c, t0:t0 + n], w[:, c, :], start=c == 0, stop=c == KC - 1)
                    last.then_inc(full(("v", j, t))[0], 1)
            for i in range(8):
                weights_times("g", i, xt)

            pe.wait_ge(qk_ready, 4)
            for t, (t0, n) in enumerate(TILES):
                o = claim(("a", t))
                for h in range(HEADS):
                    last = mm(o[0:n, h * n:(h + 1) * n], ke[:, h, t0:t0 + n], qe[:, h, t0:t0 + n], start=True, stop=True)
                last.then_inc(full(("a", t))[0], 1)
            for t, (t0, n) in enumerate(TILES):
                o = claim(("kt", t))
                for h in range(HEADS):
                    last = nc.tensor.transpose(o[0:n, h * 128:(h + 1) * 128], k[:, h, t0:t0 + n], ident)
                last.then_inc(full(("kt", t))[0], 1)
            pe.wait_ge(klt_ready, 3)
            pe.wait_ge(v_ready, 12)
            pe.wait_ge(at_ready, 3)
            for h in range(HEADS):
                for half in range(2):
                    o = claim(("kv", h, half))
                    for c2 in range(2):
                        p0 = half * C
                        last = mm(o[:, c2 * DV:(c2 + 1) * DV], klt[p0:p0 + C, c2, h * 128:(h + 1) * 128],
                                  v[p0:p0 + C, c2, h * DV:(h + 1) * DV], start=True, stop=True)
                    last.then_inc(full(("kv", h, half))[0], 1)
                pe.wait_ge(klm_ready, h + 1)
                for i in range(4):
                    o = claim(("kvs", h, i))
                    for half in range(2):
                        last = mm(o[:, half * DV:(half + 1) * DV], klm[:, 2 * i + half, :],
                                  v[0:NS, 2, h * DV:(h + 1) * DV], start=True, stop=True)
                    last.then_inc(full(("kvs", h, i))[0], 1)
                pe.wait_ge(sp_ready, 4 * (h + 1))
                pe.wait_ge(ss_in[h], 16)
                for vc in range(2):
                    o = claim(("o", h, vc))
                    f0 = h * DV + vc * 128
                    for t, (t0, n) in enumerate(TILES):
                        mm(o[:, t0:t0 + n], v[0:n, t, f0:f0 + 128], at_[0:n, t, h * n:(h + 1) * n],
                           start=t == 0, stop=False, skip_group_check=True)
                    for c in range(1, NP // C):
                        mm(o[:, c * C:(c + 1) * C], sp_st[:, h % 2, c - 1, vc * 128:(vc + 1) * 128],
                           q[:, h, c * C:(c + 1) * C], start=False, stop=False, skip_group_check=True)
                    for b in range(B):
                        s0 = NP + b * L
                        last = mm(o[:, s0:s0 + L], ss_st[h % 2][:, b, vc * 128:(vc + 1) * 128],
                                  q[:, h, s0:s0 + L], start=False, stop=b == B - 1, skip_group_check=True)
                    last.then_inc(full(("o", h, vc))[0], 1)
            for h in range(HEADS):
                pe.wait_ge(sq_ready, 2 * h + 2)
                o = claim(("rms", h))
                for vc in range(2):
                    last = mm(o[:, 0:NT], cst("ones"), sq[:, 2 * h + vc, :], start=vc == 0, stop=vc == 1)
                last.then_inc(full(("rms", h))[0], 1)
            for i in range(8):
                weights_times("ga", i, xt)
            pe.wait_ge(ot_ready, 1)
            for i in range(8):
                weights_times("ba", i, ot)
            for i in range(4):
                weights_times("u", i, xt)
            pe.wait_ge(late_in, 48)
            o = claim(("pb",))
            for g in range(4):
                last = nc.tensor.transpose(o[:, g * 120:(g + 1) * 120], spb[:, g * 128:(g + 1) * 128],
                                           ident[0:120, 0:120])
            last.then_inc(full(("pb",))[0], 1)
            pe.wait_ge(u_ready, 4)
            o = claim(("up",))
            for g in range(4):
                last = nc.tensor.transpose(o[0:PBUF, g * 128:(g + 1) * 128], up_pad[:, g, NP:NP + PBUF], ident)
            last.then_inc(full(("up",))[0], 1)
            pe.wait_ge(po_ready, 1)
            o = claim(("us",))
            for g in range(4):
                last = nc.tensor.transpose(o[0:NS, g * 128:(g + 1) * 128], po[:, g, NP:NT], ident)
            last.then_inc(full(("us",))[0], 1)
            for i in range(8):
                weights_times("gb", i, xt)
            for g in range(4):
                pe.wait_ge(po_ready, g + 2)
                o = claim(("grp", g))
                mm(o[:, 0:NT], wgrp[:, g, :], po[:, g, :], start=True, stop=True).then_inc(full(("grp", g))[0], 1)
            pe.wait_ge(pg_ready, 4)
            for i in range(8):
                weights_times("bb", i, pg, chunks=4, cols_per_unit=4)
            pe.wait_ge(merged, 8)
            for j in range(4):
                w = unit("out", j).rearrange("p (c n) -> p c n", c=KC)
                pe.wait_ge(*unit_landed("out", j))
                for t, (t0, n) in enumerate(TILES):
                    o = claim(("out", j, t))
                    for c in range(KC):
                        last = mm(o[0:n, 0:256], ga[:, c, t0:t0 + n], w[:, c, :], start=c == 0, stop=c == KC - 1)
                    last.then_inc(full(("out", j, t))[0], 1)
            pe.wait_ge(h_ready, 3)
            for c in range(KC):
                o = claim(("ht", c))
                for t, (t0, n) in enumerate(TILES):
                    last = nc.tensor.transpose(o[:, t0:t0 + n], hrow[0:n, t, c * 128:(c + 1) * 128], ident[0:n, 0:n])
                last.then_inc(full(("ht", c))[0], 1)
            pe.wait_ge(ht_ready, KC)
            for t, (t0, n) in enumerate(TILES):
                o = claim(("lg", t))
                for c in range(KC):
                    last = mm(o[0:n, 0:NE], ot[:, c, t0:t0 + n], wrt[:, c, :], start=c == 0, stop=c == KC - 1)
                last.then_inc(full(("lg", t))[0], 1)
            pe.wait_ge(mask_ready, 3)
            for t, (t0, n) in enumerate(TILES):
                o = claim(("rk", t))
                for s in range(t):
                    mm(o[0:n, 0:NE], cst("ones", n=n), msk[:, s, :], start=s == 0, stop=False)
                mm(o[0:n, 0:NE], cst("before", p=n, n=n), msk[0:n, t, :], start=t == 0, stop=True)\
                    .then_inc(full(("rk", t))[0], 1)
            o = claim(("cnt",))
            for t, (t0, n) in enumerate(TILES):
                last = mm(o[0:1, 0:NE], cst("ones", p=n, n=1), msk[0:n, t, :], start=t == 0, stop=t == 2)
            last.then_inc(full(("cnt",))[0], 1)
            for name in PRODUCTS[-8:]:
                pe.wait_ge(freed(name), NO[name] // 8 + 1)

            def gather(buf, n_onehot):
                pe.wait_ge(onehot_ready, n_onehot)
                for c in range(KC):
                    for t, (t0, n) in enumerate(TILES):
                        last = mm(ps[2][:, c * CAP:(c + 1) * CAP], hrow[0:n, t, c * 128:(c + 1) * 128],
                                  onehot[0:n, buf, t, :], start=c == 0 and t == 0, stop=t == 2, skip_group_check=True)
                last.then_inc(gathered, 1)

            def turn_slots(buf):
                mm(ps[6][0:CAP, 0:128], onehot[:, buf, 0, :], ident, start=True, stop=True)
                for t, (t0, n) in enumerate(TILES[1:], 1):
                    last = nc.tensor.transpose(ps[6][0:CAP, t0:t0 + n], onehot[0:n, buf, t, :], ident[0:n, 0:n])
                last.then_inc(slots_turned, 1)

            def expert_up(idx, buf, n_gathered):
                pe.wait_ge(xgt_ready, n_gathered)
                for j in range(UP_UNITS):
                    pe.wait_ge(filled[slot_of(j)], slot_count(idx, j))
                    w = ring[:, slot_of(j), :]
                    for f in range(16):
                        last = mm(ps[f // 8][:, (f % 8) * CAP:(f % 8 + 1) * CAP], w[:, f * 128:(f + 1) * 128],
                                  xgt[:, buf, j, :], start=j == 0 and f % 8 == 0, stop=j == UP_UNITS - 1,
                                  skip_group_check=True)
                    last.then_inc(units_used, 1)

            def expert_down(idx):
                pe.wait_ge(act_ready, idx + 1)
                for j in range(DOWN_UNITS):
                    s = slot_of(UP_UNITS + j)
                    pe.wait_ge(filled[s], slot_count(idx, UP_UNITS + j))
                    w = ring[:, s, :].rearrange("p (c n) -> p c n", c=2)
                    for c in range(2):
                        for f in range(KC):
                            last = mm(ps[3][:, f * CAP:(f + 1) * CAP], w[:, c, f * 128:(f + 1) * 128],
                                      actt[:, 2 * j + c, :], start=j == 0 and c == 0 and f == 0,
                                      stop=j == DOWN_UNITS - 1 and c == 1, skip_group_check=True)
                    last.then_inc(units_used, 1)

            def turn_output(idx):
                pe.wait_ge(ysb_ready, idx + 1)
                mm(ps[4][0:CAP, 0:128], ysb[:, 0, :], ident, start=True, stop=True)
                for f in range(1, KC):
                    last = nc.tensor.transpose(ps[4 + f // 4][0:CAP, (f % 4) * 128:(f % 4 + 1) * 128],
                                               ysb[:, f, :], ident)
                last.then_inc(yt_turned, 1)

            def scatter(idx, buf):
                pe.wait_ge(res_ready, idx + 1)
                pe.wait_ge(slot_ready, idx + 1)
                for i in range(6):
                    t, half = i // 2, i % 2
                    t0, n = TILES[t]
                    if i >= 2:
                        pe.wait_ge(added, idx * 6 + i - 1)
                    mm(ps[6 + i % 2][:, :], slot_t[:, buf, t0:t0 + 128], res[:, half * 512:(half + 1) * 512],
                       start=True, stop=True).then_inc(pieces, 1)

            def middle(idx, buf):
                expert_up(idx, buf, idx + 1)
                turn_output(idx - 1)
                gather(1 - buf, idx + 2)
                scatter(idx - 1, 1 - buf)
                expert_down(idx)
                pe.wait_ge(added, idx * 6)
                turn_slots(1 - buf)

            gather(0, 1)
            turn_slots(0)
            expert_up(0, 0, 1)
            gather(1, 2)
            expert_down(0)
            pe.wait_ge(slot_ready, 1)
            turn_slots(1)
            middle(1, 1)
            with pe.Fori(1, NE // 2) as it:
                middle(it * 2, 0)
                middle(it * 2 + 1, 1)
            turn_output(NE - 1)
            scatter(NE - 1, 1)
            pe.wait_ge(lists_ready, 1)
            count = pe.value_load(n_later[0:1, 0:1], min_val=0, max_val=RANKS)
            with pe.If(count > 0):
                with pe.Fori(0, count) as b:
                    gather(0, b + NE + 2)
                    pe.wait_ge(added, b * 6 + NE * 6)
                    turn_slots(0)
                    expert_up(b + NE, 0, b + NE + 2)
                    expert_down(b + NE)
                    turn_output(b + NE)
                    scatter(b + NE, 0)

        @block.scalar
        def _(act):
            A = nc.scalar.activation
            steps = [0]

            def link(ins):
                steps[0] += 1
                ins.then_inc(act_step, 1)
                act.wait_ge(act_step, steps[0])

            act.wait_ge(*full(("lr",)))
            A(lrt, bank(("lr",))[0:16, 0:NT], ACT.Copy).then_inc(lr_ready, 1)
            act.wait_ge(lr_ready, 1)
            act.sem_inc(freed(("lr",)), 1)
            for i in range(4):
                act.wait_ge(*full(("k", i)))
                A(k[:, i, :], bank(("k", i))[:, 0:NT], ACT.Copy).then_inc(freed(("k", i)), 1)
            act.wait_ge(z_ready, 1)
            link(A(ee[:, :, :], ee[:, :, :], ACT.Exp, scale=-1.0))
            A(ee[:, :, :], ee[:, :, :], ACT.Ln, bias=1.0).then_inc(soft_ready, 1)
            for i in range(4):
                act.wait_ge(*full(("q", i)))
                A(q[:, i, :], bank(("q", i))[:, 0:NT], ACT.Copy, scale=float(DK) ** -0.5)\
                    .then_inc(freed(("q", i)), 1)
            act.sem_inc(qk_in, 1)
            act.wait_ge(diff_ready, 1)
            A(qe[:, :, :], bb[:, :, :], ACT.Exp, scale=1.0 / 16).then_inc(exp_ready, 1)
            A(ke[:, :, :], bb[:, :, :], ACT.Exp, scale=-1.0 / 16).then_inc(exp_ready, 1)
            A(eb[:, :, :], ee[:, :, :], ACT.Exp, scale=1.0 / 16).then_inc(exp_ready, 1)
            A(bl[:, :, :], bl[:, :, :], ACT.Exp, scale=1.0 / 16).then_inc(exp_ready, 1)
            act.wait_ge(xt_ready, KC)
            for j in range(4):
                for t, (t0, n) in enumerate(TILES):
                    act.wait_ge(*full(("v", j, t)))
                    A(v[0:n, t, j * 256:(j + 1) * 256], bank(("v", j, t))[0:n, 0:256], ACT.Copy)\
                        .then_inc(freed(("v", j, t)), 1)
                    if t == 2:
                        pass
            act.sem_inc(v_ready, 12)
            for i in range(8):
                act.wait_ge(*full(("g", i)))
                A(gs[:, i, :], bank(("g", i))[:, 0:NT], ACT.Sigmoid).then_inc(sig_ready, 1)
            for t, (t0, n) in enumerate(TILES):
                act.wait_ge(*full(("kt", t)))
                A(klt[0:n, t, :], bank(("kt", t))[0:n, :], ACT.Copy).then_inc(klt_ready, 1)
            act.wait_ge(klt_ready, 3)
            for t in range(3):
                act.sem_inc(freed(("kt", t)), 1)
            for h in range(HEADS):
                for vc in range(2):
                    act.wait_ge(*full(("o", h, vc)))
                    A(sq[:, 2 * h + vc, :], bank(("o", h, vc))[:, 0:NT], ACT.Square).then_inc(sq_ready, 1)
                    A(ot[:, 2 * h + vc, :], bank(("o", h, vc))[:, 0:NT], ACT.Copy).then_inc(freed(("o", h, vc)), 1)
            for h in range(HEADS):
                act.wait_ge(*full(("rms", h)))
                A(rms[:, h, :], bank(("rms", h))[:, 0:NT], ACT.Sqrt, bias=eps_rms, scale=1.0 / DV)\
                    .then_inc(sqrt_ready, 1)
            act.wait_ge(sqrt_ready, 4)
            for h in range(HEADS):
                act.sem_inc(freed(("rms", h)), 1)
            act.wait_ge(stored_s, 16 * 4)
            for i in range(8):
                act.wait_ge(*full(("ga", i)))
                A(ga[:, i, :], bank(("ga", i))[:, 0:NT], ACT.Sigmoid, bias=cols[:, i:i + 1])\
                    .then_inc(freed(("ga", i)), 1)
            act.sem_inc(ga_ready, 1)
            act.wait_ge(pads_zero, 1)
            for i in range(4):
                act.wait_ge(*full(("u", i)))
                A(up_pad[:, i, PBUF:], bank(("u", i))[:, 0:NP], ACT.Copy)
                A(us_pad[:, i, :, PBUF:], bank(("u", i))[:, NP:NT].rearrange("p (b s) -> p b s", s=L), ACT.Copy)\
                    .then_inc(u_ready, 1)
            act.wait_ge(u_ready, 4)
            for i in range(4):
                act.sem_inc(freed(("u", i)), 1)
            for name, dst, n in ((("up",), pool_out_p, PBUF), (("us",), pool_out_s, NS)):
                act.wait_ge(*full(name))
                A(dst, bank(name)[0:n, :], ACT.Copy).then_inc(pool_out_ready, 1)
            act.wait_ge(pool_out_ready, 2)
            for name in (("up",), ("us",)):
                act.sem_inc(freed(name), 1)
            act.wait_ge(*full(("ba", 7)))
            for i in range(8):
                act.wait_ge(*full(("gb", i)))
                A(gb[:, i, :], bank(("gb", i))[:, 0:NT], ACT.Sigmoid, bias=cols[:, 8 + i:9 + i])\
                    .then_inc(freed(("gb", i)), 1)
            act.sem_inc(gb_ready, 1)
            for g in range(4):
                act.wait_ge(*full(("grp", g)))
                A(pg[:, g, :], bank(("grp", g))[:, 0:NT], ACT.Copy, scale=cols[:, 22 + g:23 + g])\
                    .then_inc(pg_ready, 1)
            act.wait_ge(pg_ready, 4)
            for g in range(4):
                act.sem_inc(freed(("grp", g)), 1)
            for t, (t0, n) in enumerate(TILES):
                act.wait_ge(var_ready, t + 1)
                A(rstd[0:n], mv[0:n, 1:2], ACT.Sqrt, bias=eps_ln[0:n]).then_inc(std_ready, 1)
            for c in range(KC):
                act.wait_ge(*full(("ht", c)))
                A(ot[:, c, :], bank(("ht", c))[:, 0:NT], ACT.Copy).then_inc(ht_ready, 1)
            act.wait_ge(ht_ready, KC)
            for c in range(KC):
                act.sem_inc(freed(("ht", c)), 1)
            for t, (t0, n) in enumerate(TILES):
                act.wait_ge(max_ready, t + 1)
                A(sm[0:n, 0:4], tmp8[0:n, 0:4], ACT.Exp).then_inc(soft4_ready, 1)

            def gathered_rows(buf, count):
                act.wait_ge(gathered, count)
                A(xgt[:, buf, :, :], ps[2][:, :].rearrange("p (c s) -> p c s", s=CAP), ACT.Copy)\
                    .then_inc(xgt_ready, 1)

            def swish(idx):
                act.wait_ge(gate_ready, idx + 1)
                A(sg[:, :, :], g1[:, :, :], ACT.Sigmoid, scale=GLU_ALPHA).then_inc(swish_ready, 1)

            def output_rows(idx):
                act.wait_ge(yt_turned, idx + 1)
                A(res[:, 0:512], ps[4][0:CAP, :], ACT.Copy)
                A(res[:, 512:1024], ps[5][0:CAP, :], ACT.Copy).then_inc(res_ready, 1)

            def middle(idx, buf):
                output_rows(idx - 1)
                swish(idx)
                gathered_rows(1 - buf, idx + 2)

            gathered_rows(0, 1)
            swish(0)
            gathered_rows(1, 2)
            middle(1, 1)
            with act.Fori(1, NE // 2) as it:
                middle(it * 2, 0)
                middle(it * 2 + 1, 1)
            output_rows(NE - 1)
            act.wait_ge(lists_ready, 1)
            count = act.value_load(n_later[0:1, 0:1], min_val=0, max_val=RANKS)
            with act.If(count > 0):
                with act.Fori(0, count) as b:
                    gathered_rows(0, b + NE + 2)
                    swish(b + NE)
                    output_rows(b + NE)
            for t, (t0, n) in enumerate(TILES):
                act.wait_ge(var_ready, t + 4)
                A(rstd[0:n], mv[0:n, 1:2], ACT.Sqrt, bias=eps_ln[0:n]).then_inc(std_ready, 1)

        @block.vector
        def _(dve):
            V = nc.vector
            steps = [0]

            def link(ins):
                steps[0] += 1
                ins.then_inc(dve_step, 1)
                dve.wait_ge(dve_step, steps[0])

            V.memset(eps_rms, RMS_EPS)
            V.memset(eps_ln, LN_EPS)
            for c in range(KC):
                dve.wait_ge(*full(("xt", c)))
                V.tensor_copy(xt[:, c, :], bank(("xt", c))[:, 0:NT]).then_inc(xt_ready, 1)
            dve.wait_ge(xt_ready, KC)
            for c in range(KC):
                dve.sem_inc(freed(("xt", c)), 1)
            for name, dst, n in ((("cols",), cols, 26), (("bdt",), reg(BDN, 256), 256), (("bgt",), reg(BGU, 512), 512)):
                dve.wait_ge(*full(name))
                V.tensor_copy(dst, bank(name)[:, 0:n]).then_inc(freed(name), 1)
            dve.wait_ge(freed(("cols",)), NO[("cols",)] // 8 + 1)
            for i in range(4):
                dve.wait_ge(*full(("gk", i)))
                V.tensor_scalar(bb[:, i, :], bank(("gk", i))[:, 0:NT], cols[:, 16 + i:17 + i], None, ALU.add)\
                    .then_inc(freed(("gk", i)), 1)
            for i in range(4):
                dve.wait_ge(freed(("gk", i)), NO[("gk", i)] // 8 + 1)
            V.scalar_tensor_tensor(ee[:, :, :], bb[:, :, :], -1.0, bb[:, :, :], ALU.mult, ALU.max).then_inc(z_ready, 1)
            dve.wait_ge(soft_ready, 1)
            link(V.scalar_tensor_tensor(bb[:, :, :], bb[:, :, :], 0.0, ee[:, :, :], ALU.min, ALU.subtract))
            dve.wait_ge(starts_in, 32)
            link(V.tensor_tensor_scan(reg(EE, HEADS * NT), starts, reg(BB, HEADS * NT), 0.0, ALU.mult, ALU.add))
            for t, n in ((0, C), (1, L)):
                cum, dif, rest = by_chunk(ee, t), by_chunk(bb, t), by_chunk(bl, t)
                shape = list(cum.shape)
                V.tensor_tensor(dif, cum, cum[:, :, :, n // 2:n // 2 + 1].broadcast_to(shape), ALU.subtract)
                last = V.tensor_tensor(rest, cum[:, :, :, n - 1:n].broadcast_to(shape), cum, ALU.subtract)
            last.then_inc(diff_ready, 1)
            dve.wait_ge(exp_ready, 4)
            dve.wait_ge(qk_in, 1)
            V.tensor_tensor(qe[:, :, :], qe[:, :, :], q[:, :, :], ALU.mult).then_inc(qk_ready, 1)
            V.tensor_tensor(ke[:, :, :], ke[:, :, :], k[:, :, :], ALU.mult).then_inc(qk_ready, 1)
            V.tensor_tensor(q[:, :, :], q[:, :, :], eb[:, :, :], ALU.mult).then_inc(qk_ready, 1)
            V.tensor_tensor(k[:, :, :], k[:, :, :], bl[:, :, :], ALU.mult).then_inc(qk_ready, 1)
            V.tensor_copy(dec[:, :, 0:4].rearrange("p h (c a) -> p h c a", a=1), by_chunk(eb, 0)[:, :, :, C - 1:C])
            link(V.tensor_copy(dec[:, :, 4:12].rearrange("p h (c a) -> p h c a", a=1), by_chunk(eb, 1)[:, :, :, L - 1:L]))
            link(V.memset(reg(BB, 1536), 0.0))
            for i in range(8):
                dve.wait_ge(*full(("g", i)))
                dve.wait_ge(sig_ready, i + 1)
                V.tensor_tensor(gs[:, i, :], gs[:, i, :], bank(("g", i))[:, 0:NT], ALU.mult)\
                    .then_inc(freed(("g", i)), 1)
            for t, (t0, n) in enumerate(TILES):
                dve.wait_ge(*full(("a", t)))
                m = cst("pmask" if t < 2 else "smask", p=n).bitcast(i32)
                for h in range(HEADS):
                    last = V.copy_predicated(at_[0:n, t, h * n:(h + 1) * n], m, bank(("a", t))[0:n, h * n:(h + 1) * n])
                last.then_inc(at_ready, 1)
            dve.wait_ge(at_ready, 3)
            for t in range(3):
                dve.sem_inc(freed(("a", t)), 1)
            dve.wait_ge(klt_ready, 3)
            dve.wait_ge(*full(("kt", 2)))
            for h in range(HEADS):
                if h:
                    dve.wait_ge(*full(("kvs", h - 1, 3)))
                V.tensor_tensor(klm, klt[0:NS, 2, h * 128:(h + 1) * 128].unsqueeze(1).broadcast_to([NS, B, DK]),
                                cst("bmask", p=NS).unsqueeze(2).broadcast_to([NS, B, DK]), ALU.mult)\
                    .then_inc(klm_ready, 1)
                if h >= 2:
                    dve.wait_ge(stored_p, 16 * (h - 1))
                for c in range(4):
                    name = ("kv", h, c % 2)
                    src = bank(name)[:, (c // 2) * DV:(c // 2 + 1) * DV]
                    dve.wait_ge(*full(name))
                    if c == 0:
                        V.tensor_copy(sp_st[:, h % 2, 0, :], src).then_inc(sp_ready, 1)
                    else:
                        dve.wait_ge(sp_ready, 4 * h + c)
                        V.scalar_tensor_tensor(sp_st[:, h % 2, c, :], sp_st[:, h % 2, c - 1, :], dec[:, h, c:c + 1],
                                               src, ALU.mult, ALU.add).then_inc(sp_ready, 1)
                dve.wait_ge(sp_ready, 4 * h + 4)
                dve.sem_inc(freed(("kv", h, 0)), 1)
                dve.sem_inc(freed(("kv", h, 1)), 1)
                dve.wait_ge(*full(("o", h, 1)))
                for b in range(B):
                    name = ("kvs", h, b // 2)
                    ins = V.scalar_tensor_tensor(ss_st[h % 2][:, b, :], ss_st[h % 2][:, b, :], dec[:, h, 4 + b:5 + b],
                                                 bank(name)[:, (b % 2) * DV:(b % 2 + 1) * DV], ALU.mult, ALU.add)
                    if b % 2:
                        ins.then_inc(freed(name), 1)
                for i in range(4):
                    name = ("kvs", h, i)
                    dve.wait_ge(freed(name), NO[name] // 8 + 1)
                dve.sem_inc(ss_ready, 1)
            dve.wait_ge(sqrt_ready, 4)
            link(V.reciprocal(rms[:, :, :], rms[:, :, :]))
            dve.wait_ge(freed(("o", 3, 1)), NO[("o", 3, 1)] // 8 + 1)
            dve.wait_ge(freed(("o", 3, 0)), NO[("o", 3, 0)] // 8 + 1)
            for i in range(8):
                last = V.scalar_tensor_tensor(ot[:, i, :], ot[:, i, :], cols[:, 20 + i % 2:21 + i % 2], rms[:, i // 2, :],
                                              ALU.mult, ALU.mult)
            link(last)
            V.tensor_tensor(ot[:, :, :], ot[:, :, :], gs[:, :, :], ALU.mult).then_inc(ot_ready, 1)
            V.memset(up_pad[:, :, 0:PBUF], 0.0).then_inc(pads_zero, 1)
            dve.wait_ge(ga_ready, 1)
            for i in range(8):
                dve.wait_ge(*full(("ba", i)))
                V.tensor_tensor(ga[:, i, :], ga[:, i, :], bank(("ba", i))[:, 0:NT], ALU.mult)\
                    .then_inc(freed(("ba", i)), 1)
            dve.wait_ge(*full(("pb",)))
            V.tensor_copy(us_pad[:, :, :, 0:PBUF].rearrange("p g b r -> p (g b) r"),
                          bank(("pb",))[:, 0:480].rearrange("p (g r) -> p g r", r=PBUF)).then_inc(freed(("pb",)), 1)
            dve.wait_ge(u_ready, 4)
            dve.wait_ge(freed(("pb",)), NO[("pb",)] // 8 + 1)
            for g in range(4):
                last = V.tensor_copy(po[:, g, NP:NT].rearrange("p (b s) -> p b s", s=L), us_pad[:, g, :, PBUF:])
            last.then_inc(po_ready, 1)
            dve.wait_ge(*full(("us",)))
            win = [(reg(EE, PBUF + NP), ar[:, EE + 271:EE + 271 + 184].rearrange("p (b s) -> p b s", b=B)),
                   (reg(EE + 455, PBUF + NP), ar[:, EE + 726:EE + 910].rearrange("p (b s) -> p b s", b=B))]
            for g in range(4):
                cp, cs = up_pad[:, g, :], us_pad[:, g, :, :]
                lo = 0
                for s in range(g + 1):
                    step = 2 ** s
                    lo += step
                    np_, ns_ = win[s % 2]
                    V.tensor_tensor(np_[:, lo:], cp[:, lo:], cp[:, lo - step:PBUF + NP - step], ALU.add)
                    link(V.tensor_tensor(ns_[:, :, lo:], cs[:, :, lo:], cs[:, :, lo - step:PBUF + L - step], ALU.add))
                    cp, cs = np_, ns_
                w = 2.0 ** -(g + 1)
                at = CST["rcnt"][0] + CONST + 16 * g
                link(V.tensor_tensor(win[(g + 1) % 2][0][:, 0:16], cp[:, PBUF:PBUF + 16], ar[:, at:at + 16], ALU.mult))
                V.tensor_tensor(po[:, g, 0:16], win[(g + 1) % 2][0][:, 0:16], up_pad[:, g, PBUF:PBUF + 16], ALU.subtract)
                V.scalar_tensor_tensor(po[:, g, 16:NP], cp[:, PBUF + 16:], w, up_pad[:, g, PBUF + 16:], ALU.mult,
                                       ALU.subtract)
                V.scalar_tensor_tensor(po[:, g, NP:NT].rearrange("p (b s) -> p b s", s=L), cs[:, :, PBUF:], w,
                                       us_pad[:, g, :, PBUF:], ALU.mult, ALU.subtract).then_inc(po_ready, 1)
                dve.wait_ge(po_ready, g + 2)
            dve.wait_ge(gb_ready, 1)
            for i in range(8):
                dve.wait_ge(*full(("bb", i)))
                ins = V.tensor_tensor(gb[:, i, :], gb[:, i, :], bank(("bb", i))[:, 0:NT], ALU.mult)
                ins.then_inc(freed(("bb", i)), 1)
                dve.wait_ge(freed(("bb", i)), NO[("bb", i)] // 8 + 1)
                V.tensor_tensor(ga[:, i, :], ga[:, i, :], gb[:, i, :], ALU.add).then_inc(merged, 1)
            dve.wait_ge(x_again, 48)
            for j in range(4):
                for t, (t0, n) in enumerate(TILES):
                    dve.wait_ge(*full(("out", j, t)))
                    part = xr[0:n, t, j * 256:(j + 1) * 256]
                    V.scalar_tensor_tensor(part, part, ALPHA, bank(("out", j, t))[0:n, 0:256], ALU.mult, ALU.add)\
                        .then_inc(freed(("out", j, t)), 1)
            for t in range(3):
                dve.wait_ge(freed(("out", 3, t)), NO[("out", 3, t)] // 8 + 1)

            def layer_norm(src, dst, n, count, done):
                for i in range(2):
                    last = V.bn_stats(st6[0:n, i, :], src[:, i * 512:(i + 1) * 512])
                link(last)
                V.bn_aggr(mv[0:n], st6[0:n, :, :]).then_inc(var_ready, 1)
                dve.wait_ge(std_ready, count)
                link(V.reciprocal(rstd[0:n], rstd[0:n]))
                link(V.tensor_scalar(dst, src, mv[0:n, 0:1], rstd[0:n], ALU.subtract, ALU.mult))
                link(V.tensor_tensor(dst, dst, ln_g[0:n], ALU.mult))
                V.tensor_tensor(dst, dst, ln_b[0:n], ALU.add).then_inc(done, 1)

            dve.wait_ge(ln1_in, 32)
            for t, (t0, n) in enumerate(TILES):
                layer_norm(xr[0:n, t, :], hrow[0:n, t, :], n, t + 1, h_ready)
            dve.sem_inc(ln_read, 3)
            dve.wait_ge(h_ready, 3)
            for t, (t0, n) in enumerate(TILES):
                V.tensor_scalar(y[0:n, t, :], hrow[0:n, t, :], ALPHA, None, ALU.mult)
            for t, (t0, n) in enumerate(TILES):
                dve.wait_ge(*full(("lg", t)))
                link(V.tensor_tensor(lg[0:n, t, :], bank(("lg", t))[0:n, 0:NE], brt[0:n], ALU.add))
                link(V.max(mx[0:n], lg[0:n, t, :]))
                V.max_index(top_idx[0:n, :], mx[0:n], lg[0:n, t, :]).then_inc(freed(("lg", t)), 1)
                dve.wait_ge(freed(("lg", t)), NO[("lg", t)] // 8 + 1)
                V.tensor_scalar(tmp8[0:n, 0:4], mx[0:n, 0:4], mx[0:n, 0:1], None, ALU.subtract).then_inc(max_ready, 1)
                V.tensor_copy(idxf[0:n], top_idx[0:n, :])
                dve.wait_ge(soft4_ready, t + 1)
                link(V.reduce_sum(rstd[0:n], sm[0:n, 0:4], mybir.AxisListType.X))
                link(V.reciprocal(rstd[0:n], rstd[0:n]))
                link(V.tensor_scalar(sm[0:n, 0:4], sm[0:n, 0:4], rstd[0:n], None, ALU.mult))
                for i in range(TOPK):
                    last = V.tensor_scalar(oh[0:n, i, :], cst("iota32", p=n), idxf[0:n, i:i + 1], None, ALU.is_equal)
                link(last)
                link(V.tensor_tensor(msk[0:n, t, :], oh[0:n, 0, :], oh[0:n, 1, :], ALU.add))
                link(V.tensor_tensor(msk[0:n, t, :], msk[0:n, t, :], oh[0:n, 2, :], ALU.add))
                V.tensor_tensor(msk[0:n, t, :], msk[0:n, t, :], oh[0:n, 3, :], ALU.add).then_inc(mask_ready, 1)
                link(V.tensor_scalar(gw[0:n, t, :], oh[0:n, 0, :], sm[0:n, 0:1], None, ALU.mult))
                for i in range(1, TOPK):
                    link(V.scalar_tensor_tensor(gw[0:n, t, :], oh[0:n, i, :], sm[0:n, i:i + 1], gw[0:n, t, :],
                                                ALU.mult, ALU.add))
            for t, (t0, n) in enumerate(TILES):
                dve.wait_ge(*full(("rk", t)))
                link(V.scalar_tensor_tensor(rank[0:n, t, 0:NE], bank(("rk", t))[0:n, 0:NE], 1.0, msk[0:n, t, :],
                                            ALU.add, ALU.mult))
                link(V.tensor_scalar(rank[0:n, t, 0:NE], rank[0:n, t, 0:NE], -1.0, None, ALU.add))
                for p in range(1, PASSES):
                    last = V.tensor_scalar(rank[0:n, t, p * NE:(p + 1) * NE], rank[0:n, t, 0:NE], -float(CAP * p),
                                           None, ALU.add)
                last.then_inc(freed(("rk", t)), 1)
            for t in range(3):
                dve.wait_ge(freed(("rk", t)), NO[("rk", t)] // 8 + 1)
            dve.wait_ge(*full(("cnt",)))
            dve.wait_ge(late_in, 16 * (4 + B))
            V.tensor_copy(sm[0:1, 0:1], bank(("cnt",))[0:1, 0:1])
            cnt4 = bank(("cnt",))[0:1, 0:NE].unsqueeze(1).broadcast_to([1, PASSES - 1, NE])
            link(V.tensor_tensor(found[:, 0:NID].rearrange("p (a e) -> p a e", e=NE), cnt4,
                                 lists[:, NID:2 * NID].rearrange("p (a e) -> p a e", e=NE), ALU.is_gt))
            link(V.reduce_sum(low[:, 0:1], found[:, 0:NID], mybir.AxisListType.X))
            V.tensor_copy(n_later[0:1, 0:1], low[:, 0:1])
            link(V.tensor_tensor(found[:, 0:NID], found[:, 0:NID], lists[:, 0:NID], ALU.mult))
            for r in range(RANKS // 8):
                src = found[:, (r % 2) * NID:(r % 2 + 1) * NID]
                dst = found[:, (1 - r % 2) * NID:(2 - r % 2) * NID]
                link(V.max(top24[:, 8 * r:8 * r + 8], src))
                if r < RANKS // 8 - 1:
                    link(V.match_replace(dst, top24[:, 8 * r:8 * r + 8], src, 0.0))
            link(V.tensor_copy(later[0:1, 0, :], top24))
            V.tensor_scalar(later[0:1, 1, :], later[0:1, 0, :], NE - 1, None, ALU.bitwise_and).then_inc(lists_ready, 1)
            dve.wait_ge(lists_ready, 1)
            dve.sem_inc(freed(("cnt",)), 1)

            def make_onehot(buf, col):
                for t, (t0, n) in enumerate(TILES):
                    last = V.tensor_scalar(onehot[0:n, buf, t, :], cst("iota64", p=n), rank[0:n, t, ds(col, 1)], None,
                                           ALU.is_equal)
                last.then_inc(onehot_ready, 1)

            def keep_slots(idx, buf, count):
                dve.wait_ge(slots_turned, count)
                V.tensor_copy(slot_t[:, buf, 0:NT], ps[6][0:CAP, 0:NT]).then_inc(slot_ready, 1)

            def keep_output(idx, e):
                dve.wait_ge(units_used, (idx + 1) * EXP_UNITS)
                V.tensor_tensor(ysb[:, :, :], ps[3][:, :].rearrange("p (c s) -> p c s", s=CAP),
                                bdn[:, :, ds(e, 1)].broadcast_to([128, KC, CAP]), ALU.add).then_inc(ysb_ready, 1)

            def gated(idx, e, base):
                dve.wait_ge(units_used, idx * EXP_UNITS + UP_UNITS)
                V.tensor_tensor(g1[:, :, :], ps[0][:, :].rearrange("p (c s) -> p c s", s=CAP),
                                bgu[:, 0:8, ds(e, 1)].broadcast_to([128, KC, CAP]), ALU.add).then_inc(blk, 1)
                V.tensor_tensor(u1[:, :, :], ps[1][:, :].rearrange("p (c s) -> p c s", s=CAP),
                                bgu[:, 8:16, ds(e, 1)].broadcast_to([128, KC, CAP]), ALU.add).then_inc(blk, 1)
                dve.wait_ge(blk, base + 1)
                V.tensor_scalar(g1[:, :, :], g1[:, :, :], LIMIT, None, ALU.min).then_inc(gate_ready, 1)
                dve.wait_ge(blk, base + 2)
                V.tensor_scalar(u1[:, :, :], u1[:, :, :], LIMIT, -LIMIT, ALU.min, ALU.max).then_inc(blk, 1)
                dve.wait_ge(blk, base + 3)
                dve.wait_ge(gate_ready, idx + 1)
                V.scalar_tensor_tensor(u1[:, :, :], u1[:, :, :], 1.0, g1[:, :, :], ALU.add, ALU.mult).then_inc(blk, 1)
                dve.wait_ge(blk, base + 4)
                dve.wait_ge(swish_ready, idx + 1)
                V.tensor_tensor(actt[:, :, :], u1[:, :, :], sg[:, :, :], ALU.mult).then_inc(act_ready, 1)

            def add_pieces(idx, e):
                for i in range(6):
                    t, half = i // 2, i % 2
                    n = TILES[t][1]
                    dve.wait_ge(pieces, idx * 6 + i + 1)
                    part = y[0:n, t, half * 512:(half + 1) * 512]
                    V.scalar_tensor_tensor(part, ps[6 + i % 2][0:n, :], gw[0:n, t, ds(e, 1)], part, ALU.mult, ALU.add)\
                        .then_inc(added, 1)

            def middle(idx, buf):
                e = idx if idx.__class__ is int else dve.snap(idx)
                keep_output(e - 1, e - 1)
                keep_slots(e, buf, e + 1)
                make_onehot(1 - buf, e + 1)
                gated(e, e, e * 4)
                add_pieces(e - 1, e - 1)

            V.memset(slot_t[:, :, NT:], 0.0)
            make_onehot(0, 0)
            keep_slots(0, 0, 1)
            make_onehot(1, 1)
            gated(0, 0, 0)
            middle(1, 1)
            with dve.Fori(1, NE // 2) as it:
                middle(it * 2, 0)
                middle(it * 2 + 1, 1)
            keep_output(NE - 1, NE - 1)
            add_pieces(NE - 1, NE - 1)
            count = dve.value_load(n_later[0:1, 0:1], min_val=0, max_val=RANKS)
            with dve.If(count > 0):
                with dve.Fori(0, count) as b:
                    col = dve.value_load(later[0:1, 0, ds(b, 1)], min_val=0, max_val=NE * PASSES - 1)
                    e = dve.value_load(later[0:1, 1, ds(b, 1)], min_val=0, max_val=NE - 1)
                    dve.wait_ge(slots_turned, b + NE + 1)
                    make_onehot(0, col)
                    keep_slots(0, 0, b + NE + 2)
                    gated(b + NE, e, b * 4 + NE * 4)
                    keep_output(b + NE, e)
                    add_pieces(b + NE, e)
            dve.wait_ge(ln2_in, 32)
            dve.wait_ge(added, 6 * NE)
            for t, (t0, n) in enumerate(TILES):
                layer_norm(y[0:n, t, :], y[0:n, t, :], n, t + 4, y_final)


INPUTS = ["x_prompt", "x_sample", "state_gla", "state_pool", "w_in", "w_gk2", "b_gk", "gla_norm_w", "w_branch_gla",
          "w_pool_grp", "pool_scale", "w_branch_pool", "b_gates", "w_out", "ln1_g", "ln1_b", "w_router", "b_router",
          "w_gu", "b_gu", "w_down", "b_down", "ln2_g", "ln2_b"]
OUTPUTS = [(1, NP, D), (B, L, D), (1, 1, HEADS, DK, DV), (1, 1, PBUF, 512), (1, B, HEADS, DK, DV), (1, B, PBUF, 512)]


def kernel(**inputs):
    import numpy as _np
    import concourse.bacc as _bacc
    from concourse import mybir as _mybir
    from concourse.bass_utils import run_bass_kernel_spmd as _run

    nc = _bacc.Bacc("TRN2", target_bir_lowering=False, num_devices=1)
    arrays, args = {}, []
    named = [(n, _np.ascontiguousarray(inputs[n])) for n in INPUTS]
    named += list(zip(("c_cols", "c_starts", "c_lists"), constants()))
    for name, a in named:
        arrays[f"in_{name}"] = a
        args.append(nc.dram_tensor(f"in_{name}", a.shape, _mybir.dt.from_np(a.dtype), kind="ExternalInput").ap())
    for i, shape in enumerate(OUTPUTS):
        args.append(nc.dram_tensor(f"out_{i}", shape, _mybir.dt.float32, kind="ExternalOutput").ap())
    build(nc, *args)
    r = _run(nc, [arrays], core_ids=[0])
    return tuple(r.results[0][f"out_{i}"] for i in range(len(OUTPUTS)))
```

```python
from contextlib import ExitStack

import concourse.bass as bass
from concourse import mybir

D = 1024
KC = D // 128
NP, B, L = 256, 8, 8
NS = B * L
NT = NP + NS
HEADS, DK, DV = 4, 128, 256
C = 64
PBUF = 15
WMAX = 16
NE, TOPK = 32, 4
CAP = 64
PASSES = NT // CAP
RANKS = 24
ALPHA = 2.0 ** 0.25
LIMIT, GLU_ALPHA = 7.0, 1.702
RMS_EPS, LN_EPS = 1e-6, 1e-5
TILES = [(0, 128), (128, 128), (256, 64)]

RING = 12
UNIT = 2048
MIX_UNITS = ([("k", i) for i in range(2)] + [("q", i) for i in range(2)] + [("v", i) for i in range(4)]
             + [("g", i) for i in range(4)] + [("ga", i) for i in range(4)] + [("ba", i) for i in range(4)]
             + [("u", i) for i in range(2)] + [("gb", i) for i in range(4)] + [("bb", i) for i in range(2)]
             + [("out", i) for i in range(4)])
UNIT_NO = {u: n for n, u in enumerate(MIX_UNITS)}
NMIX = len(MIX_UNITS)
UP_UNITS, DOWN_UNITS = KC, KC // 2
EXP_UNITS = UP_UNITS + DOWN_UNITS
COL0 = {"q": 0, "k": 512, "v": 1024, "lr": 2048, "g": 2064, "u": 3088, "ga": 3600, "gb": 4624}

PRODUCTS = ([("xt", i) for i in range(KC)] + [("cols",), ("bgt",), ("lr",)]
            + [("k", i) for i in range(4)] + [("gk", i) for i in range(4)] + [("q", i) for i in range(4)]
            + [("v", j, t) for j in range(4) for t in range(3)] + [("g", i) for i in range(8)]
            + [("a", t) for t in range(3)] + [("kt", t) for t in range(3)]
            + [x for h in range(HEADS) for x in
               [("kv", h, 0), ("kv", h, 1)] + [("kvs", h, i) for i in range(4)] + [("o", h, 0), ("o", h, 1)]]
            + [("rms", h) for h in range(HEADS)]
            + [("ga", i) for i in range(8)] + [("ba", i) for i in range(8)] + [("u", i) for i in range(4)]
            + [("pb",), ("up",), ("us",)] + [("gb", i) for i in range(8)] + [("grp", i) for i in range(4)]
            + [("bb", i) for i in range(8)] + [("out", j, t) for j in range(4) for t in range(3)]
            + [("ht", i) for i in range(KC)] + [("lg", t) for t in range(3)] + [("rk", t) for t in range(3)]
            + [("cnt",), ("gwt",)] + [("yb", t, i) for t in range(3) for i in range(2)])
NO = {p: n for n, p in enumerate(PRODUCTS)}
NPROD = len(PRODUCTS)

CST = {}
NCST = 0
for _name, _n in (("ident", 128), ("ones", 128), ("pmask", 128), ("smask", 64), ("before", 128),
                  ("iota64", 64), ("iota32", 32), ("bmask", B), ("rcnt", 64)):
    CST[_name] = (NCST, _n)
    NCST += _n


def constants():
    import numpy as np
    c = np.zeros((128, NCST), np.float32)
    p = np.arange(128)

    def put(name, value):
        at, n = CST[name]
        c[:, at:at + n] = value
    i = np.arange(128)
    put("ident", p[:, None] == i)
    put("ones", 1.0)
    put("pmask", (p[:, None] // C == i // C) & (p[:, None] <= i))
    j = np.arange(64)
    put("smask", (p[:, None] // L == j // L) & (p[:, None] <= j))
    put("before", p[:, None] < i)
    put("iota64", j)
    put("iota32", np.arange(32))
    put("bmask", p[:, None] // L == np.arange(B))
    t = np.arange(16)
    put("rcnt", np.concatenate([1.0 / np.minimum(2 ** (g + 1), t + 1) for g in range(4)]))
    starts = np.ones((128, HEADS, NT), np.float32)
    starts[:, :, 0:NP:C] = 0.0
    starts[:, :, NP:NT:L] = 0.0
    ids = np.arange(NE, NE * PASSES, dtype=np.float32)
    lists = np.stack([ids, (ids // NE) * CAP])
    return c, starts.reshape(128, HEADS * NT), lists.reshape(1, -1)


NID = NE * (PASSES - 1)

XT = 0
QR = 2560
KR = 3840
QE = 5120
KE = 6400
BB = 7680
EE = 8960
VR = 10240
KLT = 13312
OT = 14848
SP = 17408
SS = 19456
G = 21504
GA = 24064
CONST = 26624
BGU = CONST + NCST
COLS = BGU + 512
DEC = COLS + 32
BR = DEC + 48
MISC = BR + 32
ARENA = MISC + 64
H = 0
Y = 3072
XGT = 6144
OH = 7168
OHW = 7552
ACTT = 7936
G1 = 8448
U1 = 8960
SG = 9472
HG = 9984
HU = 10496
RES = 11008
ST = 12032
RK = 12352
GW = 12832
MSK = 12928
LG = 13024
MX = 13120
RT = 13152
LISTS = 13280
GWT = 13864
BDR = 14184


def build(nc, x_p, x_s, state_gla, state_pool, w_in, w_gk2, b_gk, gla_norm_w, w_bgla, w_grp, pool_scale,
          w_bpool, b_gates, w_out, ln1_g, ln1_b, w_router, b_router, w_gu, b_gu, w_down, b_down, ln2_g, ln2_b,
          c_cols, c_starts, c_lists, y_p, y_s, ngp, npp, ngs, nps):
    f32 = mybir.dt.float32
    i32 = mybir.dt.int32
    u32 = mybir.dt.uint32
    ALU = mybir.AluOpType
    ACT = mybir.ActivationFunctionType
    ds = bass.ds

    with ExitStack() as ctx:
        def sem(name):
            return ctx.enter_context(nc.semaphore(name))

        ar = ctx.enter_context(nc.sbuf_tensor("arena", [128, ARENA], f32))
        ring = ctx.enter_context(nc.sbuf_tensor("ring", [128, RING, UNIT], f32))
        top_idx = ctx.enter_context(nc.sbuf_tensor("top_idx", [128, 8], u32))
        later = ctx.enter_context(nc.sbuf_tensor("later", [1, 2, RANKS], i32))
        n_later = ctx.enter_context(nc.sbuf_tensor("n_later", [1, 8], i32))
        ps = [ctx.enter_context(nc.psum_tensor(f"bank{i}", [128, 512], f32)) for i in range(8)]

        def reg(at, n, *dims, p=128, p0=0):
            v = ar[p0:p0 + p, at:at + n]
            if len(dims) == 1:
                v = v.rearrange("p (a b) -> p a b", a=dims[0])
            if len(dims) == 2:
                v = v.rearrange("p (a b c) -> p a b c", a=dims[0], b=dims[1])
            return v

        def cst(name, p=128, n=None):
            at, full = CST[name]
            return ar[0:p, CONST + at:CONST + at + (n or full)]

        ident = cst("ident")
        xt = reg(XT, KC * NT, KC)
        q = reg(QR, HEADS * NT, HEADS)
        k = reg(KR, HEADS * NT, HEADS)
        qe = reg(QE, HEADS * NT, HEADS)
        ke = reg(KE, HEADS * NT, HEADS)
        bb = reg(BB, HEADS * NT, HEADS)
        ee = reg(EE, HEADS * NT, HEADS)
        xr = reg(VR, 3 * D, 3)
        v = xr
        klt = reg(KLT, 3 * 512, 3)
        ot = reg(OT, 8 * NT, 8)
        starts = reg(OT, HEADS * NT)
        eb = reg(OT + HEADS * NT, HEADS * NT, HEADS)
        bl = reg(SP, HEADS * NT, HEADS)
        at_ = reg(BB, 3 * 512, 3)
        sq = reg(QE, 8 * NT, 8)
        rms = reg(BB, HEADS * NT, HEADS)
        sp_st = reg(SP, 2 * 4 * DV, 2, 4)
        ss_st = [reg(SS, B * DV, B), reg(GA, B * DV, B)]
        gs = reg(G, 8 * NT, 8)
        ga = reg(GA, 8 * NT, 8)
        gb = reg(OT, 8 * NT, 8)
        klm = reg(KR, B * DK, B, p=NS)
        pg = reg(QR, 4 * NT, 4)
        po = reg(KR, 4 * NT, 4)
        up_pad = reg(QE, 4 * (PBUF + NP), 4)
        us_pad = reg(QE + 4 * (PBUF + NP), 4 * B * (PBUF + L), 4, B)
        spb = reg(SP, 512, p=B * PBUF)
        wgrp = reg(SP + 512, 512, 4)
        wrt = reg(SP + 1024, 256, KC)
        pool_out_p = ar[0:PBUF, SP + 1280:SP + 1792]
        pool_out_s = ar[0:NS, SS:SS + 512]
        ln_g = reg(G, D)
        ln_b = reg(G + D, D)
        wlr = reg(KE, KC * 16, KC)
        wgk2 = ar[0:16, KE + 128:KE + 640]
        lrt = ar[0:16, KE + 640:KE + 960]
        rows = ar[0:26, KE + 960:KE + 1088]
        bgu_rows = ar[0:NE, G:G + 2048]
        bdn_rows = ar[0:NE, BDR:BDR + D]
        gwt = ar[0:NE, GWT:GWT + NT]
        bgu = reg(BGU, 512, 16)
        cols = reg(COLS, 26)
        dec = reg(DEC, 48, HEADS)
        brt = reg(BR, NE)
        hrow = reg(H, 3 * D, 3)
        y = reg(Y, 3 * D, 3)
        xgt = reg(XGT, 1024, KC)
        onehot = reg(OH, 3 * 128, 3)
        onehot_w = reg(OHW, 3 * 128, 3)
        actt = reg(ACTT, 512, KC)
        g1 = reg(G1, 512, KC)
        u1 = reg(U1, 512, KC)
        sg = reg(SG, 512, KC)
        hg = reg(HG, 512)
        hu = reg(HU, 512)
        res = reg(RES, D)
        slot_t = reg(ST, NT)
        rank = reg(RK, 3 * PASSES * NE, 3)
        gw = reg(GW, 3 * NE, 3)
        msk = reg(MSK, 3 * NE, 3)
        lg = reg(LG, 3 * NE, 3)
        mx = reg(MX, 8)
        oh = reg(RT, 4 * NE, 4)
        lists = ar[0:1, LISTS:LISTS + 2 * NID]
        found = ar[0:1, LISTS + 2 * NID:LISTS + 4 * NID]
        st6 = reg(MISC, 12, 2)
        mv = reg(MISC + 12, 2)
        rstd = reg(MISC + 14, 1)
        eps_rms = reg(MISC + 16, 1)
        eps_ln = reg(MISC + 17, 1)
        tmp8 = reg(MISC + 18, 8)
        idxf = reg(MISC + 26, 8)
        sm = reg(MISC + 34, 8)
        top24 = ar[0:1, LISTS + 4 * NID:LISTS + 4 * NID + RANKS]
        low = ar[0:1, LISTS + 4 * NID + RANKS:LISTS + 4 * NID + 2 * RANKS]

        filled = [sem(f"slot{i}_filled") for i in range(RING)]
        bank_full = [sem(f"bank{i}_full") for i in range(8)]
        bank_free = [sem(f"bank{i}_free") for i in range(8)]
        x_in = sem("x_in")
        cst_in = sem("cst_in")
        small_in = sem("small_in")
        bgu_in = sem("bgu_in")
        starts_in = sem("starts_in")
        ss_in = [sem(f"ss_in{i}") for i in range(HEADS)]
        x_again = sem("x_again")
        late_in = sem("late_in")
        ln1_in = sem("ln1_in")
        ln2_in = sem("ln2_in")
        stored_s = sem("stored_s")
        stored_p = sem("stored_p")
        stored = sem("stored")
        y_stored = sem("y_stored")
        xt_ready = sem("xt_ready")
        cols_ready = sem("cols_ready")
        lr_ready = sem("lr_ready")
        z_ready = sem("z_ready")
        soft_ready = sem("soft_ready")
        diff_ready = sem("diff_ready")
        exp_ready = sem("exp_ready")
        qk_in = sem("qk_in")
        qk_ready = sem("qk_ready")
        v_ready = sem("v_ready")
        sig_ready = sem("sig_ready")
        g_ready = sem("g_ready")
        at_ready = sem("at_ready")
        klt_ready = sem("klt_ready")
        klm_ready = sem("klm_ready")
        sp_ready = sem("sp_ready")
        ss_ready = sem("ss_ready")
        sq_ready = sem("sq_ready")
        sqrt_ready = sem("sqrt_ready")
        ot_ready = sem("ot_ready")
        ga_ready = sem("ga_ready")
        merged = sem("merged")
        pads_zero = sem("pads_zero")
        u_ready = sem("u_ready")
        pb_ready = sem("pb_ready")
        po_ready = sem("po_ready")
        pg_ready = sem("pg_ready")
        pool_out_ready = sem("pool_out_ready")
        gb_ready = sem("gb_ready")
        var_ready = sem("var_ready")
        std_ready = sem("std_ready")
        h_ready = sem("h_ready")
        ln_read = sem("ln_read")
        ht_ready = sem("ht_ready")
        mask_ready = sem("mask_ready")
        max_ready = sem("max_ready")
        soft4_ready = sem("soft4_ready")
        soft4_done = sem("soft4_done")
        gwt_ready = sem("gwt_ready")
        lists_ready = sem("lists_ready")
        y_final = sem("y_final")
        dve_step = sem("dve_step")
        act_step = sem("act_step")
        onehot_ready = sem("onehot_ready")
        onehot_w_ready = sem("onehot_w_ready")
        gathered = sem("gathered")
        xgt_ready = sem("xgt_ready")
        slots_turned = sem("slots_turned")
        slot_ready = sem("slot_ready")
        up_used = sem("up_used")
        down_used = sem("down_used")
        hg_ready = sem("hg_ready")
        hu_ready = sem("hu_ready")
        turned = sem("turned")
        gate_ready = sem("gate_ready")
        swish_ready = sem("swish_ready")
        act_ready = sem("act_ready")
        res_ready = sem("res_ready")
        pieces = sem("pieces")
        added = sem("added")
        blk = sem("blk_step")

        def full(name):
            n = NO[name]
            return bank_full[n % 8], n // 8 + 1

        def freed(name):
            return bank_free[NO[name] % 8]

        def bank(name):
            return ps[NO[name] % 8]

        def unit_landed(kind, i):
            n = UNIT_NO[(kind, i)]
            return filled[n % RING], 16 * (n // RING + 1)

        def unit(kind, i):
            return ring[:, UNIT_NO[(kind, i)] % RING, :]

        def slot_of(j):
            return (NMIX + j) % RING

        def slot_count(idx, j):
            return idx * 16 + 16 * ((NMIX + j) // RING + 1)

        LAST = {}
        for kind, i in MIX_UNITS:
            if kind == "v" or kind == "out":
                LAST[(kind, i)] = (kind, i, 2)
            elif kind == "bb":
                LAST[(kind, i)] = (kind, 4 * i + 3)
            else:
                LAST[(kind, i)] = (kind, 2 * i + 1)

        def by_chunk(view, t):
            if t == 0:
                return view[:, :, 0:NP].rearrange("p h (c i) -> p h c i", i=C)
            return view[:, :, NP:NT].rearrange("p h (c i) -> p h c i", i=L)

        block = ctx.enter_context(nc.Block())

        @block.sync
        def _(sp):
            for n, (kind, i) in enumerate(MIX_UNITS):
                if n >= RING:
                    sp.wait_ge(*full(LAST[MIX_UNITS[n - RING]]))
                dst = ring[:, n % RING, :]
                if kind in COL0:
                    src = w_in[0, :, COL0[kind] + 256 * i:COL0[kind] + 256 * (i + 1)]
                    sp.dma_start(dst.rearrange("p (c n) -> p c n", c=KC),
                                 src.rearrange("(c p) n -> p c n", p=128)).then_inc(filled[n % RING], 16)
                elif kind == "bb":
                    src = w_bpool[0, :, 512 * i:512 * (i + 1)]
                    sp.dma_start(dst.rearrange("p (c n) -> p c n", c=4),
                                 src.rearrange("(c p) n -> p c n", p=128)).then_inc(filled[n % RING], 16)
                else:
                    w = w_bgla if kind == "ba" else w_out
                    src = w[0, :, 256 * i:256 * (i + 1)]
                    sp.dma_start(dst.rearrange("p (c n) -> p c n", c=KC),
                                 src.rearrange("(c p) n -> p c n", p=128)).then_inc(filled[n % RING], 16)

            def load_unit(e, j):
                s = slot_of(j)
                if j < UP_UNITS:
                    src = w_gu[0, ds(e, 1), j * 128:(j + 1) * 128, :].rearrange("e p n -> p (e n)")
                    sp.dma_start(ring[:, s, :], src).then_inc(filled[s], 16)
                else:
                    r = (j - UP_UNITS) * 256
                    src = w_down[0, ds(e, 1), r:r + 256, :].rearrange("e (c p) n -> p (e c) n", p=128)
                    sp.dma_start(ring[:, s, :].rearrange("p (c n) -> p c n", c=2), src).then_inc(filled[s], 16)

            for j in range(EXP_UNITS):
                sp.wait_ge(*full(LAST[MIX_UNITS[NMIX + j - RING]]))
                load_unit(0, j)
            for j in range(UP_UNITS):
                sp.wait_ge(up_used, j + 1)
                load_unit(1, j)
            with sp.Fori(1, NE - 1) as idx:
                e = sp.snap(idx)
                for j in range(UP_UNITS):
                    sp.wait_ge(up_used, e * UP_UNITS + j + 1)
                    load_unit(e + 1, j)
                for j in range(DOWN_UNITS):
                    sp.wait_ge(down_used, (e - 1) * DOWN_UNITS + j + 1)
                    load_unit(e, UP_UNITS + j)
            for j in range(DOWN_UNITS):
                sp.wait_ge(down_used, (NE - 2) * DOWN_UNITS + j + 1)
                load_unit(NE - 1, UP_UNITS + j)
            sp.wait_ge(lists_ready, 1)
            count = sp.value_load(n_later[0:1, 0:1], min_val=0, max_val=RANKS)
            with sp.If(count > 0):
                with sp.Fori(0, count) as b:
                    e = sp.value_load(later[0:1, 1, ds(b, 1)], min_val=0, max_val=NE - 1)
                    sp.wait_ge(down_used, b * DOWN_UNITS + NE * DOWN_UNITS)
                    for j in range(EXP_UNITS):
                        load_unit(e, j)
            for t, (t0, n) in enumerate(TILES):
                sp.wait_ge(y_final, t + 1)
                dst = y_p[0, t0:t0 + n, :] if t < 2 else y_s.rearrange("b s d -> (b s) d")
                sp.dma_start(dst, y[0:n, t, :]).then_inc(y_stored, 16)
            sp.wait_ge(y_stored, 16 * 3)
            sp.wait_ge(stored_s, 16 * 4)
            sp.wait_ge(stored_p, 16 * 4)

        @block.gpsimd
        def _(pool):
            def load_x(s):
                for t, (t0, n) in enumerate(TILES):
                    src = x_p[0, t0:t0 + n, :] if t < 2 else x_s.rearrange("b s d -> (b s) d")
                    pool.dma_start(xr[0:n, t, :], src).then_inc(s, 16)

            pool.dma_start(ar[:, CONST:CONST + NCST], c_cols).then_inc(cst_in, 16)
            load_x(x_in)
            pool.dma_start(wlr, w_in[0, :, COL0["lr"]:COL0["lr"] + 16].rearrange("(c p) n -> p c n", p=128))\
                .then_inc(small_in, 16)
            pool.dma_start(wgk2, w_gk2[0, :, :]).then_inc(small_in, 16)
            at = 0
            for vec, n in ((b_gates, 16), (b_gk, 4), (gla_norm_w, 2), (pool_scale, 4)):
                pool.dma_start(rows[at:at + n, :], vec[0, :].rearrange("(c p) -> c p", p=128)).then_inc(small_in, 16)
                at += n
            pool.dma_start(bgu_rows, b_gu[0, :, :]).then_inc(bgu_in, 16)
            pool.dma_start(starts, c_starts).then_inc(starts_in, 16)
            pool.dma_start(brt, b_router[0:1, :].broadcast_to([128, NE])).then_inc(starts_in, 16)

            def load_states(h):
                pool.dma_start(ss_st[h % 2], state_gla[0, :, h, :, :].rearrange("b d v -> d b v"))\
                    .then_inc(ss_in[h], 16)
            load_states(0)
            load_states(1)
            for h in range(HEADS):
                pool.wait_ge(sp_ready, 4 * (h + 1))
                pool.dma_start(ngp[0, 0, h, :, :], sp_st[:, h % 2, 3, :]).then_inc(stored_p, 16)
                pool.wait_ge(ss_ready, h + 1)
                pool.dma_start(ngs[0, :, h, :, :].rearrange("b d v -> d b v"), ss_st[h % 2]).then_inc(stored_s, 16)
                if h < 2:
                    pool.wait_ge(stored_s, 16 * (h + 1))
                    load_states(h + 2)
            pool.wait_ge(*full(("o", 3, 1)))
            load_x(x_again)
            pool.wait_ge(stored_p, 16 * 4)
            pool.wait_ge(stored_s, 16 * 4)
            pool.dma_start(spb, state_pool[0, :, :, :].rearrange("b r c -> (b r) c")).then_inc(late_in, 16)
            pool.dma_start(wgrp, w_grp[0, :, :, :].rearrange("g c d -> c g d")).then_inc(late_in, 16)
            pool.dma_start(wrt, w_router[0, :, :].rearrange("(c p) n -> p c n", p=128)).then_inc(late_in, 16)
            pool.wait_ge(ot_ready, 1)
            pool.dma_start(ln_g, ln1_g[0:1, :].broadcast_to([128, D])).then_inc(ln1_in, 16)
            pool.dma_start(ln_b, ln1_b[0:1, :].broadcast_to([128, D])).then_inc(ln1_in, 16)
            pool.dma_start(nps[0, :, 0:PBUF - L, :], state_pool[0, :, L:PBUF, :]).then_inc(stored, 16)
            pool.wait_ge(pool_out_ready, 2)
            pool.dma_start(npp[0, 0, :, :], pool_out_p).then_inc(stored, 16)
            for b in range(B):
                pool.dma_start(nps[0, b, PBUF - L:PBUF, :], pool_out_s[b * L:(b + 1) * L, :]).then_inc(late_in, 16)
            pool.wait_ge(late_in, 16 * (3 + B))
            pool.wait_ge(h_ready, 3)
            pool.dma_start(lists, c_lists).then_inc(late_in, 16)
            pool.wait_ge(*full(("lg", 2)))
            pool.dma_start(bdn_rows, b_down[0, :, :]).then_inc(bgu_in, 16)
            pool.wait_ge(ln_read, 3)
            pool.dma_start(ln_g, ln2_g[0:1, :].broadcast_to([128, D])).then_inc(ln2_in, 16)
            pool.dma_start(ln_b, ln2_b[0:1, :].broadcast_to([128, D])).then_inc(ln2_in, 16)
            pool.wait_ge(stored, 16 * 2)

        @block.tensor
        def _(pe):
            mm = nc.tensor.matmul

            def claim(name):
                n = NO[name]
                if n >= 8:
                    pe.wait_ge(bank_free[n % 8], n // 8)
                return ps[n % 8]

            def weights_times(kind, i, rhs, chunks=KC, cols_per_unit=2):
                w = unit(kind, i // cols_per_unit).rearrange("p (c n) -> p c n", c=chunks)
                if i % cols_per_unit == 0:
                    pe.wait_ge(*unit_landed(kind, i // cols_per_unit))
                o = claim((kind, i))
                f0 = (i % cols_per_unit) * 128
                for c in range(chunks):
                    last = mm(o[:, 0:NT], w[:, c, f0:f0 + 128], rhs[:, c, :], start=c == 0, stop=c == chunks - 1)
                last.then_inc(full((kind, i))[0], 1)

            pe.wait_ge(cst_in, 16)
            pe.wait_ge(x_in, 48)
            for c in range(KC):
                o = claim(("xt", c))
                for t, (t0, n) in enumerate(TILES):
                    last = nc.tensor.transpose(o[:, t0:t0 + n], xr[0:n, t, c * 128:(c + 1) * 128], ident[0:n, 0:n])
                last.then_inc(full(("xt", c))[0], 1)
            pe.wait_ge(small_in, 16 * 6)
            o = claim(("cols",))
            nc.tensor.transpose(o[:, 0:26], rows, ident[0:26, 0:26]).then_inc(full(("cols",))[0], 1)
            pe.wait_ge(bgu_in, 16)
            o = claim(("bgt",))
            for c in range(16):
                last = nc.tensor.transpose(o[:, c * NE:(c + 1) * NE], bgu_rows[:, c * 128:(c + 1) * 128],
                                           ident[0:NE, 0:NE])
            last.then_inc(full(("bgt",))[0], 1)
            pe.wait_ge(xt_ready, KC)
            o = claim(("lr",))
            for c in range(KC):
                last = mm(o[0:16, 0:NT], wlr[:, c, :], xt[:, c, :], start=c == 0, stop=c == KC - 1)
            last.then_inc(full(("lr",))[0], 1)
            for i in range(4):
                weights_times("k", i, xt)
            pe.wait_ge(lr_ready, 1)
            for i in range(4):
                o = claim(("gk", i))
                mm(o[:, 0:NT], wgk2[:, i * 128:(i + 1) * 128], lrt, start=True, stop=True)\
                    .then_inc(full(("gk", i))[0], 1)
            for i in range(4):
                weights_times("q", i, xt)
            for j in range(4):
                w = unit("v", j).rearrange("p (c n) -> p c n", c=KC)
                pe.wait_ge(*unit_landed("v", j))
                for t, (t0, n) in enumerate(TILES):
                    o = claim(("v", j, t))
                    for c in range(KC):
                        last = mm(o[0:n, 0:256], xt[:, c, t0:t0 + n], w[:, c, :], start=c == 0, stop=c == KC - 1)
                    last.then_inc(full(("v", j, t))[0], 1)
            for i in range(8):
                weights_times("g", i, xt)

            pe.wait_ge(qk_ready, 4)
            for t, (t0, n) in enumerate(TILES):
                o = claim(("a", t))
                for h in range(HEADS):
                    last = mm(o[0:n, h * n:(h + 1) * n], ke[:, h, t0:t0 + n], qe[:, h, t0:t0 + n], start=True, stop=True)
                last.then_inc(full(("a", t))[0], 1)
            for t, (t0, n) in enumerate(TILES):
                o = claim(("kt", t))
                for h in range(HEADS):
                    last = nc.tensor.transpose(o[0:n, h * 128:(h + 1) * 128], k[:, h, t0:t0 + n], ident)
                last.then_inc(full(("kt", t))[0], 1)
            pe.wait_ge(klt_ready, 3)
            pe.wait_ge(v_ready, 12)
            pe.wait_ge(at_ready, 3)
            for h in range(HEADS):
                for half in range(2):
                    o = claim(("kv", h, half))
                    for c2 in range(2):
                        p0 = half * C
                        last = mm(o[:, c2 * DV:(c2 + 1) * DV], klt[p0:p0 + C, c2, h * 128:(h + 1) * 128],
                                  v[p0:p0 + C, c2, h * DV:(h + 1) * DV], start=True, stop=True)
                    last.then_inc(full(("kv", h, half))[0], 1)
                pe.wait_ge(klm_ready, h + 1)
                for i in range(4):
                    o = claim(("kvs", h, i))
                    for half in range(2):
                        last = mm(o[:, half * DV:(half + 1) * DV], klm[:, 2 * i + half, :],
                                  v[0:NS, 2, h * DV:(h + 1) * DV], start=True, stop=True)
                    last.then_inc(full(("kvs", h, i))[0], 1)
                pe.wait_ge(sp_ready, 4 * (h + 1))
                pe.wait_ge(ss_in[h], 16)
                for vc in range(2):
                    o = claim(("o", h, vc))
                    f0 = h * DV + vc * 128
                    for t, (t0, n) in enumerate(TILES):
                        mm(o[:, t0:t0 + n], v[0:n, t, f0:f0 + 128], at_[0:n, t, h * n:(h + 1) * n],
                           start=t == 0, stop=False, skip_group_check=True)
                    for c in range(1, NP // C):
                        mm(o[:, c * C:(c + 1) * C], sp_st[:, h % 2, c - 1, vc * 128:(vc + 1) * 128],
                           q[:, h, c * C:(c + 1) * C], start=False, stop=False, skip_group_check=True)
                    for b in range(B):
                        s0 = NP + b * L
                        last = mm(o[:, s0:s0 + L], ss_st[h % 2][:, b, vc * 128:(vc + 1) * 128],
                                  q[:, h, s0:s0 + L], start=False, stop=b == B - 1, skip_group_check=True)
                    last.then_inc(full(("o", h, vc))[0], 1)
            for h in range(HEADS):
                pe.wait_ge(sq_ready, 2 * h + 2)
                o = claim(("rms", h))
                for vc in range(2):
                    last = mm(o[:, 0:NT], cst("ones"), sq[:, 2 * h + vc, :], start=vc == 0, stop=vc == 1)
                last.then_inc(full(("rms", h))[0], 1)
            for i in range(8):
                weights_times("ga", i, xt)
            pe.wait_ge(ot_ready, 1)
            for i in range(8):
                weights_times("ba", i, ot)
            for i in range(4):
                weights_times("u", i, xt)
            pe.wait_ge(late_in, 48)
            o = claim(("pb",))
            for g in range(4):
                last = nc.tensor.transpose(o[:, g * 120:(g + 1) * 120], spb[:, g * 128:(g + 1) * 128],
                                           ident[0:120, 0:120])
            last.then_inc(full(("pb",))[0], 1)
            pe.wait_ge(u_ready, 4)
            o = claim(("up",))
            for g in range(4):
                last = nc.tensor.transpose(o[0:PBUF, g * 128:(g + 1) * 128], up_pad[:, g, NP:NP + PBUF], ident)
            last.then_inc(full(("up",))[0], 1)
            pe.wait_ge(po_ready, 1)
            o = claim(("us",))
            for g in range(4):
                last = nc.tensor.transpose(o[0:NS, g * 128:(g + 1) * 128], po[:, g, NP:NT], ident)
            last.then_inc(full(("us",))[0], 1)
            for i in range(8):
                weights_times("gb", i, xt)
            for g in range(4):
                pe.wait_ge(po_ready, g + 2)
                o = claim(("grp", g))
                mm(o[:, 0:NT], wgrp[:, g, :], po[:, g, :], start=True, stop=True).then_inc(full(("grp", g))[0], 1)
            pe.wait_ge(pg_ready, 4)
            for i in range(8):
                weights_times("bb", i, pg, chunks=4, cols_per_unit=4)
            pe.wait_ge(merged, 8)
            for j in range(4):
                w = unit("out", j).rearrange("p (c n) -> p c n", c=KC)
                pe.wait_ge(*unit_landed("out", j))
                for t, (t0, n) in enumerate(TILES):
                    o = claim(("out", j, t))
                    for c in range(KC):
                        last = mm(o[0:n, 0:256], ga[:, c, t0:t0 + n], w[:, c, :], start=c == 0, stop=c == KC - 1)
                    last.then_inc(full(("out", j, t))[0], 1)
            pe.wait_ge(h_ready, 3)
            for c in range(KC):
                o = claim(("ht", c))
                for t, (t0, n) in enumerate(TILES):
                    last = nc.tensor.transpose(o[:, t0:t0 + n], hrow[0:n, t, c * 128:(c + 1) * 128], ident[0:n, 0:n])
                last.then_inc(full(("ht", c))[0], 1)
            pe.wait_ge(ht_ready, KC)
            for t, (t0, n) in enumerate(TILES):
                o = claim(("lg", t))
                for c in range(KC):
                    last = mm(o[0:n, 0:NE], ot[:, c, t0:t0 + n], wrt[:, c, :], start=c == 0, stop=c == KC - 1)
                last.then_inc(full(("lg", t))[0], 1)
            pe.wait_ge(mask_ready, 3)
            for t, (t0, n) in enumerate(TILES):
                o = claim(("rk", t))
                for s in range(t):
                    mm(o[0:n, 0:NE], cst("ones", n=n), msk[:, s, :], start=s == 0, stop=False)
                mm(o[0:n, 0:NE], cst("before", p=n, n=n), msk[0:n, t, :], start=t == 0, stop=True)\
                    .then_inc(full(("rk", t))[0], 1)
            o = claim(("cnt",))
            for t, (t0, n) in enumerate(TILES):
                last = mm(o[0:1, 0:NE], cst("ones", p=n, n=1), msk[0:n, t, :], start=t == 0, stop=t == 2)
            last.then_inc(full(("cnt",))[0], 1)
            pe.wait_ge(soft4_done, 3)
            o = claim(("gwt",))
            for t, (t0, n) in enumerate(TILES):
                last = nc.tensor.transpose(o[0:NE, t0:t0 + n], gw[0:n, t, :], ident[0:n, 0:n])
            last.then_inc(full(("gwt",))[0], 1)
            pe.wait_ge(gwt_ready, 1)
            pe.wait_ge(bgu_in, 32)
            for t, (t0, n) in enumerate(TILES):
                for i in range(2):
                    o = claim(("yb", t, i))
                    mm(o[0:n, :], gwt[:, t0:t0 + n], bdn_rows[:, i * 512:(i + 1) * 512], start=True, stop=True)\
                        .then_inc(full(("yb", t, i))[0], 1)
            for name in PRODUCTS[-8:]:
                pe.wait_ge(freed(name), NO[name] // 8 + 1)

            def gather(pair_count):
                pe.wait_ge(onehot_ready, pair_count)
                for c in range(KC):
                    for t, (t0, n) in enumerate(TILES):
                        last = mm(ps[6 + c // 4][:, (c % 4) * 128:(c % 4 + 1) * 128], hrow[0:n, t, c * 128:(c + 1) * 128],
                                  onehot[0:n, t, :], start=t == 0, stop=t == 2)
                last.then_inc(gathered, 1)

            def turn_slots(pair_count):
                pe.wait_ge(onehot_w_ready, pair_count)
                for t, (t0, n) in enumerate(TILES):
                    last = nc.tensor.transpose(ps[5][:, t0:t0 + n], onehot_w[0:n, t, :], ident[0:n, 0:n])
                last.then_inc(slots_turned, 1)

            def expert_up(idx, half):
                for j in range(UP_UNITS):
                    pe.wait_ge(filled[slot_of(j)], slot_count(idx, j))
                    w = ring[:, slot_of(j), :]
                    for i in range(2):
                        for side in range(2):
                            last = mm(ps[i][side * CAP:(side + 1) * CAP, :], xgt[:, j, half * CAP:(half + 1) * CAP],
                                      w[:, i * D + side * 512:i * D + (side + 1) * 512],
                                      start=j == 0, stop=j == UP_UNITS - 1)
                    last.then_inc(up_used, 1)

            def turn_up(idx):
                pe.wait_ge(hg_ready, idx + 1)
                for c in range(4):
                    nc.tensor.transpose(ps[2][:, c * 128:(c + 1) * 128], hg[:, c * 128:(c + 1) * 128], ident)
                pe.wait_ge(hu_ready, idx + 1)
                for c in range(4):
                    last = nc.tensor.transpose(ps[3][:, c * 128:(c + 1) * 128], hu[:, c * 128:(c + 1) * 128], ident)
                last.then_inc(turned, 1)

            def expert_down(idx):
                pe.wait_ge(act_ready, idx + 1)
                for j in range(DOWN_UNITS):
                    s = slot_of(UP_UNITS + j)
                    pe.wait_ge(filled[s], slot_count(idx, UP_UNITS + j))
                    w = ring[:, s, :].rearrange("p (c n) -> p c n", c=2)
                    for c in range(2):
                        for side in range(2):
                            last = mm(ps[4][side * CAP:(side + 1) * CAP, :], actt[:, 2 * j + c, :],
                                      w[:, c, side * 512:(side + 1) * 512], start=j == 0 and c == 0,
                                      stop=j == DOWN_UNITS - 1 and c == 1)
                    last.then_inc(down_used, 1)

            def scatter(pair, blocks):
                pe.wait_ge(res_ready, blocks)
                pe.wait_ge(slot_ready, pair + 1)
                for i in range(6):
                    t, half = i // 2, i % 2
                    t0, n = TILES[t]
                    if i >= 3:
                        pe.wait_ge(added, pair * 6 + i - 2)
                    mm(ps[5 + i % 3][0:n, :], slot_t[:, t0:t0 + n], res[:, half * 512:(half + 1) * 512],
                       start=True, stop=True).then_inc(pieces, 1)

            def pair_of_blocks(pair, first=False, last=False):
                e = pair * 2
                turn_up(e)
                if not first:
                    scatter(pair - 1, e)
                expert_up(e + 1, 1)
                turn_slots(pair + 1)
                if not last:
                    if not first:
                        pe.wait_ge(added, pair * 6)
                    gather(pair + 2)
                expert_down(e)
                turn_up(e + 1)
                if not last:
                    pe.wait_ge(xgt_ready, pair + 2)
                    expert_up(e + 2, 0)
                pe.wait_ge(res_ready, e + 1)
                expert_down(e + 1)

            gather(1)
            pe.wait_ge(xgt_ready, 1)
            expert_up(0, 0)
            pair_of_blocks(0, first=True)
            with pe.Fori(1, NE // 2 - 1) as pair:
                pair_of_blocks(pe.snap(pair))
            pair_of_blocks(NE // 2 - 1, last=True)
            scatter(NE // 2 - 1, NE)
            pe.wait_ge(lists_ready, 1)
            count = pe.value_load(n_later[0:1, 0:1], min_val=0, max_val=RANKS)
            with pe.If(count > 0):
                with pe.Fori(0, count) as loop:
                    b = pe.snap(loop)
                    pe.wait_ge(added, b * 6 + 6 * (NE // 2))
                    gather(b + NE // 2 + 1)
                    turn_slots(b + NE // 2 + 1)
                    pe.wait_ge(xgt_ready, b + NE // 2 + 1)
                    expert_up(b + NE, 0)
                    turn_up(b + NE)
                    expert_down(b + NE)
                    scatter(b + NE // 2, b + NE + 1)

        @block.scalar
        def _(act):
            A = nc.scalar.activation
            steps = [0]

            def link(ins):
                steps[0] += 1
                ins.then_inc(act_step, 1)
                act.wait_ge(act_step, steps[0])

            act.wait_ge(*full(("lr",)))
            A(lrt, bank(("lr",))[0:16, 0:NT], ACT.Copy).then_inc(lr_ready, 1)
            act.wait_ge(lr_ready, 1)
            act.sem_inc(freed(("lr",)), 1)
            for i in range(4):
                act.wait_ge(*full(("k", i)))
                A(k[:, i, :], bank(("k", i))[:, 0:NT], ACT.Copy).then_inc(freed(("k", i)), 1)
            act.wait_ge(z_ready, 1)
            link(A(ee[:, :, :], ee[:, :, :], ACT.Exp, scale=-1.0))
            A(ee[:, :, :], ee[:, :, :], ACT.Ln, bias=1.0).then_inc(soft_ready, 1)
            for i in range(4):
                act.wait_ge(*full(("q", i)))
                A(q[:, i, :], bank(("q", i))[:, 0:NT], ACT.Copy, scale=float(DK) ** -0.5)\
                    .then_inc(freed(("q", i)), 1)
            act.sem_inc(qk_in, 1)
            act.wait_ge(diff_ready, 1)
            A(qe[:, :, :], bb[:, :, :], ACT.Exp, scale=1.0 / 16).then_inc(exp_ready, 1)
            A(ke[:, :, :], bb[:, :, :], ACT.Exp, scale=-1.0 / 16).then_inc(exp_ready, 1)
            A(eb[:, :, :], ee[:, :, :], ACT.Exp, scale=1.0 / 16).then_inc(exp_ready, 1)
            A(bl[:, :, :], bl[:, :, :], ACT.Exp, scale=1.0 / 16).then_inc(exp_ready, 1)
            act.wait_ge(xt_ready, KC)
            for j in range(4):
                for t, (t0, n) in enumerate(TILES):
                    act.wait_ge(*full(("v", j, t)))
                    A(v[0:n, t, j * 256:(j + 1) * 256], bank(("v", j, t))[0:n, 0:256], ACT.Copy)\
                        .then_inc(freed(("v", j, t)), 1)
            act.sem_inc(v_ready, 12)
            for i in range(8):
                act.wait_ge(*full(("g", i)))
                A(gs[:, i, :], bank(("g", i))[:, 0:NT], ACT.Sigmoid).then_inc(sig_ready, 1)
            for t, (t0, n) in enumerate(TILES):
                act.wait_ge(*full(("kt", t)))
                A(klt[0:n, t, :], bank(("kt", t))[0:n, :], ACT.Copy).then_inc(klt_ready, 1)
            act.wait_ge(klt_ready, 3)
            for t in range(3):
                act.sem_inc(freed(("kt", t)), 1)
            for h in range(HEADS):
                for vc in range(2):
                    act.wait_ge(*full(("o", h, vc)))
                    A(sq[:, 2 * h + vc, :], bank(("o", h, vc))[:, 0:NT], ACT.Square).then_inc(sq_ready, 1)
                    A(ot[:, 2 * h + vc, :], bank(("o", h, vc))[:, 0:NT], ACT.Copy).then_inc(freed(("o", h, vc)), 1)
            for h in range(HEADS):
                act.wait_ge(*full(("rms", h)))
                A(rms[:, h, :], bank(("rms", h))[:, 0:NT], ACT.Sqrt, bias=eps_rms, scale=1.0 / DV)\
                    .then_inc(sqrt_ready, 1)
            act.wait_ge(sqrt_ready, 4)
            for h in range(HEADS):
                act.sem_inc(freed(("rms", h)), 1)
            act.wait_ge(stored_s, 16 * 4)
            for i in range(8):
                act.wait_ge(*full(("ga", i)))
                A(ga[:, i, :], bank(("ga", i))[:, 0:NT], ACT.Sigmoid, bias=cols[:, i:i + 1])\
                    .then_inc(freed(("ga", i)), 1)
            act.sem_inc(ga_ready, 1)
            act.wait_ge(pads_zero, 1)
            for i in range(4):
                act.wait_ge(*full(("u", i)))
                A(up_pad[:, i, PBUF:], bank(("u", i))[:, 0:NP], ACT.Copy)
                A(us_pad[:, i, :, PBUF:], bank(("u", i))[:, NP:NT].rearrange("p (b s) -> p b s", s=L), ACT.Copy)\
                    .then_inc(u_ready, 1)
            act.wait_ge(u_ready, 4)
            for i in range(4):
                act.sem_inc(freed(("u", i)), 1)
            for name, dst, n in ((("up",), pool_out_p, PBUF), (("us",), pool_out_s, NS)):
                act.wait_ge(*full(name))
                A(dst, bank(name)[0:n, :], ACT.Copy).then_inc(pool_out_ready, 1)
            act.wait_ge(pool_out_ready, 2)
            for name in (("up",), ("us",)):
                act.sem_inc(freed(name), 1)
            act.wait_ge(*full(("ba", 7)))
            for i in range(8):
                act.wait_ge(*full(("gb", i)))
                A(gb[:, i, :], bank(("gb", i))[:, 0:NT], ACT.Sigmoid, bias=cols[:, 8 + i:9 + i])\
                    .then_inc(freed(("gb", i)), 1)
            act.sem_inc(gb_ready, 1)
            for g in range(4):
                act.wait_ge(*full(("grp", g)))
                A(pg[:, g, :], bank(("grp", g))[:, 0:NT], ACT.Copy, scale=cols[:, 22 + g:23 + g])\
                    .then_inc(pg_ready, 1)
            act.wait_ge(pg_ready, 4)
            for g in range(4):
                act.sem_inc(freed(("grp", g)), 1)
            for t, (t0, n) in enumerate(TILES):
                act.wait_ge(var_ready, t + 1)
                A(rstd[0:n], mv[0:n, 1:2], ACT.Sqrt, bias=eps_ln[0:n]).then_inc(std_ready, 1)
            for c in range(KC):
                act.wait_ge(*full(("ht", c)))
                A(ot[:, c, :], bank(("ht", c))[:, 0:NT], ACT.Copy).then_inc(ht_ready, 1)
            act.wait_ge(ht_ready, KC)
            for c in range(KC):
                act.sem_inc(freed(("ht", c)), 1)
            for t, (t0, n) in enumerate(TILES):
                act.wait_ge(max_ready, t + 1)
                A(sm[0:n, 0:4], tmp8[0:n, 0:4], ACT.Exp).then_inc(soft4_ready, 1)

            def keep_gathered(count):
                act.wait_ge(gathered, count)
                A(xgt[:, 0:4, :], ps[6][:, :].rearrange("p (c s) -> p c s", s=128), ACT.Copy)
                A(xgt[:, 4:8, :], ps[7][:, :].rearrange("p (c s) -> p c s", s=128), ACT.Copy).then_inc(xgt_ready, 1)

            def keep_slots(count):
                act.wait_ge(slots_turned, count)
                A(slot_t, ps[5][:, 0:NT], ACT.Copy).then_inc(slot_ready, 1)

            def keep_gate(idx):
                act.wait_ge(up_used, (idx + 1) * UP_UNITS)
                A(hg, ps[0][:, :], ACT.Copy).then_inc(hg_ready, 1)

            def swish(idx):
                act.wait_ge(gate_ready, idx + 1)
                A(sg[:, :, :], g1[:, :, :], ACT.Sigmoid, scale=GLU_ALPHA).then_inc(swish_ready, 1)

            def keep_output(idx, half):
                act.wait_ge(down_used, (idx + 1) * DOWN_UNITS)
                for side in range(2):
                    last = A(res[half * CAP:(half + 1) * CAP, side * 512:(side + 1) * 512],
                             ps[4][side * CAP:(side + 1) * CAP, :], ACT.Copy)
                last.then_inc(res_ready, 1)

            def pair_of_blocks(pair, last=False):
                e = pair * 2
                swish(e)
                keep_gate(e + 1)
                keep_slots(pair + 1)
                if not last:
                    keep_gathered(pair + 2)
                keep_output(e, 0)
                swish(e + 1)
                if not last:
                    keep_gate(e + 2)
                keep_output(e + 1, 1)

            keep_gathered(1)
            keep_gate(0)
            pair_of_blocks(0)
            with act.Fori(1, NE // 2 - 1) as pair:
                pair_of_blocks(act.snap(pair))
            pair_of_blocks(NE // 2 - 1, last=True)
            act.wait_ge(lists_ready, 1)
            count = act.value_load(n_later[0:1, 0:1], min_val=0, max_val=RANKS)
            with act.If(count > 0):
                with act.Fori(0, count) as loop:
                    b = act.snap(loop)
                    keep_gathered(b + NE // 2 + 1)
                    keep_slots(b + NE // 2 + 1)
                    keep_gate(b + NE)
                    swish(b + NE)
                    keep_output(b + NE, 0)
            for t, (t0, n) in enumerate(TILES):
                act.wait_ge(var_ready, t + 4)
                A(rstd[0:n], mv[0:n, 1:2], ACT.Sqrt, bias=eps_ln[0:n]).then_inc(std_ready, 1)

        @block.vector
        def _(dve):
            V = nc.vector
            steps = [0]

            def link(ins):
                steps[0] += 1
                ins.then_inc(dve_step, 1)
                dve.wait_ge(dve_step, steps[0])

            V.memset(eps_rms, RMS_EPS)
            V.memset(eps_ln, LN_EPS)
            for c in range(KC):
                dve.wait_ge(*full(("xt", c)))
                V.tensor_copy(xt[:, c, :], bank(("xt", c))[:, 0:NT]).then_inc(xt_ready, 1)
            dve.wait_ge(xt_ready, KC)
            for c in range(KC):
                dve.sem_inc(freed(("xt", c)), 1)
            for name, dst, n in ((("cols",), cols, 26), (("bgt",), reg(BGU, 512), 512)):
                dve.wait_ge(*full(name))
                V.tensor_copy(dst, bank(name)[:, 0:n]).then_inc(freed(name), 1)
            dve.wait_ge(freed(("cols",)), NO[("cols",)] // 8 + 1)
            for i in range(4):
                dve.wait_ge(*full(("gk", i)))
                V.tensor_scalar(bb[:, i, :], bank(("gk", i))[:, 0:NT], cols[:, 16 + i:17 + i], None, ALU.add)\
                    .then_inc(freed(("gk", i)), 1)
            for i in range(4):
                dve.wait_ge(freed(("gk", i)), NO[("gk", i)] // 8 + 1)
            V.scalar_tensor_tensor(ee[:, :, :], bb[:, :, :], -1.0, bb[:, :, :], ALU.mult, ALU.max).then_inc(z_ready, 1)
            dve.wait_ge(soft_ready, 1)
            link(V.scalar_tensor_tensor(bb[:, :, :], bb[:, :, :], 0.0, ee[:, :, :], ALU.min, ALU.subtract))
            dve.wait_ge(starts_in, 32)
            link(V.tensor_tensor_scan(reg(EE, HEADS * NT), starts, reg(BB, HEADS * NT), 0.0, ALU.mult, ALU.add))
            for t, n in ((0, C), (1, L)):
                cum, dif, rest = by_chunk(ee, t), by_chunk(bb, t), by_chunk(bl, t)
                shape = list(cum.shape)
                V.tensor_tensor(dif, cum, cum[:, :, :, n // 2:n // 2 + 1].broadcast_to(shape), ALU.subtract)
                last = V.tensor_tensor(rest, cum[:, :, :, n - 1:n].broadcast_to(shape), cum, ALU.subtract)
            last.then_inc(diff_ready, 1)
            dve.wait_ge(exp_ready, 4)
            dve.wait_ge(qk_in, 1)
            V.tensor_tensor(qe[:, :, :], qe[:, :, :], q[:, :, :], ALU.mult).then_inc(qk_ready, 1)
            V.tensor_tensor(ke[:, :, :], ke[:, :, :], k[:, :, :], ALU.mult).then_inc(qk_ready, 1)
            V.tensor_tensor(q[:, :, :], q[:, :, :], eb[:, :, :], ALU.mult).then_inc(qk_ready, 1)
            V.tensor_tensor(k[:, :, :], k[:, :, :], bl[:, :, :], ALU.mult).then_inc(qk_ready, 1)
            V.tensor_copy(dec[:, :, 0:4].rearrange("p h (c a) -> p h c a", a=1), by_chunk(eb, 0)[:, :, :, C - 1:C])
            link(V.tensor_copy(dec[:, :, 4:12].rearrange("p h (c a) -> p h c a", a=1), by_chunk(eb, 1)[:, :, :, L - 1:L]))
            link(V.memset(reg(BB, 1536), 0.0))
            for i in range(8):
                dve.wait_ge(*full(("g", i)))
                dve.wait_ge(sig_ready, i + 1)
                V.tensor_tensor(gs[:, i, :], gs[:, i, :], bank(("g", i))[:, 0:NT], ALU.mult)\
                    .then_inc(freed(("g", i)), 1)
            for t, (t0, n) in enumerate(TILES):
                dve.wait_ge(*full(("a", t)))
                m = cst("pmask" if t < 2 else "smask", p=n).bitcast(i32)
                for h in range(HEADS):
                    last = V.copy_predicated(at_[0:n, t, h * n:(h + 1) * n], m, bank(("a", t))[0:n, h * n:(h + 1) * n])
                last.then_inc(at_ready, 1)
            dve.wait_ge(at_ready, 3)
            for t in range(3):
                dve.sem_inc(freed(("a", t)), 1)
            dve.wait_ge(klt_ready, 3)
            dve.wait_ge(*full(("kt", 2)))
            for h in range(HEADS):
                if h:
                    dve.wait_ge(*full(("kvs", h - 1, 3)))
                V.tensor_tensor(klm, klt[0:NS, 2, h * 128:(h + 1) * 128].unsqueeze(1).broadcast_to([NS, B, DK]),
                                cst("bmask", p=NS).unsqueeze(2).broadcast_to([NS, B, DK]), ALU.mult)\
                    .then_inc(klm_ready, 1)
                if h >= 2:
                    dve.wait_ge(stored_p, 16 * (h - 1))
                for c in range(4):
                    name = ("kv", h, c % 2)
                    src = bank(name)[:, (c // 2) * DV:(c // 2 + 1) * DV]
                    dve.wait_ge(*full(name))
                    if c == 0:
                        V.tensor_copy(sp_st[:, h % 2, 0, :], src).then_inc(sp_ready, 1)
                    else:
                        dve.wait_ge(sp_ready, 4 * h + c)
                        V.scalar_tensor_tensor(sp_st[:, h % 2, c, :], sp_st[:, h % 2, c - 1, :], dec[:, h, c:c + 1],
                                               src, ALU.mult, ALU.add).then_inc(sp_ready, 1)
                dve.wait_ge(sp_ready, 4 * h + 4)
                dve.sem_inc(freed(("kv", h, 0)), 1)
                dve.sem_inc(freed(("kv", h, 1)), 1)
                dve.wait_ge(*full(("o", h, 1)))
                for b in range(B):
                    name = ("kvs", h, b // 2)
                    ins = V.scalar_tensor_tensor(ss_st[h % 2][:, b, :], ss_st[h % 2][:, b, :], dec[:, h, 4 + b:5 + b],
                                                 bank(name)[:, (b % 2) * DV:(b % 2 + 1) * DV], ALU.mult, ALU.add)
                    if b % 2:
                        ins.then_inc(freed(name), 1)
                for i in range(4):
                    name = ("kvs", h, i)
                    dve.wait_ge(freed(name), NO[name] // 8 + 1)
                dve.sem_inc(ss_ready, 1)
            dve.wait_ge(sqrt_ready, 4)
            link(V.reciprocal(rms[:, :, :], rms[:, :, :]))
            dve.wait_ge(freed(("o", 3, 1)), NO[("o", 3, 1)] // 8 + 1)
            dve.wait_ge(freed(("o", 3, 0)), NO[("o", 3, 0)] // 8 + 1)
            for i in range(8):
                last = V.scalar_tensor_tensor(ot[:, i, :], ot[:, i, :], cols[:, 20 + i % 2:21 + i % 2], rms[:, i // 2, :],
                                              ALU.mult, ALU.mult)
            link(last)
            V.tensor_tensor(ot[:, :, :], ot[:, :, :], gs[:, :, :], ALU.mult).then_inc(ot_ready, 1)
            V.memset(up_pad[:, :, 0:PBUF], 0.0).then_inc(pads_zero, 1)
            dve.wait_ge(ga_ready, 1)
            for i in range(8):
                dve.wait_ge(*full(("ba", i)))
                V.tensor_tensor(ga[:, i, :], ga[:, i, :], bank(("ba", i))[:, 0:NT], ALU.mult)\
                    .then_inc(freed(("ba", i)), 1)
            dve.wait_ge(*full(("pb",)))
            V.tensor_copy(us_pad[:, :, :, 0:PBUF].rearrange("p g b r -> p (g b) r"),
                          bank(("pb",))[:, 0:480].rearrange("p (g r) -> p g r", r=PBUF)).then_inc(freed(("pb",)), 1)
            dve.wait_ge(u_ready, 4)
            dve.wait_ge(freed(("pb",)), NO[("pb",)] // 8 + 1)
            for g in range(4):
                last = V.tensor_copy(po[:, g, NP:NT].rearrange("p (b s) -> p b s", s=L), us_pad[:, g, :, PBUF:])
            last.then_inc(po_ready, 1)
            dve.wait_ge(*full(("us",)))
            win = [(reg(EE, PBUF + NP), ar[:, EE + 271:EE + 271 + 184].rearrange("p (b s) -> p b s", b=B)),
                   (reg(EE + 455, PBUF + NP), ar[:, EE + 726:EE + 910].rearrange("p (b s) -> p b s", b=B))]
            for g in range(4):
                cp, cs = up_pad[:, g, :], us_pad[:, g, :, :]
                lo = 0
                for s in range(g + 1):
                    step = 2 ** s
                    lo += step
                    np_, ns_ = win[s % 2]
                    V.tensor_tensor(np_[:, lo:], cp[:, lo:], cp[:, lo - step:PBUF + NP - step], ALU.add)
                    link(V.tensor_tensor(ns_[:, :, lo:], cs[:, :, lo:], cs[:, :, lo - step:PBUF + L - step], ALU.add))
                    cp, cs = np_, ns_
                w = 2.0 ** -(g + 1)
                at = CST["rcnt"][0] + CONST + 16 * g
                link(V.tensor_tensor(win[(g + 1) % 2][0][:, 0:16], cp[:, PBUF:PBUF + 16], ar[:, at:at + 16], ALU.mult))
                V.tensor_tensor(po[:, g, 0:16], win[(g + 1) % 2][0][:, 0:16], up_pad[:, g, PBUF:PBUF + 16], ALU.subtract)
                V.scalar_tensor_tensor(po[:, g, 16:NP], cp[:, PBUF + 16:], w, up_pad[:, g, PBUF + 16:], ALU.mult,
                                       ALU.subtract)
                V.scalar_tensor_tensor(po[:, g, NP:NT].rearrange("p (b s) -> p b s", s=L), cs[:, :, PBUF:], w,
                                       us_pad[:, g, :, PBUF:], ALU.mult, ALU.subtract).then_inc(po_ready, 1)
                dve.wait_ge(po_ready, g + 2)
            dve.wait_ge(gb_ready, 1)
            for i in range(8):
                dve.wait_ge(*full(("bb", i)))
                ins = V.tensor_tensor(gb[:, i, :], gb[:, i, :], bank(("bb", i))[:, 0:NT], ALU.mult)
                ins.then_inc(freed(("bb", i)), 1)
                dve.wait_ge(freed(("bb", i)), NO[("bb", i)] // 8 + 1)
                V.tensor_tensor(ga[:, i, :], ga[:, i, :], gb[:, i, :], ALU.add).then_inc(merged, 1)
            dve.wait_ge(x_again, 48)
            for j in range(4):
                for t, (t0, n) in enumerate(TILES):
                    dve.wait_ge(*full(("out", j, t)))
                    part = xr[0:n, t, j * 256:(j + 1) * 256]
                    V.scalar_tensor_tensor(part, part, ALPHA, bank(("out", j, t))[0:n, 0:256], ALU.mult, ALU.add)\
                        .then_inc(freed(("out", j, t)), 1)
            for t in range(3):
                dve.wait_ge(freed(("out", 3, t)), NO[("out", 3, t)] // 8 + 1)

            def layer_norm(src, dst, n, count, done):
                for i in range(2):
                    last = V.bn_stats(st6[0:n, i, :], src[:, i * 512:(i + 1) * 512])
                link(last)
                V.bn_aggr(mv[0:n], st6[0:n, :, :]).then_inc(var_ready, 1)
                dve.wait_ge(std_ready, count)
                link(V.reciprocal(rstd[0:n], rstd[0:n]))
                link(V.tensor_scalar(dst, src, mv[0:n, 0:1], rstd[0:n], ALU.subtract, ALU.mult))
                link(V.tensor_tensor(dst, dst, ln_g[0:n], ALU.mult))
                V.tensor_tensor(dst, dst, ln_b[0:n], ALU.add).then_inc(done, 1)

            dve.wait_ge(ln1_in, 32)
            for t, (t0, n) in enumerate(TILES):
                layer_norm(xr[0:n, t, :], hrow[0:n, t, :], n, t + 1, h_ready)
            dve.sem_inc(ln_read, 3)
            dve.wait_ge(h_ready, 3)
            for t, (t0, n) in enumerate(TILES):
                dve.wait_ge(*full(("lg", t)))
                link(V.tensor_tensor(lg[0:n, t, :], bank(("lg", t))[0:n, 0:NE], brt[0:n], ALU.add))
                link(V.max(mx[0:n], lg[0:n, t, :]))
                V.max_index(top_idx[0:n, :], mx[0:n], lg[0:n, t, :]).then_inc(freed(("lg", t)), 1)
                dve.wait_ge(freed(("lg", t)), NO[("lg", t)] // 8 + 1)
                V.tensor_scalar(tmp8[0:n, 0:4], mx[0:n, 0:4], mx[0:n, 0:1], None, ALU.subtract).then_inc(max_ready, 1)
                V.tensor_copy(idxf[0:n], top_idx[0:n, :])
                dve.wait_ge(soft4_ready, t + 1)
                link(V.reduce_sum(rstd[0:n], sm[0:n, 0:4], mybir.AxisListType.X))
                link(V.reciprocal(rstd[0:n], rstd[0:n]))
                link(V.tensor_scalar(sm[0:n, 0:4], sm[0:n, 0:4], rstd[0:n], None, ALU.mult))
                for i in range(TOPK):
                    last = V.tensor_scalar(oh[0:n, i, :], cst("iota32", p=n), idxf[0:n, i:i + 1], None, ALU.is_equal)
                link(last)
                link(V.tensor_tensor(msk[0:n, t, :], oh[0:n, 0, :], oh[0:n, 1, :], ALU.add))
                link(V.tensor_tensor(msk[0:n, t, :], msk[0:n, t, :], oh[0:n, 2, :], ALU.add))
                V.tensor_tensor(msk[0:n, t, :], msk[0:n, t, :], oh[0:n, 3, :], ALU.add).then_inc(mask_ready, 1)
                link(V.tensor_scalar(gw[0:n, t, :], oh[0:n, 0, :], sm[0:n, 0:1], None, ALU.mult))
                for i in range(1, TOPK):
                    link(V.scalar_tensor_tensor(gw[0:n, t, :], oh[0:n, i, :], sm[0:n, i:i + 1], gw[0:n, t, :],
                                                ALU.mult, ALU.add))
                dve.sem_inc(soft4_done, 1)
            for t, (t0, n) in enumerate(TILES):
                dve.wait_ge(*full(("rk", t)))
                link(V.scalar_tensor_tensor(rank[0:n, t, 0:NE], bank(("rk", t))[0:n, 0:NE], 1.0, msk[0:n, t, :],
                                            ALU.add, ALU.mult))
                link(V.tensor_scalar(rank[0:n, t, 0:NE], rank[0:n, t, 0:NE], -1.0, None, ALU.add))
                for p in range(1, PASSES):
                    last = V.tensor_scalar(rank[0:n, t, p * NE:(p + 1) * NE], rank[0:n, t, 0:NE], -float(CAP * p),
                                           None, ALU.add)
                last.then_inc(freed(("rk", t)), 1)
            for t in range(3):
                dve.wait_ge(freed(("rk", t)), NO[("rk", t)] // 8 + 1)
            dve.wait_ge(*full(("cnt",)))
            dve.wait_ge(late_in, 16 * (4 + B))
            V.tensor_copy(sm[0:1, 0:1], bank(("cnt",))[0:1, 0:1])
            cnt4 = bank(("cnt",))[0:1, 0:NE].unsqueeze(1).broadcast_to([1, PASSES - 1, NE])
            link(V.tensor_tensor(found[:, 0:NID].rearrange("p (a e) -> p a e", e=NE), cnt4,
                                 lists[:, NID:2 * NID].rearrange("p (a e) -> p a e", e=NE), ALU.is_gt))
            link(V.reduce_sum(low[:, 0:1], found[:, 0:NID], mybir.AxisListType.X))
            V.tensor_copy(n_later[0:1, 0:1], low[:, 0:1])
            link(V.tensor_tensor(found[:, 0:NID], found[:, 0:NID], lists[:, 0:NID], ALU.mult))
            for r in range(RANKS // 8):
                src = found[:, (r % 2) * NID:(r % 2 + 1) * NID]
                dst = found[:, (1 - r % 2) * NID:(2 - r % 2) * NID]
                link(V.max(top24[:, 8 * r:8 * r + 8], src))
                if r < RANKS // 8 - 1:
                    link(V.match_replace(dst, top24[:, 8 * r:8 * r + 8], src, 0.0))
            link(V.tensor_copy(later[0:1, 0, :], top24))
            V.tensor_scalar(later[0:1, 1, :], later[0:1, 0, :], NE - 1, None, ALU.bitwise_and).then_inc(lists_ready, 1)
            dve.wait_ge(lists_ready, 1)
            dve.sem_inc(freed(("cnt",)), 1)

            dve.wait_ge(*full(("gwt",)))
            V.tensor_copy(gwt, bank(("gwt",))[0:NE, 0:NT]).then_inc(gwt_ready, 1)
            dve.wait_ge(gwt_ready, 1)
            dve.sem_inc(freed(("gwt",)), 1)

            def make_onehot(half, col):
                for t, (t0, n) in enumerate(TILES):
                    last = V.tensor_scalar(onehot[0:n, t, half * CAP:(half + 1) * CAP], cst("iota64", p=n),
                                           rank[0:n, t, ds(col, 1)], None, ALU.is_equal)
                return last

            def make_onehot_w(half, col, e):
                for t, (t0, n) in enumerate(TILES):
                    last = V.tensor_scalar(onehot_w[0:n, t, half * CAP:(half + 1) * CAP], cst("iota64", p=n),
                                           rank[0:n, t, ds(col, 1)], gw[0:n, t, ds(e, 1)], ALU.is_equal, ALU.mult)
                return last

            def keep_up(idx):
                dve.wait_ge(up_used, (idx + 1) * UP_UNITS)
                V.tensor_copy(hu, ps[1][:, :]).then_inc(hu_ready, 1)

            def gated(idx, e, base):
                dve.wait_ge(turned, idx + 1)
                for i, dst in ((0, g1), (1, u1)):
                    bias = bgu[:, 8 * i:8 * i + 8, ds(e, 1)].rearrange("p (h c) a -> p h c a", h=2)
                    V.tensor_tensor(dst.rearrange("p (h c) s -> p h c s", h=2),
                                    ps[2 + i][:, :].rearrange("p (c h s) -> p h c s", h=2, s=CAP),
                                    bias.broadcast_to([128, 2, 4, CAP]), ALU.add).then_inc(blk, 1)
                dve.wait_ge(blk, base + 1)
                V.tensor_scalar(g1[:, :, :], g1[:, :, :], LIMIT, None, ALU.min).then_inc(gate_ready, 1)
                dve.wait_ge(blk, base + 2)
                V.tensor_scalar(u1[:, :, :], u1[:, :, :], LIMIT, -LIMIT, ALU.min, ALU.max).then_inc(blk, 1)
                dve.wait_ge(blk, base + 3)
                dve.wait_ge(gate_ready, idx + 1)
                V.scalar_tensor_tensor(u1[:, :, :], u1[:, :, :], 1.0, g1[:, :, :], ALU.add, ALU.mult).then_inc(blk, 1)
                dve.wait_ge(blk, base + 4)
                dve.wait_ge(swish_ready, idx + 1)
                V.tensor_tensor(actt[:, :, :], u1[:, :, :], sg[:, :, :], ALU.mult).then_inc(act_ready, 1)

            def add_pieces(pair):
                for i in range(6):
                    t, half = i // 2, i % 2
                    n = TILES[t][1]
                    dve.wait_ge(pieces, pair * 6 + i + 1)
                    part = y[0:n, t, half * 512:(half + 1) * 512]
                    V.tensor_tensor(part, part, ps[5 + i % 3][0:n, :], ALU.add).then_inc(added, 1)

            def pair_of_blocks(pair, first=False, last=False):
                e = pair * 2
                gated(e, e, e * 4)
                if not first:
                    add_pieces(pair - 1)
                    dve.wait_ge(slots_turned, pair)
                make_onehot_w(0, e, e)
                make_onehot_w(1, e + 1, e + 1).then_inc(onehot_w_ready, 1)
                if not last:
                    dve.wait_ge(gathered, pair + 1)
                    make_onehot(0, e + 2)
                    make_onehot(1, e + 3).then_inc(onehot_ready, 1)
                keep_up(e + 1)
                gated(e + 1, e + 1, e * 4 + 4)
                if not last:
                    keep_up(e + 2)

            make_onehot(0, 0)
            make_onehot(1, 1).then_inc(onehot_ready, 1)
            for t, (t0, n) in enumerate(TILES):
                for i in range(2):
                    dve.wait_ge(*full(("yb", t, i)))
                    V.scalar_tensor_tensor(y[0:n, t, i * 512:(i + 1) * 512], hrow[0:n, t, i * 512:(i + 1) * 512], ALPHA,
                                           bank(("yb", t, i))[0:n, :], ALU.mult, ALU.add)\
                        .then_inc(freed(("yb", t, i)), 1)
            keep_up(0)
            pair_of_blocks(0, first=True)
            with dve.Fori(1, NE // 2 - 1) as pair:
                pair_of_blocks(dve.snap(pair))
            pair_of_blocks(NE // 2 - 1, last=True)
            add_pieces(NE // 2 - 1)
            count = dve.value_load(n_later[0:1, 0:1], min_val=0, max_val=RANKS)
            with dve.If(count > 0):
                dve.wait_ge(slots_turned, NE // 2)
                V.memset(onehot[:, :, CAP:], 0.0)
                V.memset(onehot_w[:, :, CAP:], 0.0)
                V.memset(res[CAP:, :], 0.0)
                with dve.Fori(0, count) as loop:
                    b = dve.snap(loop)
                    col = dve.value_load(later[0:1, 0, ds(b, 1)], min_val=0, max_val=NE * PASSES - 1)
                    e = dve.value_load(later[0:1, 1, ds(b, 1)], min_val=0, max_val=NE - 1)
                    dve.wait_ge(slots_turned, b + NE // 2)
                    make_onehot(0, col).then_inc(onehot_ready, 1)
                    make_onehot_w(0, col, e).then_inc(onehot_w_ready, 1)
                    keep_up(b + NE)
                    gated(b + NE, e, b * 4 + NE * 4)
                    add_pieces(b + NE // 2)
            dve.wait_ge(ln2_in, 32)
            dve.wait_ge(added, 6 * (NE // 2))
            for t, (t0, n) in enumerate(TILES):
                layer_norm(y[0:n, t, :], y[0:n, t, :], n, t + 4, y_final)


INPUTS = ["x_prompt", "x_sample", "state_gla", "state_pool", "w_in", "w_gk2", "b_gk", "gla_norm_w", "w_branch_gla",
          "w_pool_grp", "pool_scale", "w_branch_pool", "b_gates", "w_out", "ln1_g", "ln1_b", "w_router", "b_router",
          "w_gu", "b_gu", "w_down", "b_down", "ln2_g", "ln2_b"]
OUTPUTS = [(1, NP, D), (B, L, D), (1, 1, HEADS, DK, DV), (1, 1, PBUF, 512), (1, B, HEADS, DK, DV), (1, B, PBUF, 512)]


def kernel(**inputs):
    import numpy as _np
    import concourse.bacc as _bacc
    from concourse import mybir as _mybir
    from concourse.bass_utils import run_bass_kernel_spmd as _run

    nc = _bacc.Bacc("TRN2", target_bir_lowering=False, num_devices=1)
    arrays, args = {}, []
    named = [(n, _np.ascontiguousarray(inputs[n])) for n in INPUTS]
    named += list(zip(("c_cols", "c_starts", "c_lists"), constants()))
    for name, a in named:
        arrays[f"in_{name}"] = a
        args.append(nc.dram_tensor(f"in_{name}", a.shape, _mybir.dt.from_np(a.dtype), kind="ExternalInput").ap())
    for i, shape in enumerate(OUTPUTS):
        args.append(nc.dram_tensor(f"out_{i}", shape, _mybir.dt.float32, kind="ExternalOutput").ap())
    build(nc, *args)
    r = _run(nc, [arrays], core_ids=[0])
    return tuple(r.results[0][f"out_{i}"] for i in range(len(OUTPUTS)))
```

```python
from contextlib import ExitStack

import concourse.bass as bass
from concourse import mybir

D = 1024
KC = D // 128
NP, B, L = 256, 8, 8
NS = B * L
NT = NP + NS
HEADS, DK, DV = 4, 128, 256
C = 64
PBUF = 15
NE, TOPK = 32, 4
CAP = 64
PASSES = NT // CAP
RANKS = 24
ALPHA = 2.0 ** 0.25
LIMIT, GLU_ALPHA = 7.0, 1.702
RMS_EPS, LN_EPS = 1e-6, 1e-5
TILES = [(0, 128), (128, 128), (256, 64)]
ORDER = (2, 0, 1)

RING = 8
HIGH = 8
XLOW = 10
MORE = 4
MORE_AT = 12
SLOTS = MORE_AT + MORE
UNIT = 2048
MIX_UNITS = ([("k", i) for i in range(2)] + [("q", i) for i in range(2)] + [("v", i) for i in range(4)]
             + [(kind, i) for i in range(4) for kind in ("g", "ga")]
             + [("u", i) for i in range(2)] + [("ba", i) for i in range(4)] + [("gb", i) for i in range(4)]
             + [("bb", i) for i in range(2)]
             + [("out", i) for i in range(4)])
NSPLIT = len(MIX_UNITS) - 4
UNIT_NO = {u: n for n, u in enumerate(MIX_UNITS)}
NMIX = len(MIX_UNITS)
UP_UNITS, DOWN_UNITS = KC, KC // 2
EXP_UNITS = UP_UNITS + DOWN_UNITS
COL0 = {"q": 0, "k": 512, "v": 1024, "lr": 2048, "g": 2064, "u": 3088, "ga": 3600, "gb": 4624}

PRODUCTS = ([("xt", i) for i in range(KC)] + [("k", i) for i in range(4)] + [("lr",), ("cols",)] + [("q", 0)]
            + [("gk", i) for i in range(4)] + [("q", i) for i in range(1, 4)] + [("bgt",)]
            + [("v", j, t) for j in range(4) for t in range(3)]
            + [("a", t) for t in range(3)] + [("kt", t) for t in range(3)]
            + [x for h in range(HEADS) for x in
               [("o", h, 0), ("o", h, 1), ("g", 2 * h), ("kv", h, 0), ("kv", h, 1), ("g", 2 * h + 1)]
               + [("kvs", h, i) for i in range(4)] + [("ga", 2 * h), ("ga", 2 * h + 1), ("rms", h)]]
            + [("u", i) for i in range(4)] + [("ba", i) for i in range(8)]
            + [("pb",), ("up",), ("us",)] + [("gb", i) for i in range(6)] + [("grp", i) for i in range(4)]
            + [("gb", i) for i in range(6, 8)] + [("bb", i) for i in range(8)]
            + [("outs", 0), ("outs", 1)] + [("out", j, 0) for j in range(4)]
            + [("ht", 2, 0), ("ht", 2, 1), ("lg", 2), ("out", 0, 1), ("ht", 0, 0), ("ht", 0, 1), ("out", 1, 1), ("rk", 2)]
            + [("lg", 0), ("out", 2, 1), ("rk", 0), ("out", 3, 1), ("ht", 1, 0), ("ht", 1, 1), ("lg", 1)]
            + [("rk", 1), ("cnt",), ("gwt",)])
NO = {p: n for n, p in enumerate(PRODUCTS)}
LAST_USE = [len(range(i, len(PRODUCTS), 8)) for i in range(8)]



def unit_at(n):
    if n < UP_UNITS:
        return True, 0, n
    if n >= NE * EXP_UNITS - DOWN_UNITS:
        return False, NE - 1, n - (NE * EXP_UNITS - DOWN_UNITS)
    e, r = divmod(n - UP_UNITS, EXP_UNITS)
    return (True, e + 1, r) if r < UP_UNITS else (False, e, r - UP_UNITS)


UNIT_SEQ = {unit_at(n): n for n in range(NE * EXP_UNITS)}
PERIOD = 4

CST = {}
NCST = 0
for _name, _n in (("ident", 128), ("ones", 128), ("pmask", 128), ("smask", 64), ("upto", 128),
                  ("iota64", 64), ("iota32", 32), ("bmask", B), ("rcnt", 64)):
    CST[_name] = (NCST, _n)
    NCST += _n


def constants():
    import numpy as np
    c = np.zeros((128, NCST), np.float32)
    p = np.arange(128)

    def put(name, value):
        at, n = CST[name]
        c[:, at:at + n] = value
    i = np.arange(128)
    put("ident", p[:, None] == i)
    put("ones", 1.0)
    put("pmask", (p[:, None] // C == i // C) & (p[:, None] <= i))
    j = np.arange(64)
    put("smask", (p[:, None] // L == j // L) & (p[:, None] <= j))
    put("upto", p[:, None] <= i)
    put("iota64", j + 1.0)
    put("iota32", np.arange(32))
    put("bmask", p[:, None] // L == np.arange(B))
    t = np.arange(16)
    put("rcnt", np.concatenate([1.0 / np.minimum(2 ** (g + 1), t + 1) for g in range(4)]))
    starts = np.ones((128, HEADS, NT), np.float32)
    starts[:, :, 0:NP:C] = 0.0
    starts[:, :, NP:NT:L] = 0.0
    ids = np.arange(NE, NE * PASSES, dtype=np.float32)
    lists = np.stack([ids, (ids // NE) * CAP])
    return c, starts.reshape(128, HEADS * NT), lists.reshape(1, -1)


NID = NE * (PASSES - 1)

XT = 0
QR = 2560
KR = 3840
QE = 5120
KE = 6400
WLR = 7680
BB = 7680
EE = 8960
GA2 = 9216
VR = 10240
KLT = 13312
OT = 14848
WRT = GA2 + 640
SP = 17408
SS = 19456
G = 21504
SO = 24064
RMS = SO + 2048
CONST = 26624
BGU = CONST + NCST
COLS = BGU + 512
DEC = COLS + 32
BR = DEC + 48
MISC = BR + 32
ARENA = MISC + 64
H = 0
Y = 3072
XGT = 6144
OHW = 7168
ACTT = 7552
G1 = 8064
OH = 8704
U1 = 9088
SG = 9600
HG = 10112
HU = 10624
RES = 11136
RK = 12352
GW = 12832
MSK = 12928
LG = 13024
MX = 13120
RT = 13152
LISTS = 13536
GWT = 14120
BDR = 14440
LN2 = BDR + D
ST = LN2 + 2 * D
MORE_SLOTS = 18432


def build(nc, x_p, x_s, state_gla, state_pool, w_in, w_gk2, b_gk, gla_norm_w, w_bgla, w_grp, pool_scale,
          w_bpool, b_gates, w_out, ln1_g, ln1_b, w_router, b_router, w_gu, b_gu, w_down, b_down, ln2_g, ln2_b,
          c_cols, c_starts, c_lists, y_p, y_s, ngp, npp, ngs, nps):
    f32 = mybir.dt.float32
    i32 = mybir.dt.int32
    u32 = mybir.dt.uint32
    ALU = mybir.AluOpType
    ACT = mybir.ActivationFunctionType
    ds = bass.ds

    with ExitStack() as ctx:
        def sem(name):
            return ctx.enter_context(nc.semaphore(name))

        f32r = mybir.dt.float32r
        with nc.sbuf_tensor("arena_r", [128, ARENA], f32r) as ar_r, \
                nc.sbuf_tensor("ring_r", [128, MORE_AT, UNIT], f32r) as ring_r:
            pass
        ar = ctx.enter_context(nc.sbuf_tensor("arena", [128, ARENA], f32))
        ring = ctx.enter_context(nc.sbuf_tensor("ring", [128, MORE_AT, UNIT], f32))
        top_idx = ctx.enter_context(nc.sbuf_tensor("top_idx", [128, 8], u32))
        later = ctx.enter_context(nc.sbuf_tensor("later", [1, 2, RANKS], i32))
        n_later = ctx.enter_context(nc.sbuf_tensor("n_later", [1, 8], i32))
        ps = [ctx.enter_context(nc.psum_tensor(f"bank{i}", [128, 512], f32)) for i in range(8)]

        def reg(at, n, *dims, p=128, p0=0):
            v = ar[p0:p0 + p, at:at + n]
            if len(dims) == 1:
                v = v.rearrange("p (a b) -> p a b", a=dims[0])
            if len(dims) == 2:
                v = v.rearrange("p (a b c) -> p a b c", a=dims[0], b=dims[1])
            return v

        def cst(name, p=128, n=None):
            at, full = CST[name]
            return ar[0:p, CONST + at:CONST + at + (n or full)]

        ident = cst("ident")

        def reg_r(at, n, dim):
            return ar_r[:, at:at + n].rearrange("p (a b) -> p a b", a=dim)

        xt = (reg_r(XT, KC * NT, KC),
              ring_r[:, XLOW:XLOW + 2, :].rearrange("p s n -> p (s n)")[:, 0:KC * NT].rearrange("p (a b) -> p a b", a=KC))
        wlr_parts = (reg_r(WLR, KC * 128, KC), reg_r(WLR + KC * 128, KC * 128, KC))
        o_parts = (reg_r(VR, 8 * NT, 8), reg_r(OT, 8 * NT, 8))
        pg = (reg_r(QR, 4 * NT, 4), reg_r(KLT, 4 * NT, 4))
        q = reg(QR, HEADS * NT, HEADS)
        k = reg(KR, HEADS * NT, HEADS)
        qe = reg(QE, HEADS * NT, HEADS)
        ke = reg(KE, HEADS * NT, HEADS)
        bb = reg(BB, HEADS * NT, HEADS)
        ee = reg(EE, HEADS * NT, HEADS)
        xr = reg(VR, 3 * D, 3)
        v = xr
        klt = reg(KLT, 3 * 512, 3)
        ot = reg(OT, 8 * NT, 8)
        starts = reg(OT, HEADS * NT)
        eb = reg(OT + HEADS * NT, HEADS * NT, HEADS)
        bl = reg(SP, HEADS * NT, HEADS)
        at_ = reg(BB, 3 * 512, 3)
        sq = reg(QE, 2 * NT, 2)
        rms = reg(RMS, NT)
        sp_st = reg(SP, 2 * 4 * DV, 2, 4)
        ss_st = [reg(SS, B * DV, B), reg(SO, B * DV, B)]
        gs = reg(G, 8 * NT, 8)
        ga = [reg(QE + (2 + i) * NT, NT) if i < 6 else reg(GA2 + (i - 6) * NT, NT) for i in range(8)]
        gb = reg(OT, 8 * NT, 8)
        klm = reg(KR, B * DK, B, p=NS)
        po = reg(KR, 4 * NT, 4)
        up_pad = reg(BB, 4 * (PBUF + NP), 4)
        us_pad = reg(KLT, 4 * B * (PBUF + L), 4, B)
        spb = reg(SP, 512, p=B * PBUF)
        wgrp = reg(SP + 512, 512, 4)
        wrt = reg(WRT, 256, KC)
        pool_out_p = ar[0:PBUF, SP + 1024:SP + 1536]
        pool_out_s = ar[0:NS, SS:SS + 512]
        ln1 = (reg(KR, D), reg(BB, D))
        ln2 = (reg(LN2, D), reg(LN2 + D, D))
        wlr = reg(KE, KC * 16, KC)
        wgk2 = ar[0:16, KE + 128:KE + 640]
        lrt = ar[0:16, KE + 640:KE + 960]
        rows = ar[0:26, KE + 960:KE + 1088]
        bgu_rows = ar[0:NE, G:G + 2048]
        bdn_rows = ar[0:NE, BDR:BDR + D]
        gwt = ar[0:NE, GWT:GWT + NT]
        bgu = reg(BGU, 512, 16)
        cols = reg(COLS, 26)
        dec = reg(DEC, 48, HEADS)
        brt = reg(BR, NE)
        hrow = reg(H, 3 * D, 3)
        y = reg(Y, 3 * D, 3)
        xgt = reg(XGT, 1024, KC)
        onehot = reg(OH, 3 * 128, 3)
        onehot_w = reg(OHW, 3 * 128, 3)
        actt = reg(ACTT, 512, KC)
        g1 = reg(G1, 512, KC)
        u1 = reg(U1, 512, KC)
        sg = reg(SG, 512, KC)
        hg = reg(HG, 512)
        hu = reg(HU, 512)
        res = reg(RES, D)
        slot_t = reg(ST, NT)
        rank = reg(RK, 3 * PASSES * NE, 3)
        gw = reg(GW, 3 * NE, 3)
        msk = reg(MSK, 3 * NE, 3)
        lg = reg(LG, 3 * NE, 3)
        mx = reg(MX, 8)
        oh = reg(RT, 3 * TOPK * NE, 3, TOPK)
        lists = ar[0:1, LISTS:LISTS + 2 * NID]
        found = ar[0:1, LISTS + 2 * NID:LISTS + 4 * NID]
        st6 = reg(MISC, 12, 2)
        mv = reg(MISC + 12, 2)
        rstd = reg(MISC + 14, 1)
        eps_rms = reg(MISC + 16, 1)
        eps_ln = reg(MISC + 17, 1)
        idxf = reg(MISC + 22, 8)
        sm = reg(MISC + 30, 3 * TOPK, 3)
        rsum = reg(MISC + 42, 3)
        rstd2 = reg(MISC + 45, 3)
        top24 = ar[0:1, LISTS + 4 * NID:LISTS + 4 * NID + RANKS]
        low = ar[0:1, LISTS + 4 * NID + RANKS:LISTS + 4 * NID + 2 * RANKS]

        filled = [sem(f"slot{i}_filled") for i in range(SLOTS)]
        bank_full = [sem(f"bank{i}_full") for i in range(8)]
        bank_free = [sem(f"bank{i}_free") for i in range(8)]
        x_in = sem("x_in")
        ident_in = sem("ident_in")
        cst_in = sem("cst_in")
        small_in = sem("small_in")
        bgu_in = sem("bgu_in")
        starts_in = sem("starts_in")
        ss_in = [sem(f"ss_in{i}") for i in range(HEADS)]
        x_again = sem("x_again")
        late_in = sem("late_in")
        ln1_in = sem("ln1_in")
        ln2_in = sem("ln2_in")
        stored_s = sem("stored_s")
        stored_p = sem("stored_p")
        stored = sem("stored")
        y_stored = sem("y_stored")
        xt_high = sem("xt_high")
        xt_ready = sem("xt_ready")
        wlr_high = sem("wlr_high")
        wlr_ready = sem("wlr_ready")
        high_ready = sem("high_ready")
        split_ready = sem("split_ready")
        o_high = sem("o_high")
        o_split = sem("o_split")
        pg_high = sem("pg_high")
        lr_ready = sem("lr_ready")
        z_ready = sem("z_ready")
        soft_ready = sem("soft_ready")
        diff_ready = sem("diff_ready")
        exp_ready = sem("exp_ready")
        qk_in = sem("qk_in")
        qk_ready = sem("qk_ready")
        v_ready = sem("v_ready")
        sig_ready = sem("sig_ready")
        at_ready = sem("at_ready")
        klt_ready = sem("klt_ready")
        klm_ready = sem("klm_ready")
        sp_ready = sem("sp_ready")
        ss_ready = sem("ss_ready")
        sq_ready = sem("sq_ready")
        ot_ready = sem("ot_ready")
        ga_ready = sem("ga_ready")
        merged = sem("merged")
        pads_zero = sem("pads_zero")
        u_ready = sem("u_ready")
        po_ready = sem("po_ready")
        pg_ready = sem("pg_ready")
        pool_out_ready = sem("pool_out_ready")
        gb_ready = sem("gb_ready")
        var_ready = sem("var_ready")
        std_ready = sem("std_ready")
        h_ready = sem("h_ready")
        ln_step = sem("ln_step")
        ht_ready = sem("ht_ready")
        mask_ready = sem("mask_ready")
        max_ready = sem("max_ready")
        soft4_ready = sem("soft4_ready")
        soft4_done = sem("soft4_done")
        gwt_ready = sem("gwt_ready")
        lists_ready = sem("lists_ready")
        yb_full = sem("yb_full")
        yb_used = sem("yb_used")
        y_final = sem("y_final")
        ys_final = sem("ys_final")
        y_centred = sem("y_centred")
        y_scaled = sem("y_scaled")
        dve_step = sem("dve_step")
        act_step = sem("act_step")
        onehot_early = sem("onehot_early")
        onehot_ready = sem("onehot_ready")
        onehot_w_ready = sem("onehot_w_ready")
        gathered = sem("gathered")
        xgt_ready = sem("xgt_ready")
        slots_turned = sem("slots_turned")
        slot_ready = sem("slot_ready")
        up_used = sem("up_used")
        down_used = sem("down_used")
        hg_ready = sem("hg_ready")
        hu_ready = sem("hu_ready")
        turned = sem("turned")
        gate_ready = sem("gate_ready")
        swish_ready = sem("swish_ready")
        act_ready = sem("act_ready")
        res_ready = sem("res_ready")
        pieces = sem("pieces")
        added = sem("added")
        blk = sem("blk_step")

        def full(name):
            n = NO[name]
            return bank_full[n % 8], n // 8 + 1

        def freed(name):
            return bank_free[NO[name] % 8]

        def bank(name):
            return ps[NO[name] % 8]

        def unit_landed(kind, i):
            n = UNIT_NO[(kind, i)]
            return filled[n % RING], 16 * (n // RING + 1)

        def unit(kind, i):
            return ring[:, UNIT_NO[(kind, i)] % RING, :]

        LAST = {}
        for kind, i in MIX_UNITS:
            if kind == "v":
                LAST[(kind, i)] = ("v", i, 2)
            elif kind == "out":
                LAST[(kind, i)] = (kind, i, 1)
            elif kind == "bb":
                LAST[(kind, i)] = (kind, 4 * i + 3)
            else:
                LAST[(kind, i)] = (kind, 2 * i + 1)

        AFTER = {}
        for n, (kind, i) in enumerate(MIX_UNITS[:NSPLIT - 2]):
            for half in range(2):
                if kind == "v":
                    p = ("v", i, 2)
                elif MIX_UNITS[n + 2][0] == "bb":
                    p = (kind, 2 * i + 1)
                else:
                    p = (kind, 2 * i + half)
                AFTER.setdefault(p, []).append((n + 2, half))

        def parts(n):
            chunks = 4 if MIX_UNITS[n][0] == "bb" else KC
            return [x.rearrange("p (c n) -> p c n", c=chunks)
                    for x in (ring[:, n % RING, :], ring_r[:, HIGH + n % 2, :], ring_r[:, n % RING, :])]

        def half_of(view, half):
            n = view.shape[2] // 2
            return view[:, :, half * n:(half + 1) * n]

        POSITIONS = ([MORE_AT + i for i in range(MORE)] + [XLOW, XLOW + 1] + [(NMIX + i) % RING for i in range(4)]
                     + [HIGH, HIGH + 1] + [(NMIX + i) % RING for i in range(4, 8)])
        FREE_AFTER = ([None] * MORE + [("gb", 7)] * 2 + [LAST[u] for u in MIX_UNITS[-8:-4]] + [LAST[("bb", 1)]] * 2
                      + [LAST[u] for u in MIX_UNITS[-4:]])
        MIX_FILLS = [len(range(s, NMIX, RING)) if s < RING else 0 for s in range(SLOTS)]

        def slot_view(pos):
            s = POSITIONS[pos]
            if s < MORE_AT:
                return ring[:, s, :]
            return reg(MORE_SLOTS + (s - MORE_AT) * UNIT, UNIT)

        def landed(n, m=None):
            s = POSITIONS[n % SLOTS]
            value = 16 * (MIX_FILLS[s] + n // SLOTS + 1)
            return filled[s], value if m is None else m * (16 * PERIOD * EXP_UNITS // SLOTS) + value

        def landed_later(pos, b):
            s = POSITIONS[pos]
            return filled[s], b * 16 + 16 * (MIX_FILLS[s] + NE * EXP_UNITS // SLOTS + 1)

        def by_chunk(view, t):
            if t == 0:
                return view[:, :, 0:NP].rearrange("p h (c i) -> p h c i", i=C)
            return view[:, :, NP:NT].rearrange("p h (c i) -> p h c i", i=L)

        ex = [ps[(i + 2) % 8] for i in range(8)]

        block = ctx.enter_context(nc.Block())

        @block.sync
        def _(sp):
            for t, (t0, n) in enumerate(TILES):
                src = x_p[0, t0:t0 + n, :] if t < 2 else x_s.rearrange("b s d -> (b s) d")
                sp.dma_start(xr[0:n, t, :], src).then_inc(x_in, 16)
            sp.dma_start(ident, c_cols[:, 0:128]).then_inc(ident_in, 16)
            for n, (kind, i) in enumerate(MIX_UNITS):
                if n == 1:
                    sp.dma_start(ar[:, CONST + 128:CONST + NCST], c_cols[:, 128:]).then_inc(cst_in, 16)
                    sp.dma_start(wlr, w_in[0, :, COL0["lr"]:COL0["lr"] + 16].rearrange("(c p) n -> p c n", p=128))\
                        .then_inc(small_in, 16)
                    sp.dma_start(wgk2, w_gk2[0, :, :]).then_inc(small_in, 16)
                    at = 0
                    for vec, count in ((b_gates, 16), (b_gk, 4), (gla_norm_w, 2), (pool_scale, 4)):
                        sp.dma_start(rows[at:at + count, :], vec[0, :].rearrange("(c p) -> c p", p=128)).then_inc(small_in, 16)
                        at += count
                if n >= RING:
                    sp.wait_ge(*full(LAST[MIX_UNITS[n - RING]]))
                dst = ring[:, n % RING, :]
                if kind in COL0:
                    src = w_in[0, :, COL0[kind] + 256 * i:COL0[kind] + 256 * (i + 1)]
                    sp.dma_start(dst.rearrange("p (c n) -> p c n", c=KC),
                                 src.rearrange("(c p) n -> p c n", p=128)).then_inc(filled[n % RING], 16)
                elif kind == "bb":
                    src = w_bpool[0, :, 512 * i:512 * (i + 1)]
                    sp.dma_start(dst.rearrange("p (c n) -> p c n", c=4),
                                 src.rearrange("(c p) n -> p c n", p=128)).then_inc(filled[n % RING], 16)
                else:
                    w = w_bgla if kind == "ba" else w_out
                    src = w[0, :, 256 * i:256 * (i + 1)]
                    sp.dma_start(dst.rearrange("p (c n) -> p c n", c=KC),
                                 src.rearrange("(c p) n -> p c n", p=128)).then_inc(filled[n % RING], 16)

            def load_unit(is_up, e, j, pos):
                s = POSITIONS[pos]
                dst = slot_view(pos)
                if is_up:
                    src = w_gu[0, ds(e, 1), j * 128:(j + 1) * 128, :].rearrange("e p n -> p (e n)")
                    sp.dma_start(dst, src).then_inc(filled[s], 16)
                else:
                    src = w_down[0, ds(e, 1), j * 256:(j + 1) * 256, :].rearrange("e (c p) n -> p (e c) n", p=128)
                    sp.dma_start(dst.rearrange("p (c n) -> p c n", c=2), src).then_inc(filled[s], 16)

            def next_unit(n, m=None):
                was_up, e, j = unit_at(n - SLOTS)
                count = e * (UP_UNITS if was_up else DOWN_UNITS) + j + 1
                if m is not None:
                    count = m * (PERIOD * (UP_UNITS if was_up else DOWN_UNITS)) + count
                sp.wait_ge(up_used if was_up else down_used, count)
                is_up, e, j = unit_at(n)
                load_unit(is_up, e if m is None else m * PERIOD + e, j, n % SLOTS)

            sp.wait_ge(stored_s, 16 * HEADS)
            sp.wait_ge(stored_p, 16 * HEADS)
            sp.wait_ge(po_ready, 5)
            sp.wait_ge(stored, 16 * 2)
            sp.wait_ge(late_in, 16 * (3 + B))
            for n in range(SLOTS):
                if n >= MORE:
                    sp.wait_ge(*full(FREE_AFTER[n]))
                load_unit(*unit_at(n), n)
            first = UNIT_SEQ[(True, 3, 0)]
            for n in range(SLOTS, first):
                next_unit(n)
            with sp.Fori(0, (NE - 3) // PERIOD) as loop:
                m = sp.snap(loop)
                for n in range(first, first + PERIOD * EXP_UNITS):
                    next_unit(n, m)
            for n in range(first + (NE - 3) // PERIOD * PERIOD * EXP_UNITS, NE * EXP_UNITS):
                next_unit(n)
            sp.wait_ge(lists_ready, 1)
            count = sp.value_load(n_later[0:1, 0:1], min_val=0, max_val=RANKS)
            with sp.If(count > 0):
                with sp.Fori(0, count) as b:
                    e = sp.value_load(later[0:1, 1, ds(b, 1)], min_val=0, max_val=NE - 1)
                    sp.wait_ge(down_used, b * DOWN_UNITS + NE * DOWN_UNITS)
                    for j in range(EXP_UNITS):
                        load_unit(j < UP_UNITS, e, j if j < UP_UNITS else j - UP_UNITS, j)
            for t, (t0, n) in enumerate(TILES):
                if t < 2:
                    sp.wait_ge(y_final, 2 * t + 2)
                else:
                    sp.wait_ge(ys_final, 2)
                dst = y_p[0, t0:t0 + n, :] if t < 2 else y_s.rearrange("b s d -> (b s) d")
                sp.dma_start(dst, y[0:n, t, :]).then_inc(y_stored, 16)
            sp.wait_ge(y_stored, 16 * 3)
            sp.wait_ge(stored_s, 16 * 4)
            sp.wait_ge(stored_p, 16 * 4)

        @block.gpsimd
        def _(pool):
            pool.wait_ge(x_in, 48)
            pool.dma_start(bgu_rows, b_gu[0, :, :]).then_inc(bgu_in, 16)
            pool.dma_start(starts, c_starts).then_inc(starts_in, 16)
            pool.dma_start(brt, b_router[0:1, :].broadcast_to([128, NE])).then_inc(starts_in, 16)

            def load_states(h):
                pool.dma_start(ss_st[h % 2], state_gla[0, :, h, :, :].rearrange("b d v -> d b v"))\
                    .then_inc(ss_in[h], 16)
            load_states(0)
            load_states(1)
            for h in range(HEADS):
                pool.wait_ge(sp_ready, 4 * (h + 1))
                pool.dma_start(ngp[0, 0, h, :, :], sp_st[:, h % 2, 3, :]).then_inc(stored_p, 16)
                pool.wait_ge(ss_ready, h + 1)
                pool.dma_start(ngs[0, :, h, :, :].rearrange("b d v -> d b v"), ss_st[h % 2]).then_inc(stored_s, 16)
                if h < 2:
                    pool.wait_ge(stored_s, 16 * (h + 1))
                    load_states(h + 2)
            pool.wait_ge(stored_p, 16 * 4)
            pool.wait_ge(stored_s, 16 * 4)
            pool.dma_start(spb, state_pool[0, :, :, :].rearrange("b r c -> (b r) c")).then_inc(late_in, 16)
            pool.dma_start(wgrp, w_grp[0, :, :, :].rearrange("g c d -> c g d")).then_inc(late_in, 16)
            pool.dma_start(wrt, w_router[0, :, :].rearrange("(c p) n -> p c n", p=128)).then_inc(late_in, 16)
            pool.dma_start(nps[0, :, 0:PBUF - L, :], state_pool[0, :, L:PBUF, :]).then_inc(stored, 16)
            pool.wait_ge(pool_out_ready, 2)
            pool.dma_start(npp[0, 0, :, :], pool_out_p).then_inc(stored, 16)
            for b in range(B):
                pool.dma_start(nps[0, b, PBUF - L:PBUF, :], pool_out_s[b * L:(b + 1) * L, :]).then_inc(late_in, 16)
            pool.wait_ge(late_in, 16 * (3 + B))
            pool.wait_ge(*full(("ba", 7)))
            for t, (t0, n) in enumerate(TILES):
                src = x_p[0, t0:t0 + n, :] if t < 2 else x_s.rearrange("b s d -> (b s) d")
                pool.dma_start(xr[0:n, t, :], src).then_inc(x_again, 16)
            pool.wait_ge(*full(("grp", 3)))
            pool.dma_start(ln1[0], ln1_g[0:1, :].broadcast_to([128, D])).then_inc(ln1_in, 16)
            pool.dma_start(ln1[1], ln1_b[0:1, :].broadcast_to([128, D])).then_inc(ln1_in, 16)
            pool.wait_ge(*full(("bb", 7)))
            pool.dma_start(lists, c_lists).then_inc(late_in, 16)
            pool.wait_ge(*full(("lg", 1)))
            pool.dma_start(bdn_rows, b_down[0, :, :]).then_inc(bgu_in, 16)
            pool.dma_start(ln2[0], ln2_g[0:1, :].broadcast_to([128, D])).then_inc(ln2_in, 16)
            pool.dma_start(ln2[1], ln2_b[0:1, :].broadcast_to([128, D])).then_inc(ln2_in, 16)
            pool.wait_ge(stored, 16 * 2)
            pool.wait_ge(ln2_in, 32)
            for t in range(2):
                pool.wait_ge(y_scaled, t + 1)
                for half in range(2):
                    part = y[:, t, half * 512:(half + 1) * 512]
                    nc.gpsimd.tensor_tensor(part, part, ln2[1][:, half * 512:(half + 1) * 512], ALU.add)\
                        .then_inc(y_final, 1)

        @block.tensor
        def _(pe):
            mm = nc.tensor.matmul

            def claim(name):
                n = NO[name]
                if n >= 8:
                    pe.wait_ge(bank_free[n % 8], n // 8)
                return ps[n % 8]

            THREE = ((0, 0), (0, 1), (1, 0))

            def split(n, half):
                pe.wait_ge(split_ready, 2 * n + half + 1)

            def weights_times(kind, i, rhs, chunks=KC, per_unit=2, between=None):
                n = UNIT_NO[(kind, i // per_unit)]
                w = parts(n)[1:]
                split(n, (i % per_unit) * 2 // per_unit)
                o = claim((kind, i))
                f0 = (i % per_unit) * 128
                for c in range(chunks):
                    if between is not None:
                        between(c)
                    for a, b in THREE:
                        last = mm(o[:, 0:NT], w[a][:, c, f0:f0 + 128], rhs[b][:, c, :],
                                  start=c == 0 and a + b == 0, stop=c == chunks - 1 and a == 1)
                last.then_inc(full((kind, i))[0], 1)

            pe.wait_ge(ident_in, 16)
            pe.wait_ge(x_in, 48)
            for c in range(KC):
                o = claim(("xt", c))
                for t, (t0, n) in enumerate(TILES):
                    last = nc.tensor.transpose(o[:, t0:t0 + n], xr[0:n, t, c * 128:(c + 1) * 128], ident[0:n, 0:n])
                last.then_inc(full(("xt", c))[0], 1)
            o = claim(("k", 0))
            w = parts(0)[1:]
            pe.wait_ge(high_ready, 1)
            for a, b in THREE:
                for c in range(KC):
                    if a + b == 0:
                        pe.wait_ge(xt_high, c + 1)
                    elif b == 1:
                        pe.wait_ge(xt_ready, c + 1)
                    elif c == 0:
                        split(0, 0)
                    last = mm(o[:, 0:NT], w[a][:, c, 0:128], xt[b][:, c, :], start=c == 0 and a + b == 0,
                              stop=c == KC - 1 and a == 1)
            last.then_inc(full(("k", 0))[0], 1)
            for i in range(1, 4):
                weights_times("k", i, xt)
            pe.wait_ge(small_in, 16 * 6)
            pe.wait_ge(cst_in, 16)
            pe.wait_ge(wlr_ready, 1)
            o = claim(("lr",))
            for c in range(KC):
                for a, b in THREE:
                    last = mm(o[:, 0:NT], wlr_parts[a][:, c, :], xt[b][:, c, :],
                              start=c == 0 and a + b == 0, stop=c == KC - 1 and a == 1)
            last.then_inc(full(("lr",))[0], 1)
            o = claim(("cols",))
            nc.tensor.transpose(o[:, 0:26], rows, ident[0:26, 0:26]).then_inc(full(("cols",))[0], 1)
            weights_times("q", 0, xt)
            pe.wait_ge(lr_ready, 1)
            for i in range(4):
                o = claim(("gk", i))
                mm(o[:, 0:NT], wgk2[:, i * 128:(i + 1) * 128], lrt, start=True, stop=True)\
                    .then_inc(full(("gk", i))[0], 1)
            for i in range(1, 4):
                weights_times("q", i, xt)
            pe.wait_ge(bgu_in, 16)
            o = claim(("bgt",))
            for c in range(16):
                last = nc.tensor.transpose(o[:, c * NE:(c + 1) * NE], bgu_rows[:, c * 128:(c + 1) * 128],
                                           ident[0:NE, 0:NE])
            last.then_inc(full(("bgt",))[0], 1)

            def tokens_times(kind, j, t, acts):
                w = unit(kind, j).rearrange("p (c n) -> p c n", c=KC)
                t0 = TILES[t][0]
                o = claim((kind, j, t))
                for c in range(KC):
                    last = mm(o[:, 0:256], acts[c][:, t0:t0 + 128], w[:, c, :], start=c == 0, stop=c == KC - 1)
                last.then_inc(full((kind, j, t))[0], 1)

            def samples_times(kind, s, acts, counted=None):
                name = (kind + "s", s)
                o = claim(name)
                for c in range(KC):
                    if counted is not None:
                        pe.wait_ge(counted, c + 1)
                    for side in range(2):
                        w = unit(kind, 2 * s + side).rearrange("p (c n) -> p c n", c=KC)
                        last = mm(o[side * NS:(side + 1) * NS, 0:256], acts[c][:, NP:NT], w[:, c, :],
                                  start=c == 0, stop=c == KC - 1)
                last.then_inc(full(name)[0], 1)

            for j in range(4):
                n = UNIT_NO[("v", j)]
                w = parts(n)[1:]
                split(n, 1)
                for t in range(3):
                    t0 = (0, 128, NT - 128)[t]
                    o = claim(("v", j, t))
                    for c in range(KC):
                        for a, b in THREE:
                            last = mm(o[:, 0:256], xt[a][:, c, t0:t0 + 128], w[b][:, c, :],
                                      start=c == 0 and a + b == 0, stop=c == KC - 1 and a == 1)
                    last.then_inc(full(("v", j, t))[0], 1)

            pe.wait_ge(qk_ready, 4)
            for t, (t0, n) in enumerate(TILES):
                o = claim(("a", t))
                for h in range(HEADS):
                    last = mm(o[0:n, h * n:(h + 1) * n], ke[:, h, t0:t0 + n], qe[:, h, t0:t0 + n], start=True, stop=True)
                last.then_inc(full(("a", t))[0], 1)
            for t, (t0, n) in enumerate(TILES):
                o = claim(("kt", t))
                for h in range(HEADS):
                    last = nc.tensor.transpose(o[0:n, h * 128:(h + 1) * 128], k[:, h, t0:t0 + n], ident)
                last.then_inc(full(("kt", t))[0], 1)
            for h in range(HEADS):
                outs = [claim(("o", h, vc)) for vc in range(2)]
                pe.wait_ge(ss_in[h], 16)

                def old_states(vc):
                    def one(b):
                        s0 = NP + b * L
                        mm(outs[vc][:, s0:s0 + L], ss_st[h % 2][:, b, vc * 128:(vc + 1) * 128],
                           q[:, h, s0:s0 + L], start=b == 0, stop=False, skip_group_check=True)
                    return one
                weights_times("g", 2 * h, xt, between=old_states(0))
                if h == 0:
                    pe.wait_ge(klt_ready, 3)
                    pe.wait_ge(v_ready, 1)
                for half in range(2):
                    o = claim(("kv", h, half))
                    for c2 in range(2):
                        p0 = half * C
                        last = mm(o[:, c2 * DV:(c2 + 1) * DV], klt[p0:p0 + C, c2, h * 128:(h + 1) * 128],
                                  v[p0:p0 + C, c2, h * DV:(h + 1) * DV], start=True, stop=True)
                    last.then_inc(full(("kv", h, half))[0], 1)
                weights_times("g", 2 * h + 1, xt, between=old_states(1))
                if h == 0:
                    pe.wait_ge(at_ready, 3)
                pe.wait_ge(sp_ready, 4 * (h + 1))
                for vc in range(2):
                    o = outs[vc]
                    f0 = h * DV + vc * 128
                    for t, (t0, n) in enumerate(TILES):
                        mm(o[:, t0:t0 + n], v[0:n, t, f0:f0 + 128], at_[0:n, t, h * n:(h + 1) * n],
                           start=False, stop=False, skip_group_check=True)
                    for c in range(1, NP // C):
                        last = mm(o[:, c * C:(c + 1) * C], sp_st[:, h % 2, c - 1, vc * 128:(vc + 1) * 128],
                                  q[:, h, c * C:(c + 1) * C], start=False, stop=c == NP // C - 1,
                                  skip_group_check=True)
                    last.then_inc(full(("o", h, vc))[0], 1)
                pe.wait_ge(klm_ready, h + 1)
                for i in range(4):
                    o = claim(("kvs", h, i))
                    for half in range(2):
                        last = mm(o[:, half * DV:(half + 1) * DV], klm[:, 2 * i + half, :],
                                  v[0:NS, 2, h * DV:(h + 1) * DV], start=True, stop=True)
                    last.then_inc(full(("kvs", h, i))[0], 1)
                weights_times("ga", 2 * h, xt)
                weights_times("ga", 2 * h + 1, xt)
                pe.wait_ge(sq_ready, 2 * h + 2)
                o = claim(("rms", h))
                for vc in range(2):
                    last = mm(o[:, 0:NT], cst("ones"), sq[:, vc, :], start=vc == 0, stop=vc == 1)
                last.then_inc(full(("rms", h))[0], 1)
            for i in range(4):
                weights_times("u", i, xt)
            pe.wait_ge(o_split, 2)
            for i in range(8):
                weights_times("ba", i, o_parts)
            pe.wait_ge(late_in, 48)
            o = claim(("pb",))
            for g in range(4):
                last = nc.tensor.transpose(o[:, g * 120:(g + 1) * 120], spb[:, g * 128:(g + 1) * 128],
                                           ident[0:120, 0:120])
            last.then_inc(full(("pb",))[0], 1)
            pe.wait_ge(u_ready, 4)
            o = claim(("up",))
            for g in range(4):
                last = nc.tensor.transpose(o[0:PBUF, g * 128:(g + 1) * 128], up_pad[:, g, NP:NP + PBUF], ident)
            last.then_inc(full(("up",))[0], 1)
            pe.wait_ge(po_ready, 1)
            o = claim(("us",))
            for g in range(4):
                last = nc.tensor.transpose(o[0:NS, g * 128:(g + 1) * 128], po[:, g, NP:NT], ident)
            last.then_inc(full(("us",))[0], 1)
            for i in range(6):
                weights_times("gb", i, xt)
            for g in range(4):
                pe.wait_ge(po_ready, g + 2)
                o = claim(("grp", g))
                mm(o[:, 0:NT], wgrp[:, g, :], po[:, g, :], start=True, stop=True).then_inc(full(("grp", g))[0], 1)
            for i in range(6, 8):
                weights_times("gb", i, xt)
            pe.wait_ge(pg_ready, 4)
            for i in range(8):
                weights_times("bb", i, pg, chunks=4, per_unit=4)
            def turn_h(t, h_count):
                n = TILES[t][1]
                for half in range(2):
                    pe.wait_ge(h_ready, h_count + half)
                    o = claim(("ht", t, half))
                    for c in range(4):
                        f0 = (4 * half + c) * 128
                        last = nc.tensor.transpose(o[:, c * n:(c + 1) * n], hrow[0:n, t, f0:f0 + 128], ident[0:n, 0:n])
                    last.then_inc(full(("ht", t, half))[0], 1)

            def router(t, ht_count):
                t0, n = TILES[t]
                pe.wait_ge(ht_ready, ht_count)
                o = claim(("lg", t))
                for c in range(KC):
                    last = mm(o[0:n, 0:NE], ot[:, c, t0:t0 + n], wrt[:, c, :], start=c == 0, stop=c == KC - 1)
                last.then_inc(full(("lg", t))[0], 1)

            def ranks(t, mask_count):
                pe.wait_ge(mask_ready, mask_count)
                o = claim(("rk", t))
                before = ORDER[:ORDER.index(t)]
                for s in before:
                    n = TILES[s][1]
                    mm(o[:, 0:NE], cst("ones", p=n), msk[0:n, s, :], start=s == ORDER[0], stop=False)
                n = TILES[t][1]
                mm(o[:, 0:NE], cst("upto", p=n), msk[0:n, t, :], start=not before, stop=True)\
                    .then_inc(full(("rk", t))[0], 1)

            def released(i):
                n = (i + 2) % 8
                pe.wait_ge(bank_free[n], LAST_USE[n])

            def first_gather(tiles, first):
                for c in range(KC):
                    for t in tiles:
                        n = TILES[t][1]
                        last = mm(ex[6 + c // 4][:, (c % 4) * 128:(c % 4 + 1) * 128], hrow[0:n, t, c * 128:(c + 1) * 128],
                                  onehot[0:n, t, :], start=first and t == tiles[0] and c % 4 == 0, stop=not first,
                                  skip_group_check=True)
                return last

            for j in range(4):
                pe.wait_ge(*unit_landed("out", j))
            samples_times("out", 0, ga, counted=merged)
            samples_times("out", 1, ga)
            for j in range(4):
                tokens_times("out", j, 0, ga)
            turn_h(2, 1)
            router(2, 2)
            tokens_times("out", 0, 1, ga)
            turn_h(0, 3)
            tokens_times("out", 1, 1, ga)
            ranks(2, 2)
            router(0, 4)
            tokens_times("out", 2, 1, ga)
            ranks(0, 3)
            tokens_times("out", 3, 1, ga)
            released(6)
            released(7)
            pe.wait_ge(onehot_early, 1)
            first_gather(ORDER[:2], True)
            turn_h(1, 5)
            router(1, 6)
            ranks(1, 4)
            o = claim(("cnt",))
            for t, (t0, n) in enumerate(TILES):
                last = mm(o[0:1, 0:NE], cst("ones", p=n, n=1), msk[0:n, t, :], start=t == 0, stop=t == 2)
            last.then_inc(full(("cnt",))[0], 1)
            def gather(pair_count):
                pe.wait_ge(onehot_ready, pair_count)
                for c in range(KC):
                    for t, (t0, n) in enumerate(TILES):
                        last = mm(ex[6 + c // 4][:, (c % 4) * 128:(c % 4 + 1) * 128], hrow[0:n, t, c * 128:(c + 1) * 128],
                                  onehot[0:n, t, :], start=t == 0, stop=t == 2)
                last.then_inc(gathered, 1)

            def turn_slots(pair_count):
                pe.wait_ge(onehot_w_ready, pair_count)
                for t, (t0, n) in enumerate(TILES):
                    last = nc.tensor.transpose(ex[5][:, t0:t0 + n], onehot_w[0:n, t, :], ident[0:n, 0:n])
                last.then_inc(slots_turned, 1)

            def expert_up(where, half):
                for j in range(UP_UNITS):
                    pos, landing = where(j)
                    pe.wait_ge(*landing)
                    w = slot_view(pos)
                    for i in range(2):
                        for side in range(2):
                            last = mm(ex[i][side * CAP:(side + 1) * CAP, :], xgt[:, j, half * CAP:(half + 1) * CAP],
                                      w[:, i * D + side * 512:i * D + (side + 1) * 512],
                                      start=j == 0, stop=j == UP_UNITS - 1)
                    last.then_inc(up_used, 1)

            def turn_up(idx):
                pe.wait_ge(hg_ready, idx + 1)
                for c in range(4):
                    nc.tensor.transpose(ex[2][:, c * 128:(c + 1) * 128], hg[:, c * 128:(c + 1) * 128], ident)
                pe.wait_ge(hu_ready, idx + 1)
                for c in range(4):
                    last = nc.tensor.transpose(ex[3][:, c * 128:(c + 1) * 128], hu[:, c * 128:(c + 1) * 128], ident)
                last.then_inc(turned, 1)

            def expert_down(idx, where):
                pe.wait_ge(act_ready, idx + 1)
                for j in range(DOWN_UNITS):
                    pos, landing = where(j)
                    pe.wait_ge(*landing)
                    w = slot_view(pos).rearrange("p (c n) -> p c n", c=2)
                    for c in range(2):
                        for side in range(2):
                            last = mm(ex[4][side * CAP:(side + 1) * CAP, :], actt[:, 2 * j + c, :],
                                      w[:, c, side * 512:(side + 1) * 512], start=j == 0 and c == 0,
                                      stop=j == DOWN_UNITS - 1 and c == 1)
                    last.then_inc(down_used, 1)

            def units(is_up, e, m=None):
                def where(j):
                    n = UNIT_SEQ[(is_up, e, j)]
                    return n % SLOTS, landed(n, m)
                return where

            def scatter(pair, blocks):
                pe.wait_ge(res_ready, blocks)
                pe.wait_ge(slot_ready, pair + 1)
                for i in range(6):
                    t, half = i // 2, i % 2
                    t0, n = TILES[t]
                    if i >= 3:
                        pe.wait_ge(added, pair * 6 + i - 2)
                    mm(ex[5 + i % 3][0:n, :], slot_t[:, t0:t0 + n], res[:, half * 512:(half + 1) * 512],
                       start=True, stop=True).then_inc(pieces, 1)

            def pair_of_blocks(p, m=None, first=False, last=False):
                pair = p if m is None else m * 2 + p
                e = 2 * p if m is None else m * 4 + 2 * p
                turn_up(e)
                if not first:
                    scatter(pair - 1, e)
                expert_up(units(True, 2 * p + 1, m), 1)
                turn_slots(pair + 1)
                if last:
                    pe.wait_ge(act_ready, e + 1)
                    turn_up(e + 1)
                else:
                    if not first:
                        pe.wait_ge(added, pair * 6)
                    gather(pair + 2)
                expert_down(e, units(False, 2 * p, m))
                if not last:
                    turn_up(e + 1)
                if not last:
                    pe.wait_ge(xgt_ready, pair + 2)
                    expert_up(units(True, 2 * p + 2, m), 0)
                pe.wait_ge(res_ready, e + 1)
                expert_down(e + 1, units(False, 2 * p + 1, m))

            pe.wait_ge(onehot_ready, 1)
            first_gather(ORDER[2:], False).then_inc(gathered, 1)
            released(0)
            released(1)
            pe.wait_ge(xgt_ready, 1)
            expert_up(units(True, 0), 0)
            pe.wait_ge(soft4_done, 1)
            o = claim(("gwt",))
            for t, (t0, n) in enumerate(TILES):
                last = nc.tensor.transpose(o[0:NE, t0:t0 + n], gw[0:n, t, :], ident[0:n, 0:n])
            last.then_inc(full(("gwt",))[0], 1)
            for i in range(2, 6):
                released(i)
            pe.wait_ge(gwt_ready, 1)
            pe.wait_ge(bgu_in, 32)
            for t, (t0, n) in enumerate(TILES):
                for i in range(2):
                    mm(ex[2 + 2 * t + i][0:n, :], gwt[:, t0:t0 + n], bdn_rows[:, i * 512:(i + 1) * 512],
                       start=True, stop=True).then_inc(yb_full, 1)
            pe.wait_ge(yb_used, 6)
            pair_of_blocks(0, first=True)
            with pe.Fori(0, NE // PERIOD - 1) as loop:
                m = pe.snap(loop)
                pair_of_blocks(1, m)
                pair_of_blocks(2, m)
            pair_of_blocks(NE // 2 - 1, last=True)
            scatter(NE // 2 - 1, NE)
            pe.wait_ge(lists_ready, 1)
            count = pe.value_load(n_later[0:1, 0:1], min_val=0, max_val=RANKS)
            with pe.If(count > 0):
                with pe.Fori(0, count) as loop:
                    b = pe.snap(loop)
                    pe.wait_ge(added, b * 6 + 6 * (NE // 2))
                    gather(b + NE // 2 + 1)
                    turn_slots(b + NE // 2 + 1)
                    pe.wait_ge(xgt_ready, b + NE // 2 + 1)
                    expert_up(lambda j: (j, landed_later(j, b)), 0)
                    turn_up(b + NE)
                    expert_down(b + NE, lambda j: (UP_UNITS + j, landed_later(UP_UNITS + j, b)))
                    scatter(b + NE // 2, b + NE + 1)

        @block.scalar
        def _(act):
            A = nc.scalar.activation
            steps = [0]

            def link(ins):
                steps[0] += 1
                ins.then_inc(act_step, 1)
                act.wait_ge(act_step, steps[0])

            def high_part(n, half):
                act.wait_ge(filled[n % RING], 16 * (n // RING + 1))
                raw, hi, _ = parts(n)
                A(half_of(hi, half), half_of(raw, half), ACT.Copy).then_inc(high_ready, 1)

            def high_after(p):
                act.wait_ge(*full(p))
                for n, half in AFTER.get(p, ()):
                    high_part(n, half)

            for c in range(KC):
                act.wait_ge(*full(("xt", c)))
                A(xt[0][:, c, :], bank(("xt", c))[:, 0:NT], ACT.Copy).then_inc(xt_high, 1)
                if c == 3:
                    high_part(0, 0)
            high_part(0, 1)
            act.wait_ge(small_in, 16 * 6)
            A(wlr_parts[0].rearrange("p c (r n) -> p c r n", n=16), wlr.unsqueeze(2).broadcast_to([128, KC, 8, 16]),
              ACT.Copy).then_inc(wlr_high, 1)
            high_part(1, 0)
            high_part(1, 1)
            for i in range(4):
                act.wait_ge(*full(("k", i)))
                A(k[:, i, :], bank(("k", i))[:, 0:NT], ACT.Copy).then_inc(freed(("k", i)), 1)
                high_after(("k", i))
            act.wait_ge(*full(("lr",)))
            A(lrt, bank(("lr",))[0:16, 0:NT], ACT.Copy).then_inc(lr_ready, 1)
            act.wait_ge(lr_ready, 1)
            act.sem_inc(freed(("lr",)), 1)
            for i in range(4):
                act.wait_ge(*full(("q", i)))
                A(q[:, i, :], bank(("q", i))[:, 0:NT], ACT.Copy, scale=float(DK) ** -0.5)\
                    .then_inc(freed(("q", i)), 1)
                high_after(("q", i))
            act.sem_inc(qk_in, 1)
            act.wait_ge(z_ready, 1)
            link(A(ee[:, :, :], ee[:, :, :], ACT.Exp, scale=-1.0))
            A(ee[:, :, :], ee[:, :, :], ACT.Ln, bias=1.0).then_inc(soft_ready, 1)
            act.wait_ge(xt_ready, KC)

            def keep_v(j):
                for t, (t0, n) in enumerate(TILES):
                    act.wait_ge(*full(("v", j, t)))
                    A(v[0:n, t, j * 256:(j + 1) * 256], bank(("v", j, t))[128 - n:, 0:256], ACT.Copy)\
                        .then_inc(freed(("v", j, t)), 1)
                high_after(("v", j, 2))
            keep_v(0)
            act.wait_ge(diff_ready, 1)
            A(qe[:, :, :], bb[:, :, :], ACT.Exp, scale=1.0 / 16).then_inc(exp_ready, 1)
            A(ke[:, :, :], bb[:, :, :], ACT.Exp, scale=-1.0 / 16).then_inc(exp_ready, 1)
            A(eb[:, :, :], ee[:, :, :], ACT.Exp, scale=1.0 / 16).then_inc(exp_ready, 1)
            A(bl[:, :, :], bl[:, :, :], ACT.Exp, scale=1.0 / 16).then_inc(exp_ready, 1)
            for j in range(1, 4):
                keep_v(j)
            for t, (t0, n) in enumerate(TILES):
                act.wait_ge(*full(("kt", t)))
                A(klt[0:n, t, :], bank(("kt", t))[0:n, :], ACT.Copy).then_inc(klt_ready, 1)
            act.wait_ge(klt_ready, 3)
            for t in range(3):
                act.sem_inc(freed(("kt", t)), 1)
            for name in PRODUCTS[NO[("v", 0, 0)]:NO[("v", 3, 2)] + 1]:
                act.wait_ge(freed(name), NO[name] // 8 + 1)
            act.sem_inc(v_ready, 1)
            for h in range(HEADS):
                for i in (2 * h, 2 * h + 1):
                    act.wait_ge(*full(("g", i)))
                    A(gs[:, i, :], bank(("g", i))[:, 0:NT], ACT.Sigmoid).then_inc(sig_ready, 1)
                    high_after(("g", i))
                if h:
                    act.wait_ge(*full(("rms", h - 1)))
                for vc in range(2):
                    act.wait_ge(*full(("o", h, vc)))
                    A(sq[:, vc, :], bank(("o", h, vc))[:, 0:NT], ACT.Square).then_inc(sq_ready, 1)
                    A(ot[:, 2 * h + vc, :], bank(("o", h, vc))[:, 0:NT], ACT.Copy).then_inc(freed(("o", h, vc)), 1)
                for i in (2 * h, 2 * h + 1):
                    act.wait_ge(*full(("ga", i)))
                    A(ga[i], bank(("ga", i))[:, 0:NT], ACT.Sigmoid, bias=cols[:, i:i + 1])\
                        .then_inc(freed(("ga", i)), 1)
                    high_after(("ga", i))
                act.wait_ge(*full(("rms", h)))
                if h:
                    act.wait_ge(ot_ready, h)
                A(rms, bank(("rms", h))[:, 0:NT], ACT.Sqrt, bias=eps_rms, scale=1.0 / DV)\
                    .then_inc(freed(("rms", h)), 1)
            act.wait_ge(freed(("ga", 7)), NO[("ga", 7)] // 8 + 1)
            act.sem_inc(ga_ready, 1)
            act.wait_ge(ot_ready, HEADS)
            for half in range(2):
                A(o_parts[0][:, 4 * half:4 * half + 4, :], ot[:, 4 * half:4 * half + 4, :], ACT.Copy).then_inc(o_high, 1)
            act.wait_ge(pads_zero, 1)
            for i in range(4):
                act.wait_ge(*full(("u", i)))
                A(up_pad[:, i, PBUF:], bank(("u", i))[:, 0:NP], ACT.Copy)
                A(us_pad[:, i, :, PBUF:], bank(("u", i))[:, NP:NT].rearrange("p (b s) -> p b s", s=L), ACT.Copy)\
                    .then_inc(u_ready, 1)
                high_after(("u", i))
            act.wait_ge(u_ready, 4)
            for i in range(4):
                act.sem_inc(freed(("u", i)), 1)
            for i in range(8):
                high_after(("ba", i))
            for name, dst, n in ((("up",), pool_out_p, PBUF), (("us",), pool_out_s, NS)):
                act.wait_ge(*full(name))
                A(dst, bank(name)[0:n, :], ACT.Copy).then_inc(pool_out_ready, 1)
            act.wait_ge(pool_out_ready, 2)
            for name in (("up",), ("us",)):
                act.sem_inc(freed(name), 1)
            def keep_gb(i):
                act.wait_ge(*full(("gb", i)))
                A(gb[:, i, :], bank(("gb", i))[:, 0:NT], ACT.Sigmoid, bias=cols[:, 8 + i:9 + i])\
                    .then_inc(freed(("gb", i)), 1)
                high_after(("gb", i))

            for i in range(6):
                keep_gb(i)
            for g in range(4):
                act.wait_ge(*full(("grp", g)))
                A(pg[0][:, g, :], bank(("grp", g))[:, 0:NT], ACT.Copy, scale=cols[:, 22 + g:23 + g])\
                    .then_inc(pg_high, 1)
            for i in range(6, 8):
                keep_gb(i)
            act.wait_ge(freed(("gb", 7)), NO[("gb", 7)] // 8 + 1)
            act.sem_inc(gb_ready, 1)

            def turned_h(t):
                t0, n = TILES[t]
                for half in range(2):
                    act.wait_ge(*full(("ht", t, half)))
                    A(ot[:, 4 * half:4 * half + 4, t0:t0 + n],
                      bank(("ht", t, half))[:, 0:4 * n].rearrange("p (c n) -> p c n", n=n), ACT.Copy)\
                        .then_inc(ht_ready, 1)

            for i, t in enumerate(ORDER):
                n = TILES[t][1]
                act.wait_ge(var_ready, i + 1)
                A(rstd[0:n], mv[0:n, 1:2], ACT.Sqrt, bias=eps_ln[0:n]).then_inc(std_ready, 1)
                turned_h(t)
                act.wait_ge(ht_ready, 2 * i + 2)
                for half in range(2):
                    act.sem_inc(freed(("ht", t, half)), 1)

            def keep_gathered(count):
                act.wait_ge(gathered, count)
                A(xgt[:, 0:4, :], ex[6][:, :].rearrange("p (c s) -> p c s", s=128), ACT.Copy)
                A(xgt[:, 4:8, :], ex[7][:, :].rearrange("p (c s) -> p c s", s=128), ACT.Copy).then_inc(xgt_ready, 1)

            def keep_slots(count):
                act.wait_ge(slots_turned, count)
                A(slot_t, ex[5][:, 0:NT], ACT.Copy).then_inc(slot_ready, 1)

            def keep_gate(idx):
                act.wait_ge(up_used, (idx + 1) * UP_UNITS)
                A(hg, ex[0][:, :], ACT.Copy).then_inc(hg_ready, 1)

            def swish(idx):
                act.wait_ge(gate_ready, idx + 1)
                A(sg[:, :, :], g1[:, :, :], ACT.Sigmoid, scale=GLU_ALPHA).then_inc(swish_ready, 1)

            def keep_output(idx, half):
                act.wait_ge(down_used, (idx + 1) * DOWN_UNITS)
                for side in range(2):
                    last = A(res[half * CAP:(half + 1) * CAP, side * 512:(side + 1) * 512],
                             ex[4][side * CAP:(side + 1) * CAP, :], ACT.Copy)
                last.then_inc(res_ready, 1)

            def pair_of_blocks(pair, last=False):
                e = pair * 2
                swish(e)
                keep_gate(e + 1)
                keep_slots(pair + 1)
                if not last:
                    keep_gathered(pair + 2)
                if last:
                    swish(e + 1)
                keep_output(e, 0)
                if not last:
                    swish(e + 1)
                    keep_gate(e + 2)
                keep_output(e + 1, 1)

            for i, t in enumerate(ORDER):
                n = TILES[t][1]
                act.wait_ge(max_ready, i + 1)
                A(sm[0:n, t, :], lg[0:n, t, 0:4], ACT.Exp).then_inc(soft4_ready, 1)
            keep_gathered(1)
            keep_gate(0)
            pair_of_blocks(0)
            with act.Fori(1, NE // 2 - 1) as pair:
                pair_of_blocks(act.snap(pair))
            pair_of_blocks(NE // 2 - 1, last=True)
            act.wait_ge(lists_ready, 1)
            count = act.value_load(n_later[0:1, 0:1], min_val=0, max_val=RANKS)
            with act.If(count > 0):
                with act.Fori(0, count) as loop:
                    b = act.snap(loop)
                    keep_gathered(b + NE // 2 + 1)
                    keep_slots(b + NE // 2 + 1)
                    keep_gate(b + NE)
                    swish(b + NE)
                    keep_output(b + NE, 0)
            for t, (t0, n) in enumerate(TILES):
                act.wait_ge(var_ready, t + 4)
                A(rstd2[0:n, t:t + 1], mv[0:n, 1:2], ACT.Sqrt, bias=eps_ln[0:n]).then_inc(std_ready, 1)
                if t < 2:
                    act.wait_ge(y_centred, t + 1)
                    A(y[:, t, :], y[:, t, :], ACT.Copy, scale=rstd2[:, t:t + 1]).then_inc(y_scaled, 1)

        @block.vector
        def _(dve):
            V = nc.vector
            steps = [0]

            def link(ins):
                steps[0] += 1
                ins.then_inc(dve_step, 1)
                dve.wait_ge(dve_step, steps[0])

            def low_part(n, half):
                dve.wait_ge(high_ready, 2 * n + half + 1)
                raw, hi, lo = parts(n)
                V.tensor_tensor(half_of(lo, half), half_of(raw, half), half_of(hi, half), ALU.subtract)\
                    .then_inc(split_ready, 1)

            def low_after(p):
                for n, half in AFTER.get(p, ()):
                    low_part(n, half)

            def xt_banks_free(chunks):
                dve.wait_ge(xt_ready, chunks[-1] + 1)
                for c in chunks:
                    dve.sem_inc(freed(("xt", c)), 1)

            V.memset(eps_rms, RMS_EPS)
            V.memset(eps_ln, LN_EPS)
            for c in range(KC):
                dve.wait_ge(*full(("xt", c)))
                dve.wait_ge(xt_high, c + 1)
                V.tensor_tensor(xt[1][:, c, :], bank(("xt", c))[:, 0:NT], xt[0][:, c, :], ALU.subtract)\
                    .then_inc(xt_ready, 1)
                if c == 3:
                    low_part(0, 0)
                    xt_banks_free(range(4))
            xt_banks_free(range(4, KC))
            low_part(0, 1)
            dve.wait_ge(wlr_high, 1)
            V.tensor_tensor(wlr_parts[1].rearrange("p c (r n) -> p c r n", n=16),
                            wlr.unsqueeze(2).broadcast_to([128, KC, 8, 16]),
                            wlr_parts[0].rearrange("p c (r n) -> p c r n", n=16), ALU.subtract).then_inc(wlr_ready, 1)
            low_part(1, 0)
            low_part(1, 1)
            for i in range(4):
                low_after(("k", i))
            dve.wait_ge(*full(("cols",)))
            V.tensor_copy(cols, bank(("cols",))[:, 0:26]).then_inc(freed(("cols",)), 1)
            dve.wait_ge(freed(("cols",)), NO[("cols",)] // 8 + 1)
            low_after(("q", 0))
            for i in range(4):
                dve.wait_ge(*full(("gk", i)))
                V.tensor_scalar(bb[:, i, :], bank(("gk", i))[:, 0:NT], cols[:, 16 + i:17 + i], None, ALU.add)\
                    .then_inc(freed(("gk", i)), 1)
            for i in range(4):
                dve.wait_ge(freed(("gk", i)), NO[("gk", i)] // 8 + 1)
            V.scalar_tensor_tensor(ee[:, :, :], bb[:, :, :], -1.0, bb[:, :, :], ALU.mult, ALU.max).then_inc(z_ready, 1)
            for i in range(1, 4):
                low_after(("q", i))
            dve.wait_ge(soft_ready, 1)
            link(V.scalar_tensor_tensor(bb[:, :, :], bb[:, :, :], 0.0, ee[:, :, :], ALU.min, ALU.subtract))
            dve.wait_ge(starts_in, 32)
            link(V.tensor_tensor_scan(reg(EE, HEADS * NT), starts, reg(BB, HEADS * NT), 0.0, ALU.mult, ALU.add))
            for t, n in ((0, C), (1, L)):
                cum, dif, rest = by_chunk(ee, t), by_chunk(bb, t), by_chunk(bl, t)
                shape = list(cum.shape)
                V.tensor_tensor(dif, cum, cum[:, :, :, n // 2:n // 2 + 1].broadcast_to(shape), ALU.subtract)
                last = V.tensor_tensor(rest, cum[:, :, :, n - 1:n].broadcast_to(shape), cum, ALU.subtract)
            last.then_inc(diff_ready, 1)
            dve.wait_ge(*full(("bgt",)))
            V.tensor_copy(reg(BGU, 512), bank(("bgt",))[:, :]).then_inc(freed(("bgt",)), 1)
            low_after(("v", 0, 2))
            dve.wait_ge(exp_ready, 4)
            dve.wait_ge(qk_in, 1)
            V.tensor_tensor(qe[:, :, :], qe[:, :, :], q[:, :, :], ALU.mult).then_inc(qk_ready, 1)
            V.tensor_tensor(ke[:, :, :], ke[:, :, :], k[:, :, :], ALU.mult).then_inc(qk_ready, 1)
            low_after(("v", 1, 2))
            V.tensor_tensor(q[:, :, :], q[:, :, :], eb[:, :, :], ALU.mult).then_inc(qk_ready, 1)
            V.tensor_tensor(k[:, :, :], k[:, :, :], bl[:, :, :], ALU.mult).then_inc(qk_ready, 1)
            V.tensor_copy(dec[:, :, 0:4].rearrange("p h (c a) -> p h c a", a=1), by_chunk(eb, 0)[:, :, :, C - 1:C])
            link(V.tensor_copy(dec[:, :, 4:12].rearrange("p h (c a) -> p h c a", a=1), by_chunk(eb, 1)[:, :, :, L - 1:L]))
            link(V.memset(reg(BB, 1536), 0.0))
            low_after(("v", 2, 2))
            for t, (t0, n) in enumerate(TILES):
                dve.wait_ge(*full(("a", t)))
                m = cst("pmask" if t < 2 else "smask", p=n).bitcast(i32)
                for h in range(HEADS):
                    last = V.copy_predicated(at_[0:n, t, h * n:(h + 1) * n], m, bank(("a", t))[0:n, h * n:(h + 1) * n])
                last.then_inc(at_ready, 1)
            dve.wait_ge(at_ready, 3)
            for t in range(3):
                dve.sem_inc(freed(("a", t)), 1)
            dve.wait_ge(klt_ready, 3)
            dve.wait_ge(*full(("kt", 2)))

            def silu(i):
                dve.wait_ge(*full(("g", i)))
                dve.wait_ge(sig_ready, i + 1)
                V.tensor_tensor(gs[:, i, :], gs[:, i, :], bank(("g", i))[:, 0:NT], ALU.mult)\
                    .then_inc(freed(("g", i)), 1)
                low_after(("g", i))

            for h in range(HEADS):
                if h:
                    dve.wait_ge(*full(("kvs", h - 1, 3)))
                V.tensor_tensor(klm, klt[0:NS, 2, h * 128:(h + 1) * 128].unsqueeze(1).broadcast_to([NS, B, DK]),
                                cst("bmask", p=NS).unsqueeze(2).broadcast_to([NS, B, DK]), ALU.mult)\
                    .then_inc(klm_ready, 1)
                if h == 0:
                    low_after(("v", 3, 2))
                silu(2 * h)
                if h >= 2:
                    dve.wait_ge(stored_p, 16 * (h - 1))
                for c in range(4):
                    name = ("kv", h, c % 2)
                    src = bank(name)[:, (c // 2) * DV:(c // 2 + 1) * DV]
                    dve.wait_ge(*full(name))
                    if c == 0:
                        V.tensor_copy(sp_st[:, h % 2, 0, :], src).then_inc(sp_ready, 1)
                    else:
                        dve.wait_ge(sp_ready, 4 * h + c)
                        V.scalar_tensor_tensor(sp_st[:, h % 2, c, :], sp_st[:, h % 2, c - 1, :], dec[:, h, c:c + 1],
                                               src, ALU.mult, ALU.add).then_inc(sp_ready, 1)
                dve.wait_ge(sp_ready, 4 * h + 4)
                dve.sem_inc(freed(("kv", h, 0)), 1)
                dve.sem_inc(freed(("kv", h, 1)), 1)
                silu(2 * h + 1)
                dve.wait_ge(*full(("kvs", h, 3)))
                for b in range(B):
                    name = ("kvs", h, b // 2)
                    ins = V.scalar_tensor_tensor(ss_st[h % 2][:, b, :], ss_st[h % 2][:, b, :], dec[:, h, 4 + b:5 + b],
                                                 bank(name)[:, (b % 2) * DV:(b % 2 + 1) * DV], ALU.mult, ALU.add)
                    if b % 2:
                        ins.then_inc(freed(name), 1)
                for i in range(4):
                    name = ("kvs", h, i)
                    dve.wait_ge(freed(name), NO[name] // 8 + 1)
                dve.sem_inc(ss_ready, 1)
                for i in (2 * h, 2 * h + 1):
                    low_after(("ga", i))
                dve.wait_ge(freed(("rms", h)), NO[("rms", h)] // 8 + 1)
                link(V.reciprocal(rms, rms))
                for vc in range(2):
                    dve.wait_ge(freed(("o", h, vc)), NO[("o", h, vc)] // 8 + 1)
                    i = 2 * h + vc
                    dve.wait_ge(freed(("g", i)), NO[("g", i)] // 8 + 1)
                    last = V.scalar_tensor_tensor(ot[:, i, :], ot[:, i, :], cols[:, 20 + vc:21 + vc], rms,
                                                  ALU.mult, ALU.mult)
                link(last)
                V.tensor_tensor(ot[:, 2 * h:2 * h + 2, :], ot[:, 2 * h:2 * h + 2, :], gs[:, 2 * h:2 * h + 2, :],
                                ALU.mult).then_inc(ot_ready, 1)
            V.memset(up_pad[:, :, 0:PBUF], 0.0).then_inc(pads_zero, 1)
            for half in range(2):
                dve.wait_ge(o_high, half + 1)
                V.tensor_tensor(o_parts[1][:, 4 * half:4 * half + 4, :], ot[:, 4 * half:4 * half + 4, :],
                                o_parts[0][:, 4 * half:4 * half + 4, :], ALU.subtract).then_inc(o_split, 1)
            for i in range(4):
                low_after(("u", i))
            dve.wait_ge(u_ready, 4)
            for g in range(4):
                last = V.tensor_copy(po[:, g, NP:NT].rearrange("p (b s) -> p b s", s=L), us_pad[:, g, :, PBUF:])
            last.then_inc(po_ready, 1)
            dve.wait_ge(ga_ready, 1)
            for i in range(8):
                dve.wait_ge(*full(("ba", i)))
                V.tensor_tensor(ga[i], ga[i], bank(("ba", i))[:, 0:NT], ALU.mult)\
                    .then_inc(freed(("ba", i)), 1)
                low_after(("ba", i))
            dve.wait_ge(*full(("pb",)))
            V.tensor_copy(us_pad[:, :, :, 0:PBUF].rearrange("p g b r -> p (g b) r"),
                          bank(("pb",))[:, 0:480].rearrange("p (g r) -> p g r", r=PBUF)).then_inc(freed(("pb",)), 1)
            dve.wait_ge(u_ready, 4)
            dve.wait_ge(freed(("pb",)), NO[("pb",)] // 8 + 1)
            dve.wait_ge(*full(("us",)))
            win = []
            for at in (SS + 512, SS + 512 + (PBUF + NP) + B * (PBUF + L)):
                ws = reg(at + PBUF + NP, B * (PBUF + L), B)
                win.append((reg(at, PBUF + NP), ws))
            for g in range(4):
                cp, cs = up_pad[:, g, :], us_pad[:, g, :, :]
                lo = 0
                for s in range(g + 1):
                    step = 2 ** s
                    lo += step
                    np_, ns_ = win[s % 2]
                    V.tensor_tensor(np_[:, lo:], cp[:, lo:], cp[:, lo - step:PBUF + NP - step], ALU.add)
                    link(V.tensor_tensor(ns_[:, :, lo:], cs[:, :, lo:], cs[:, :, lo - step:PBUF + L - step], ALU.add))
                    cp, cs = np_, ns_
                w = 2.0 ** -(g + 1)
                at = CST["rcnt"][0] + CONST + 16 * g
                link(V.tensor_tensor(win[(g + 1) % 2][0][:, 0:16], cp[:, PBUF:PBUF + 16], ar[:, at:at + 16], ALU.mult))
                V.tensor_tensor(po[:, g, 0:16], win[(g + 1) % 2][0][:, 0:16], up_pad[:, g, PBUF:PBUF + 16], ALU.subtract)
                V.scalar_tensor_tensor(po[:, g, 16:NP], cp[:, PBUF + 16:], w, up_pad[:, g, PBUF + 16:], ALU.mult,
                                       ALU.subtract)
                V.scalar_tensor_tensor(po[:, g, NP:NT].rearrange("p (b s) -> p b s", s=L), cs[:, :, PBUF:], w,
                                       us_pad[:, g, :, PBUF:], ALU.mult, ALU.subtract).then_inc(po_ready, 1)
                dve.wait_ge(po_ready, g + 2)
                low_after(("gb", g))
            for i in range(4, 6):
                low_after(("gb", i))
            for g in range(4):
                dve.wait_ge(*full(("grp", g)))
                dve.wait_ge(pg_high, g + 1)
                V.scalar_tensor_tensor(pg[1][:, g, :], bank(("grp", g))[:, 0:NT], cols[:, 22 + g:23 + g], pg[0][:, g, :],
                                       ALU.mult, ALU.subtract).then_inc(pg_ready, 1)
            dve.wait_ge(pg_ready, 4)
            for g in range(4):
                dve.sem_inc(freed(("grp", g)), 1)
            for i in range(6, 8):
                low_after(("gb", i))
            dve.wait_ge(gb_ready, 1)
            for i in range(8):
                dve.wait_ge(*full(("bb", i)))
                ins = V.tensor_tensor(gb[:, i, :], gb[:, i, :], bank(("bb", i))[:, 0:NT], ALU.mult)
                ins.then_inc(freed(("bb", i)), 1)
                dve.wait_ge(freed(("bb", i)), NO[("bb", i)] // 8 + 1)
                V.tensor_tensor(ga[i], ga[i], gb[:, i, :], ALU.add).then_inc(merged, 1)
            dve.wait_ge(x_again, 48)
            normed = [0]

            def stats(src, n, half):
                V.bn_stats(st6[0:n, half, :], src[:, half * 512:(half + 1) * 512]).then_inc(ln_step, 1)
                normed[0] += 1

            def scaled(dst, n, scale, bias, done):
                for half in range(2):
                    d = dst[:, half * 512:(half + 1) * 512]
                    V.scalar_tensor_tensor(d, d, scale, bias[0:n, half * 512:(half + 1) * 512],
                                           ALU.mult, ALU.add).then_inc(done, 1)

            def centred(src, dst, n, count, gain, scale):
                dve.wait_ge(ln_step, normed[0])
                V.bn_aggr(mv[0:n], st6[0:n, :, :]).then_inc(var_ready, 1)
                dve.wait_ge(var_ready, count)
                link(V.scalar_tensor_tensor(dst, src, mv[0:n, 0:1], gain[0:n], ALU.subtract, ALU.mult))
                dve.wait_ge(std_ready, count)
                return V.reciprocal(scale, scale)

            def route(i, t):
                n = TILES[t][1]
                dve.wait_ge(*full(("lg", t)))
                link(V.tensor_tensor(lg[0:n, t, :], bank(("lg", t))[0:n, 0:NE], brt[0:n], ALU.add))
                link(V.max(mx[0:n], lg[0:n, t, :]))
                V.max_index(top_idx[0:n, :], mx[0:n], lg[0:n, t, :]).then_inc(freed(("lg", t)), 1)
                dve.wait_ge(freed(("lg", t)), NO[("lg", t)] // 8 + 1)
                link(V.tensor_copy(idxf[0:n], top_idx[0:n, :]))
                link(V.tensor_tensor(oh[0:n, t, :, :], cst("iota32", p=n).unsqueeze(1).broadcast_to([n, TOPK, NE]),
                                     idxf[0:n, 0:TOPK].unsqueeze(2).broadcast_to([n, TOPK, NE]), ALU.is_equal))
                V.tensor_reduce(msk[0:n, t, :], oh[0:n, t, :, :].rearrange("p i e -> p e i"), mybir.AxisListType.X,
                                ALU.add).then_inc(mask_ready, 1)
                V.tensor_scalar(lg[0:n, t, 0:TOPK], mx[0:n, 0:TOPK], mx[0:n, 0:1], None, ALU.subtract)\
                    .then_inc(max_ready, 1)
                dve.wait_ge(max_ready, i + 1)
                dve.wait_ge(mask_ready, i + 2)

            def first_onehot(t):
                n = TILES[t][1]
                dve.wait_ge(*full(("rk", t)))
                V.tensor_tensor(rank[:, t, 0:NE], bank(("rk", t))[:, 0:NE], msk[:, t, :], ALU.mult)\
                    .then_inc(freed(("rk", t)), 1)
                dve.wait_ge(freed(("rk", t)), NO[("rk", t)] // 8 + 1)
                for e in range(2):
                    last = V.tensor_scalar(onehot[0:n, t, e * CAP:(e + 1) * CAP], cst("iota64", p=n),
                                           rank[0:n, t, e:e + 1], None, ALU.is_equal)
                return last

            dve.wait_ge(ln1_in, 32)
            for s in range(2):
                dve.wait_ge(*full(("outs", s)))
                for side in range(2):
                    j = 2 * s + side
                    part = xr[0:NS, 2, j * 256:(j + 1) * 256]
                    last = V.scalar_tensor_tensor(part, part, ALPHA, bank(("outs", s))[side * NS:(side + 1) * NS, 0:256],
                                                  ALU.mult, ALU.add)
                last.then_inc(freed(("outs", s)), 1)
                dve.wait_ge(freed(("outs", s)), NO[("outs", s)] // 8 + 1)
                stats(xr[0:NS, 2, :], NS, s)
            link(centred(xr[0:NS, 2, :], hrow[0:NS, 2, :], NS, 1, ln1[0], rstd[0:NS]))
            scaled(hrow[0:NS, 2, :], NS, rstd[0:NS], ln1[1], h_ready)
            for t in range(2):
                for j in range(4):
                    dve.wait_ge(*full(("out", j, t)))
                    part = xr[:, t, j * 256:(j + 1) * 256]
                    V.scalar_tensor_tensor(part, part, ALPHA, bank(("out", j, t))[:, 0:256], ALU.mult, ALU.add)\
                        .then_inc(freed(("out", j, t)), 1)
                    dve.wait_ge(freed(("out", j, t)), NO[("out", j, t)] // 8 + 1)
                    if j % 2:
                        stats(xr[:, t, :], 128, j // 2)
                    if t == 0:
                        continue
                    if j == 0:
                        V.memset(msk[NS:, 2, :], 0.0).then_inc(mask_ready, 1)
                        route(0, 2)
                    elif j == 1:
                        first_onehot(2)
                        route(1, 0)
                    elif j == 2:
                        first_onehot(0).then_inc(onehot_early, 1)
                link(centred(xr[:, t, :], hrow[:, t, :], 128, t + 2, ln1[0], rstd))
                scaled(hrow[:, t, :], 128, rstd, ln1[1], h_ready)
            dve.wait_ge(h_ready, 6)
            route(2, 1)
            first_onehot(1).then_inc(onehot_ready, 1)

            def make_onehot(half, col):
                for t, (t0, n) in enumerate(TILES):
                    last = V.tensor_scalar(onehot[0:n, t, half * CAP:(half + 1) * CAP], cst("iota64", p=n),
                                           rank[0:n, t, ds(col, 1)], None, ALU.is_equal)
                return last

            def make_onehot_w(half, col, e):
                for t, (t0, n) in enumerate(TILES):
                    last = V.tensor_scalar(onehot_w[0:n, t, half * CAP:(half + 1) * CAP], cst("iota64", p=n),
                                           rank[0:n, t, ds(col, 1)], gw[0:n, t, ds(e, 1)], ALU.is_equal, ALU.mult)
                return last

            def keep_up(idx):
                dve.wait_ge(up_used, (idx + 1) * UP_UNITS)
                V.tensor_copy(hu, ex[1][:, :]).then_inc(hu_ready, 1)

            def gated(idx, e, base, actt_read=None):
                dve.wait_ge(turned, idx + 1)
                for i, dst in ((0, g1), (1, u1)):
                    bias = bgu[:, 8 * i:8 * i + 8, ds(e, 1)].rearrange("p (h c) a -> p h c a", h=2)
                    V.tensor_tensor(dst.rearrange("p (h c) s -> p h c s", h=2),
                                    ex[2 + i][:, :].rearrange("p (c h s) -> p h c s", h=2, s=CAP),
                                    bias.broadcast_to([128, 2, 4, CAP]), ALU.add).then_inc(blk, 1)
                dve.wait_ge(blk, base + 1)
                V.tensor_scalar(g1[:, :, :], g1[:, :, :], LIMIT, None, ALU.min).then_inc(gate_ready, 1)
                dve.wait_ge(blk, base + 2)
                V.tensor_scalar(u1[:, :, :], u1[:, :, :], LIMIT, -LIMIT, ALU.min, ALU.max).then_inc(blk, 1)
                dve.wait_ge(blk, base + 3)
                dve.wait_ge(gate_ready, idx + 1)
                V.scalar_tensor_tensor(u1[:, :, :], u1[:, :, :], 1.0, g1[:, :, :], ALU.add, ALU.mult).then_inc(blk, 1)
                dve.wait_ge(blk, base + 4)
                dve.wait_ge(swish_ready, idx + 1)
                if actt_read is not None:
                    dve.wait_ge(down_used, actt_read)
                V.tensor_tensor(actt[:, :, :], u1[:, :, :], sg[:, :, :], ALU.mult).then_inc(act_ready, 1)

            def add_pieces(pair):
                for i in range(6):
                    t, half = i // 2, i % 2
                    n = TILES[t][1]
                    dve.wait_ge(pieces, pair * 6 + i + 1)
                    part = y[0:n, t, half * 512:(half + 1) * 512]
                    V.tensor_tensor(part, part, ex[5 + i % 3][0:n, :], ALU.add).then_inc(added, 1)

            def pair_of_blocks(pair, first=False, last=False):
                e = pair * 2
                gated(e, e, e * 4)
                if not first:
                    add_pieces(pair - 1)
                    dve.wait_ge(slots_turned, pair)
                make_onehot_w(0, e, e)
                make_onehot_w(1, e + 1, e + 1).then_inc(onehot_w_ready, 1)
                if not last:
                    dve.wait_ge(gathered, pair + 1)
                    make_onehot(0, e + 2)
                    make_onehot(1, e + 3).then_inc(onehot_ready, 1)
                keep_up(e + 1)
                gated(e + 1, e + 1, e * 4 + 4, actt_read=(e + 1) * DOWN_UNITS if last else None)
                if not last:
                    keep_up(e + 2)

            for p in range(1, PASSES):
                last = V.tensor_scalar(rank[:, :, p * NE:(p + 1) * NE], rank[:, :, 0:NE], -float(CAP * p), None, ALU.add)
            link(last)
            dve.wait_ge(soft4_ready, 3)
            for t, (t0, n) in enumerate(TILES):
                last = V.reduce_sum(rsum[0:n, t:t + 1], sm[0:n, t, :], mybir.AxisListType.X)
            link(last)
            for t, (t0, n) in enumerate(TILES):
                last = V.reciprocal(rsum[0:n, t:t + 1], rsum[0:n, t:t + 1])
            link(last)
            for t, (t0, n) in enumerate(TILES):
                last = V.tensor_scalar(sm[0:n, t, :], sm[0:n, t, :], rsum[0:n, t:t + 1], None, ALU.mult)
            link(last)
            for t, (t0, n) in enumerate(TILES):
                last = V.tensor_tensor(oh[0:n, t, :, :], oh[0:n, t, :, :],
                                       sm[0:n, t, :].unsqueeze(2).broadcast_to([n, TOPK, NE]), ALU.mult)
            link(last)
            for t, (t0, n) in enumerate(TILES):
                last = V.tensor_reduce(gw[0:n, t, :], oh[0:n, t, :, :].rearrange("p i e -> p e i"),
                                       mybir.AxisListType.X, ALU.add)
            link(last)
            dve.sem_inc(soft4_done, 1)
            dve.wait_ge(*full(("cnt",)))
            dve.wait_ge(late_in, 16 * (4 + B))
            cnt4 = bank(("cnt",))[0:1, 0:NE].unsqueeze(1).broadcast_to([1, PASSES - 1, NE])
            link(V.tensor_tensor(found[:, 0:NID].rearrange("p (a e) -> p a e", e=NE), cnt4,
                                 lists[:, NID:2 * NID].rearrange("p (a e) -> p a e", e=NE), ALU.is_gt))
            link(V.reduce_sum(low[:, 0:1], found[:, 0:NID], mybir.AxisListType.X))
            V.tensor_copy(n_later[0:1, 0:1], low[:, 0:1])
            link(V.tensor_tensor(found[:, 0:NID], found[:, 0:NID], lists[:, 0:NID], ALU.mult))
            for r in range(RANKS // 8):
                src = found[:, (r % 2) * NID:(r % 2 + 1) * NID]
                dst = found[:, (1 - r % 2) * NID:(2 - r % 2) * NID]
                link(V.max(top24[:, 8 * r:8 * r + 8], src))
                if r < RANKS // 8 - 1:
                    link(V.match_replace(dst, top24[:, 8 * r:8 * r + 8], src, 0.0))
            link(V.tensor_copy(later[0:1, 0, :], top24))
            V.tensor_scalar(later[0:1, 1, :], later[0:1, 0, :], NE - 1, None, ALU.bitwise_and).then_inc(lists_ready, 1)
            dve.wait_ge(lists_ready, 1)
            dve.sem_inc(freed(("cnt",)), 1)

            dve.wait_ge(*full(("gwt",)))
            V.tensor_copy(gwt, bank(("gwt",))[0:NE, 0:NT]).then_inc(gwt_ready, 1)
            dve.wait_ge(gwt_ready, 1)
            dve.sem_inc(freed(("gwt",)), 1)

            keep_up(0)
            for t, (t0, n) in enumerate(TILES):
                for i in range(2):
                    dve.wait_ge(yb_full, 2 * t + i + 1)
                    V.scalar_tensor_tensor(y[0:n, t, i * 512:(i + 1) * 512], hrow[0:n, t, i * 512:(i + 1) * 512], ALPHA,
                                           ex[2 + 2 * t + i][0:n, :], ALU.mult, ALU.add).then_inc(yb_used, 1)
            pair_of_blocks(0, first=True)
            with dve.Fori(1, NE // 2 - 1) as pair:
                pair_of_blocks(dve.snap(pair))
            pair_of_blocks(NE // 2 - 1, last=True)
            add_pieces(NE // 2 - 1)
            count = dve.value_load(n_later[0:1, 0:1], min_val=0, max_val=RANKS)
            with dve.If(count > 0):
                dve.wait_ge(slots_turned, NE // 2)
                V.memset(onehot[:, :, CAP:], 0.0)
                V.memset(onehot_w[:, :, CAP:], 0.0)
                V.memset(res[CAP:, :], 0.0)
                with dve.Fori(0, count) as loop:
                    b = dve.snap(loop)
                    col = dve.value_load(later[0:1, 0, ds(b, 1)], min_val=0, max_val=NE * PASSES - 1)
                    e = dve.value_load(later[0:1, 1, ds(b, 1)], min_val=0, max_val=NE - 1)
                    dve.wait_ge(slots_turned, b + NE // 2)
                    make_onehot(0, col).then_inc(onehot_ready, 1)
                    make_onehot_w(0, col, e).then_inc(onehot_w_ready, 1)
                    keep_up(b + NE)
                    gated(b + NE, e, b * 4 + NE * 4)
                    add_pieces(b + NE // 2)
            dve.wait_ge(ln2_in, 32)
            dve.wait_ge(added, 6 * (NE // 2))
            for t, (t0, n) in enumerate(TILES):
                for half in range(2):
                    stats(y[0:n, t, :], n, half)
                last = centred(y[0:n, t, :], y[0:n, t, :], n, t + 4, ln2[0], rstd2[0:n, t:t + 1])
                if t < 2:
                    last.then_inc(y_centred, 1)
                else:
                    link(last)
                    scaled(y[0:n, t, :], n, rstd2[0:n, t:t + 1], ln2[1], ys_final)


INPUTS = ["x_prompt", "x_sample", "state_gla", "state_pool", "w_in", "w_gk2", "b_gk", "gla_norm_w", "w_branch_gla",
          "w_pool_grp", "pool_scale", "w_branch_pool", "b_gates", "w_out", "ln1_g", "ln1_b", "w_router", "b_router",
          "w_gu", "b_gu", "w_down", "b_down", "ln2_g", "ln2_b"]
OUTPUTS = [(1, NP, D), (B, L, D), (1, 1, HEADS, DK, DV), (1, 1, PBUF, 512), (1, B, HEADS, DK, DV), (1, B, PBUF, 512)]


def kernel(**inputs):
    import numpy as _np
    import concourse.bacc as _bacc
    from concourse import mybir as _mybir
    from concourse.bass_utils import run_bass_kernel_spmd as _run

    nc = _bacc.Bacc("TRN2", target_bir_lowering=False, num_devices=1)
    arrays, args = {}, []
    named = [(n, _np.ascontiguousarray(inputs[n])) for n in INPUTS]
    named += list(zip(("c_cols", "c_starts", "c_lists"), constants()))
    for name, a in named:
        arrays[f"in_{name}"] = a
        args.append(nc.dram_tensor(f"in_{name}", a.shape, _mybir.dt.from_np(a.dtype), kind="ExternalInput").ap())
    for i, shape in enumerate(OUTPUTS):
        args.append(nc.dram_tensor(f"out_{i}", shape, _mybir.dt.float32, kind="ExternalOutput").ap())
    build(nc, *args)
    r = _run(nc, [arrays], core_ids=[0])
    return tuple(r.results[0][f"out_{i}"] for i in range(len(OUTPUTS)))
```
